# Optimizing a Trainium2 kernel written in Bass

```python
import jax, jax.numpy as jnp
from jax import lax
import numpy as np
import math
import jax
import jax.numpy as jnp

D_MODEL = 1024
BATCH = 1
SEQ = 256
DEPTH = 2

N_HEADS = 16
HEAD_DIM = D_MODEL // N_HEADS
D_FF = ((8 * D_MODEL // 3 + 127) // 128) * 128
CONV_WIDTH = 3
Q_BLOCK = 128
N_MIXERS = 2
N_MOD = 6
RMS_EPS = 1e-6
N_SB_LAYERS = (DEPTH + 1) // 2
N_FOX_LAYERS = DEPTH // 2


def rmsnorm(x, g):
    xf = x.astype(jnp.float32)
    y = xf * lax.rsqrt(jnp.mean(xf * xf, axis=-1, keepdims=True) + RMS_EPS)
    return (y * g.astype(jnp.float32)).astype(x.dtype)

def modulate(h, shift, scale):
    return h * (1.0 + scale[:, None, :]) + shift[:, None, :]

def split_heads(t):
    b, s, _ = t.shape
    return t.reshape(b, s, N_HEADS, HEAD_DIM).transpose(0, 2, 1, 3)

def merge_heads(t):
    b, h, s, d = t.shape
    return t.transpose(0, 2, 1, 3).reshape(b, s, h * d)

def stick_breaking_attention(q, k, v):
    s_len = q.shape[2]
    scale = HEAD_DIM ** -0.5
    outs = []
    for blk in range(s_len // Q_BLOCK):
        q0 = blk * Q_BLOCK
        k_end = q0 + Q_BLOCK
        qb, kb, vb = q[:, :, q0:k_end], k[:, :, :k_end], v[:, :, :k_end]
        z = jnp.einsum('bhqd,bhkd->bhqk', qb, kb).astype(jnp.float32) * scale
        t_idx = q0 + jnp.arange(Q_BLOCK)[:, None]
        s_idx = jnp.arange(k_end)[None, :]
        strict = s_idx < t_idx
        log_beta = jax.nn.log_sigmoid(z)
        log_1mb = jnp.where(strict, jax.nn.log_sigmoid(-z), 0.0)
        after = lax.cumsum(log_1mb, axis=3, reverse=True) - log_1mb
        a = jnp.where(strict, jnp.exp(log_beta + after), 0.0)
        outs.append(jnp.einsum('bhqk,bhkd->bhqd', a.astype(vb.dtype), vb))
    return jnp.concatenate(outs, axis=2)

def forgetting_attention(q, k, v, log_f):
    s_len = q.shape[2]
    scale = HEAD_DIM ** -0.5
    cum = lax.cumsum(log_f, axis=2)
    outs = []
    for blk in range(s_len // Q_BLOCK):
        q0 = blk * Q_BLOCK
        k_end = q0 + Q_BLOCK
        qb, kb, vb = q[:, :, q0:k_end], k[:, :, :k_end], v[:, :, :k_end]
        z = jnp.einsum('bhqd,bhkd->bhqk', qb, kb).astype(jnp.float32) * scale
        decay = cum[:, :, q0:k_end, None] - cum[:, :, None, :k_end]
        t_idx = q0 + jnp.arange(Q_BLOCK)[:, None]
        s_idx = jnp.arange(k_end)[None, :]
        logits = jnp.where(s_idx <= t_idx, z + decay, -jnp.inf)
        p = jax.nn.softmax(logits, axis=-1)
        outs.append(jnp.einsum('bhqk,bhkd->bhqd', p.astype(vb.dtype), vb))
    return jnp.concatenate(outs, axis=2)

def causal_depthwise_conv(h, w, b):
    s_len = h.shape[1]
    hp = jnp.pad(h, ((0, 0), (CONV_WIDTH - 1, 0), (0, 0)))
    out = b[None, None, :]
    for kk in range(CONV_WIDTH):
        out = out + w[kk][None, None, :] * hp[:, kk:kk + s_len]
    return out

def first_inputs(seed: int = 0) -> dict:
    key = jax.random.key(seed)
    ks = jax.random.split(key, 20)
    f32 = jnp.float32
    d, f, h = D_MODEL, D_FF, N_HEADS

    def nrm(k, shape, s):
        return jax.random.normal(k, shape, f32) * s

    return {
        "x": nrm(ks[0], (BATCH, SEQ, d), 1.0),
        "c": nrm(ks[1], (BATCH, d), 1.0),
        "w_mod": nrm(ks[2], (DEPTH, d, N_MOD * d), 0.5 * d ** -0.5),
        "b_mod": nrm(ks[3], (DEPTH, N_MOD * d), 0.02),
        "g_mix_pre": 1.0 + nrm(ks[4], (DEPTH, d), 0.05),
        "g_mix_post": 1.0 + nrm(ks[5], (DEPTH, d), 0.05),
        "w_qkv": nrm(ks[6], (DEPTH, d, 3 * d), d ** -0.5),
        "w_o": nrm(ks[7], (DEPTH, d, d), d ** -0.5),
        "w_fg": nrm(ks[8], (N_FOX_LAYERS, d, h), d ** -0.5),
        "b_fg": 3.0 + nrm(ks[9], (N_FOX_LAYERS, h), 0.5),
        "g_ffn_pre": 1.0 + nrm(ks[10], (DEPTH, d), 0.05),
        "g_ffn_post": 1.0 + nrm(ks[11], (DEPTH, d), 0.05),
        "w_ffn_gate": nrm(ks[12], (DEPTH, d, f), d ** -0.5),
        "w_ffn_up": nrm(ks[13], (DEPTH, d, f), d ** -0.5),
        "w_conv": nrm(ks[14], (DEPTH, CONV_WIDTH, f), CONV_WIDTH ** -0.5),
        "b_conv": nrm(ks[15], (DEPTH, f), 0.02),
        "w_ffn_down": nrm(ks[16], (DEPTH, f, d), f ** -0.5),
    }

def first_block(x, c, w_mod, b_mod, g_mix_pre, g_mix_post, w_qkv, w_o, w_fg, b_fg,
              g_ffn_pre, g_ffn_post, w_ffn_gate, w_ffn_up, w_conv, b_conv, w_ffn_down):
    c_act = jax.nn.silu(c)
    for i in range(DEPTH):
        mod = jnp.einsum('bd,dm->bm', c_act, w_mod[i]) + b_mod[i]
        sh_a, sc_a, gt_a, sh_f, sc_f, gt_f = jnp.split(mod, N_MOD, axis=-1)

        h = modulate(rmsnorm(x, g_mix_pre[i]), sh_a, sc_a)
        qkv = jnp.einsum('bsd,de->bse', h, w_qkv[i])
        q, k, v = (split_heads(t) for t in jnp.split(qkv, 3, axis=-1))
        if i % N_MIXERS == 0:
            o = stick_breaking_attention(q, k, v)
        else:
            j = i // N_MIXERS
            f_logit = jnp.einsum('bsd,dh->bhs', h, w_fg[j]) + b_fg[j][None, :, None]
            log_f = jax.nn.log_sigmoid(f_logit.astype(jnp.float32))
            o = forgetting_attention(q, k, v, log_f)
        o = jnp.einsum('bse,ed->bsd', merge_heads(o), w_o[i])
        x = x + gt_a[:, None, :] * rmsnorm(o, g_mix_post[i])

        h = modulate(rmsnorm(x, g_ffn_pre[i]), sh_f, sc_f)
        gate = jnp.einsum('bsd,df->bsf', h, w_ffn_gate[i])
        up = jnp.einsum('bsd,df->bsf', h, w_ffn_up[i])
        gate = causal_depthwise_conv(gate, w_conv[i], b_conv[i])
        y = jnp.einsum('bsf,fd->bsd', jax.nn.silu(gate) * up, w_ffn_down[i])
        x = x + gt_f[:, None, :] * rmsnorm(y, g_ffn_post[i])
    return x


GRID_W = 64
CTX_LEN = 256
N_MIXERS_2 = 4
NORM_EPS = 1e-6
ROPE_THETA = 10000.0
HEAD_DIM_2 = 64
BLOCK = 128
NEG_INF = -1e30

DIFF_HEADS = D_MODEL // (2 * HEAD_DIM_2)
DIFF_V_DIM = 2 * HEAD_DIM_2
DIFF_QK_WIDTH = 2 * DIFF_HEADS * HEAD_DIM_2
DIFF_V_WIDTH = DIFF_HEADS * DIFF_V_DIM
SHORT_CONV_W = 3
WIN_Q_HEADS = D_MODEL // HEAD_DIM_2
WIN_KV_HEADS = 4
WIN_GROUP = WIN_Q_HEADS // WIN_KV_HEADS
WINDOW = 128
SPAN = BLOCK + 2 * WINDOW
CONF_CONV_W = 31
D_FF_2 = -(-(8 * D_MODEL) // (3 * 256)) * 256


def _n_layers_of(kind):
    return (DEPTH - kind + N_MIXERS_2 - 1) // N_MIXERS_2

def rmsnorm_2(x, g):
    xf = x.astype(jnp.float32)
    y = xf * lax.rsqrt(jnp.mean(xf * xf, axis=-1, keepdims=True) + NORM_EPS)
    return (y * g.astype(jnp.float32)).astype(x.dtype)

def layernorm(x, g, b):
    xf = x.astype(jnp.float32)
    mu = jnp.mean(xf, axis=-1, keepdims=True)
    var = jnp.mean(jnp.square(xf - mu), axis=-1, keepdims=True)
    y = (xf - mu) * lax.rsqrt(var + NORM_EPS)
    return (y * g.astype(jnp.float32) + b.astype(jnp.float32)).astype(x.dtype)

def rope_tables(n):
    n_rows = n // GRID_W
    rows = jnp.broadcast_to(jnp.arange(n_rows, dtype=jnp.float32)[:, None], (n_rows, GRID_W)).reshape(-1)
    cols = jnp.broadcast_to(jnp.arange(GRID_W, dtype=jnp.float32)[None, :], (n_rows, GRID_W)).reshape(-1)
    n_freq = HEAD_DIM_2 // 4
    inv_freq = ROPE_THETA ** (-jnp.arange(n_freq, dtype=jnp.float32) / n_freq)
    ang_r = rows[:, None] * inv_freq[None, :]
    ang_c = cols[:, None] * inv_freq[None, :]
    ang = jnp.concatenate([ang_r, ang_r, ang_c, ang_c], axis=-1)
    return jnp.cos(ang), jnp.sin(ang)

def apply_rope(x, cos, sin):
    x1, x2, x3, x4 = jnp.split(x, 4, axis=-1)
    rot = jnp.concatenate([-x2, x1, -x4, x3], axis=-1)
    shape = (1, x.shape[1]) + (1,) * (x.ndim - 3) + (x.shape[-1],)
    y = x.astype(jnp.float32) * cos.reshape(shape) + rot.astype(jnp.float32) * sin.reshape(shape)
    return y.astype(x.dtype)

def dwconv(x, w):
    k = w.shape[0]
    return lax.conv_general_dilated(
        x, w[:, None, :].astype(x.dtype), window_strides=(1,), padding=[(k // 2, k // 2)],
        dimension_numbers=("NWC", "WIO", "NWC"), feature_group_count=x.shape[-1])

def _diff_attend(q, k, v, lam):
    s = jnp.einsum("bqmhd,bkmhd->bmhqk", q, k, preferred_element_type=jnp.float32) * (HEAD_DIM_2 ** -0.5)
    p = jax.nn.softmax(s, axis=-1)
    a = (p[:, 0] - lam * p[:, 1]).astype(v.dtype)
    return jnp.einsum("bhqk,bkhd->bqhd", a, v, preferred_element_type=jnp.float32)

def diff_attention(h_lat, h_ctx, w_qkv, w_o, q_norm, k_norm, lam_q1, lam_k1, lam_q2, lam_k2,
                   subln, lam_init, cos, sin, with_ctx):
    bsz, n, _ = h_lat.shape

    def project(h, rotary):
        q, k, v = jnp.split(h @ w_qkv, [DIFF_QK_WIDTH, 2 * DIFF_QK_WIDTH], axis=-1)
        q = rmsnorm_2(q.reshape(bsz, -1, 2, DIFF_HEADS, HEAD_DIM_2), q_norm)
        k = rmsnorm_2(k.reshape(bsz, -1, 2, DIFF_HEADS, HEAD_DIM_2), k_norm)
        if rotary:
            q, k = apply_rope(q, cos, sin), apply_rope(k, cos, sin)
        return q, k, v.reshape(bsz, -1, DIFF_HEADS, DIFF_V_DIM)

    lam = (jnp.exp(jnp.sum(lam_q1.astype(jnp.float32) * lam_k1.astype(jnp.float32)))
           - jnp.exp(jnp.sum(lam_q2.astype(jnp.float32) * lam_k2.astype(jnp.float32))) + lam_init)
    q_l, k_l, v_l = project(h_lat, True)
    q_c, k_c, v_c = project(h_ctx, False)
    k_all = jnp.concatenate([k_l, k_c], axis=1)
    v_all = jnp.concatenate([v_l, v_c], axis=1)
    nb = n // BLOCK
    q_blocks = jnp.moveaxis(q_l.reshape(bsz, nb, BLOCK, 2, DIFF_HEADS, HEAD_DIM_2), 1, 0)
    o_blocks = lax.map(lambda qb: _diff_attend(qb, k_all, v_all, lam), q_blocks)
    o_l = jnp.moveaxis(o_blocks, 0, 1).reshape(bsz, n, DIFF_HEADS, DIFF_V_DIM)

    def out(o):
        o = rmsnorm_2(o, subln) * (1.0 - lam_init)
        return o.reshape(bsz, -1, DIFF_V_WIDTH).astype(h_lat.dtype) @ w_o

    y_c = out(_diff_attend(q_c, k_c, v_c, lam)) if with_ctx else None
    return out(o_l), y_c

def short_conv(h, w_in, conv_w, w_out):
    b_gate, c_gate, u = jnp.split(h @ w_in, 3, axis=-1)
    return (b_gate * dwconv(c_gate * u, conv_w)) @ w_out

def _sink_attend(scores, values, sink):
    b, kv, g, q, _ = scores[0].shape
    sink_col = jnp.broadcast_to(sink.astype(jnp.float32)[None, :, :, None, None], (b, kv, g, q, 1))
    p = jax.nn.softmax(jnp.concatenate(scores + [sink_col], axis=-1), axis=-1)
    out = 0.0
    start = 0
    for s, v in zip(scores, values):
        kn = s.shape[-1]
        out = out + jnp.einsum("bkgqj,bjkd->bqkgd", p[..., start:start + kn].astype(v.dtype), v,
                               preferred_element_type=jnp.float32)
        start += kn
    return out

def window_gqa(h_lat, h_ctx, w_qkv, w_o, q_norm, k_norm, sink, cos, sin, with_ctx):
    bsz, n, _ = h_lat.shape
    qw = WIN_Q_HEADS * HEAD_DIM_2
    kw = WIN_KV_HEADS * HEAD_DIM_2
    scale = HEAD_DIM_2 ** -0.5

    def project(h, rotary):
        q, k, v = jnp.split(h @ w_qkv, [qw, qw + kw], axis=-1)
        q = rmsnorm_2(q.reshape(bsz, -1, WIN_KV_HEADS, WIN_GROUP, HEAD_DIM_2), q_norm)
        k = rmsnorm_2(k.reshape(bsz, -1, WIN_KV_HEADS, HEAD_DIM_2), k_norm)
        if rotary:
            q, k = apply_rope(q, cos, sin), apply_rope(k, cos, sin)
        return q, k, v.reshape(bsz, -1, WIN_KV_HEADS, HEAD_DIM_2)

    sink_kg = sink.reshape(WIN_KV_HEADS, WIN_GROUP)
    q_l, k_l, v_l = project(h_lat, True)
    q_c, k_c, v_c = project(h_ctx, False)
    pad = ((0, 0), (WINDOW, WINDOW), (0, 0), (0, 0))
    k_pad, v_pad = jnp.pad(k_l, pad), jnp.pad(v_l, pad)
    nb = n // BLOCK

    def block(args):
        qb, bi = args
        start = bi * BLOCK
        kb = lax.dynamic_slice_in_dim(k_pad, start, SPAN, axis=1)
        vb = lax.dynamic_slice_in_dim(v_pad, start, SPAN, axis=1)
        s_win = jnp.einsum("bqkgd,bjkd->bkgqj", qb, kb, preferred_element_type=jnp.float32) * scale
        kpos = start - WINDOW + jnp.arange(SPAN)
        qpos = start + jnp.arange(BLOCK)
        valid = ((jnp.abs(kpos[None, :] - qpos[:, None]) <= WINDOW)
                 & (kpos[None, :] >= 0) & (kpos[None, :] < n))
        s_win = jnp.where(valid, s_win, NEG_INF)
        s_ctx = jnp.einsum("bqkgd,bjkd->bkgqj", qb, k_c, preferred_element_type=jnp.float32) * scale
        return _sink_attend([s_win, s_ctx], [vb, v_c], sink_kg)

    q_blocks = jnp.moveaxis(q_l.reshape(bsz, nb, BLOCK, WIN_KV_HEADS, WIN_GROUP, HEAD_DIM_2), 1, 0)
    o_blocks = lax.map(block, (q_blocks, jnp.arange(nb)))
    o_l = jnp.moveaxis(o_blocks, 0, 1)

    def out(o):
        return o.reshape(bsz, -1, D_MODEL).astype(h_lat.dtype) @ w_o

    if with_ctx:
        s_cc = jnp.einsum("bqkgd,bjkd->bkgqj", q_c, k_c, preferred_element_type=jnp.float32) * scale
        y_c = out(_sink_attend([s_cc], [v_c], sink_kg))
    else:
        y_c = None
    return out(o_l), y_c

def conformer_conv(h, w_pw1, b_pw1, dw_w, dw_b, ln_g, ln_b, w_pw2, b_pw2):
    a, g = jnp.split(h @ w_pw1 + b_pw1, 2, axis=-1)
    u = dwconv(a * jax.nn.sigmoid(g), dw_w) + dw_b
    u = jax.nn.silu(layernorm(u, ln_g, ln_b))
    return u @ w_pw2 + b_pw2

def swiglu(h, w_gate_up, w_down):
    g, u = jnp.split(h @ w_gate_up, 2, axis=-1)
    return (jax.nn.silu(g) * u) @ w_down

def second_inputs(seed: int = 0) -> dict:
    key = jax.random.key(seed)
    keys = iter(jax.random.split(key, 48))

    def nrm(shape, std):
        return jax.random.normal(next(keys), shape, jnp.float32) * std

    def gain(shape):
        return 1.0 + nrm(shape, 0.05)

    d = D_MODEL
    n_a, n_b, n_c, n_d = (_n_layers_of(k) for k in range(N_MIXERS_2))
    return {
        "x": nrm((BATCH, SEQ, d), 1.0),
        "c": nrm((BATCH, d), 1.0),
        "ctx": nrm((BATCH, CTX_LEN, d), 1.0),
        "c_ctx": nrm((d,), 1.0),
        "ada_w": nrm((DEPTH, d, 6 * d), 0.5 * d ** -0.5),
        "ada_b": nrm((DEPTH, 6 * d), 0.02),
        "norm1": gain((DEPTH, d)),
        "norm2": gain((DEPTH, d)),
        "ffn_w_gate_up": nrm((DEPTH, d, 2 * D_FF_2), d ** -0.5),
        "ffn_w_down": nrm((DEPTH, D_FF_2, d), D_FF_2 ** -0.5),
        "diff_w_qkv": nrm((n_a, d, 2 * DIFF_QK_WIDTH + DIFF_V_WIDTH), d ** -0.5),
        "diff_w_o": nrm((n_a, DIFF_V_WIDTH, d), DIFF_V_WIDTH ** -0.5),
        "diff_q_norm": gain((n_a, HEAD_DIM_2)),
        "diff_k_norm": gain((n_a, HEAD_DIM_2)),
        "diff_lam_q1": nrm((n_a, HEAD_DIM_2), 0.1),
        "diff_lam_k1": nrm((n_a, HEAD_DIM_2), 0.1),
        "diff_lam_q2": nrm((n_a, HEAD_DIM_2), 0.1),
        "diff_lam_k2": nrm((n_a, HEAD_DIM_2), 0.1),
        "diff_subln": gain((n_a, DIFF_V_DIM)),
        "sc_w_in": nrm((n_b, d, 3 * d), d ** -0.5),
        "sc_conv_w": nrm((n_b, SHORT_CONV_W, d), SHORT_CONV_W ** -0.5),
        "sc_w_out": nrm((n_b, d, d), d ** -0.5),
        "win_w_qkv": nrm((n_c, d, (WIN_Q_HEADS + 2 * WIN_KV_HEADS) * HEAD_DIM_2), d ** -0.5),
        "win_w_o": nrm((n_c, d, d), d ** -0.5),
        "win_q_norm": gain((n_c, HEAD_DIM_2)),
        "win_k_norm": gain((n_c, HEAD_DIM_2)),
        "win_sink": nrm((n_c, WIN_Q_HEADS), 0.5),
        "cf_w_pw1": nrm((n_d, d, 2 * d), d ** -0.5),
        "cf_b_pw1": nrm((n_d, 2 * d), 0.01),
        "cf_dw_w": nrm((n_d, CONF_CONV_W, d), CONF_CONV_W ** -0.5),
        "cf_dw_b": nrm((n_d, d), 0.01),
        "cf_ln_g": gain((n_d, d)),
        "cf_ln_b": nrm((n_d, d), 0.01),
        "cf_w_pw2": nrm((n_d, d, d), d ** -0.5),
        "cf_b_pw2": nrm((n_d, d), 0.01),
    }

def second_block(x, c, ctx, c_ctx, ada_w, ada_b, norm1, norm2, ffn_w_gate_up, ffn_w_down,
              diff_w_qkv, diff_w_o, diff_q_norm, diff_k_norm, diff_lam_q1, diff_lam_k1,
              diff_lam_q2, diff_lam_k2, diff_subln,
              sc_w_in, sc_conv_w, sc_w_out,
              win_w_qkv, win_w_o, win_q_norm, win_k_norm, win_sink,
              cf_w_pw1, cf_b_pw1, cf_dw_w, cf_dw_b, cf_ln_g, cf_ln_b, cf_w_pw2, cf_b_pw2):
    n = x.shape[1]
    cos, sin = rope_tables(n)
    c_act = jax.nn.silu(c)
    cc_act = jax.nn.silu(c_ctx)
    h, hc = x, ctx
    for i in range(DEPTH):
        kind, j = i % N_MIXERS_2, i // N_MIXERS_2
        with_ctx = i < DEPTH - 1
        mod = (c_act @ ada_w[i] + ada_b[i])[:, None, :]
        mod_c = (cc_act @ ada_w[i] + ada_b[i])[None, None, :]
        sh1, sc1, g1, sh2, sc2, g2 = jnp.split(mod, 6, axis=-1)
        csh1, csc1, cg1, csh2, csc2, cg2 = jnp.split(mod_c, 6, axis=-1)
        a = rmsnorm_2(h, norm1[i]) * (1.0 + sc1) + sh1
        if with_ctx or kind in (0, 2):
            ac = rmsnorm_2(hc, norm1[i]) * (1.0 + csc1) + csh1
        if kind == 0:
            lam_init = 0.8 - 0.6 * math.exp(-0.3 * i)
            y, yc = diff_attention(a, ac, diff_w_qkv[j], diff_w_o[j], diff_q_norm[j], diff_k_norm[j],
                                   diff_lam_q1[j], diff_lam_k1[j], diff_lam_q2[j], diff_lam_k2[j],
                                   diff_subln[j], lam_init, cos, sin, with_ctx)
        elif kind == 1:
            y = short_conv(a, sc_w_in[j], sc_conv_w[j], sc_w_out[j])
            yc = short_conv(ac, sc_w_in[j], sc_conv_w[j], sc_w_out[j]) if with_ctx else None
        elif kind == 2:
            y, yc = window_gqa(a, ac, win_w_qkv[j], win_w_o[j], win_q_norm[j], win_k_norm[j],
                               win_sink[j], cos, sin, with_ctx)
        else:
            cf = (cf_w_pw1[j], cf_b_pw1[j], cf_dw_w[j], cf_dw_b[j], cf_ln_g[j], cf_ln_b[j],
                  cf_w_pw2[j], cf_b_pw2[j])
            y = conformer_conv(a, *cf)
            yc = conformer_conv(ac, *cf) if with_ctx else None
        h = h + g1 * y
        h = h + g2 * swiglu(rmsnorm_2(h, norm2[i]) * (1.0 + sc2) + sh2, ffn_w_gate_up[i], ffn_w_down[i])
        if with_ctx:
            hc = hc + cg1 * yc
            hc = hc + cg2 * swiglu(rmsnorm_2(hc, norm2[i]) * (1.0 + csc2) + csh2,
                                   ffn_w_gate_up[i], ffn_w_down[i])
    return h


def setup_inputs(seed=0):
    out = dict(first_inputs(seed))
    for name, value in second_inputs(seed + 1).items():
        if name != "x":
            out[name + "_2"] = value
    return out


def reference(
    x, c, w_mod, b_mod, g_mix_pre, g_mix_post, w_qkv, w_o, w_fg, b_fg, g_ffn_pre, g_ffn_post,
    w_ffn_gate, w_ffn_up, w_conv, b_conv, w_ffn_down, c_2, ctx_2, c_ctx_2, ada_w_2, ada_b_2,
    norm1_2, norm2_2, ffn_w_gate_up_2, ffn_w_down_2, diff_w_qkv_2, diff_w_o_2, diff_q_norm_2,
    diff_k_norm_2, diff_lam_q1_2, diff_lam_k1_2, diff_lam_q2_2, diff_lam_k2_2, diff_subln_2,
    sc_w_in_2, sc_conv_w_2, sc_w_out_2, win_w_qkv_2, win_w_o_2, win_q_norm_2, win_k_norm_2,
    win_sink_2, cf_w_pw1_2, cf_b_pw1_2, cf_dw_w_2, cf_dw_b_2, cf_ln_g_2, cf_ln_b_2, cf_w_pw2_2,
    cf_b_pw2_2,
):
    x = first_block(
        x, c, w_mod, b_mod, g_mix_pre, g_mix_post, w_qkv, w_o, w_fg, b_fg, g_ffn_pre,
        g_ffn_post, w_ffn_gate, w_ffn_up, w_conv, b_conv, w_ffn_down,
    )
    return second_block(
        x, c_2, ctx_2, c_ctx_2, ada_w_2, ada_b_2, norm1_2, norm2_2, ffn_w_gate_up_2,
        ffn_w_down_2, diff_w_qkv_2, diff_w_o_2, diff_q_norm_2, diff_k_norm_2, diff_lam_q1_2,
        diff_lam_k1_2, diff_lam_q2_2, diff_lam_k2_2, diff_subln_2, sc_w_in_2, sc_conv_w_2,
        sc_w_out_2, win_w_qkv_2, win_w_o_2, win_q_norm_2, win_k_norm_2, win_sink_2, cf_w_pw1_2,
        cf_b_pw1_2, cf_dw_w_2, cf_dw_b_2, cf_ln_g_2, cf_ln_b_2, cf_w_pw2_2, cf_b_pw2_2,
    )


_drawn_inputs = setup_inputs


def setup_inputs(seed=0):
    import zlib

    import numpy as np

    out = dict(_drawn_inputs(seed))
    spreads = {}
    factors = {'g_ffn_post': 2.685,
     'b_conv': 6.979,
     'norm2_2': 3.083,
     'diff_q_norm_2': 8.0,
     'diff_k_norm_2': 8.0,
     'diff_lam_q1_2': 64.0,
     'diff_lam_k1_2': 64.0,
     'diff_lam_q2_2': 8.0,
     'diff_lam_k2_2': 8.0,
     'diff_subln_2': 5.291}
    for name, (base, spread) in spreads.items():
        noise = np.random.default_rng([zlib.crc32(name.encode()), seed]).standard_normal(out[name].shape)
        drawn = base * np.exp(spread * noise) if base else spread * noise
        out[name] = jnp.asarray(drawn.astype(out[name].dtype))
    for name, factor in factors.items():
        out[name] = (out[name] * factor).astype(out[name].dtype)
    return out
```

```python
import numpy as np
from contextlib import ExitStack
import concourse.bass as bass
from concourse import mybir

D, S, FF, H, P = 1024, 256, 2816, 16, 128
KT, FT = D // P, FF // P
EPS = 1e-6
NRAW, NSPL = 4, 3
LAYERS = 4
LAM_INIT = 0.8 - 0.6 * float(np.exp(-0.3 * 0))
NEG = -1e30

SM = {}


def _layout():
    at = 0
    for name, n in [("c", 8), ("c2", 8), ("cc", 8)] + [(f"g{l}{k}", 8) for l in range(4) for k in "af"] + \
            [(f"b{l}{p}", 8) for l in range(4) for p in (0, 1, 3, 4)] + \
            [(f"wc{l}{k}", FT) for l in range(2) for k in range(3)] + [(f"bc{l}", FT) for l in range(2)] + \
            [(f"sc{k}", 8) for k in range(3)]:
        SM[name] = (at, n)
        at += n
    return at


NSM = _layout()


class Queue:

    def __init__(self, eng, sem):
        self.eng, self.sem, self.n, self.seen = eng, sem, 0, {}

    def wait(self, *tokens):
        for sem, value in tokens:
            if self.seen.get(sem.name, 0) < value:
                self.eng.wait_ge(sem, value)
                self.seen[sem.name] = value

    def do(self, f, *tokens):
        self.wait(*tokens)
        self.n += 1
        f(self.eng).then_inc(self.sem, 1)
        return self.sem, self.n

    def quiet(self, f, *tokens):
        self.wait(*tokens)
        f(self.eng)

    def dma(self, f, sem, value, *tokens):
        self.wait(*tokens)
        f(self.eng).then_inc(sem, 16)
        return sem, value


class Slots:

    def __init__(self, items):
        self.items, self.at, self.readers = items, 0, [()] * len(items)

    def take(self):
        i = self.at % len(self.items)
        self.at += 1
        readers, self.readers[i] = self.readers[i], None
        assert readers is not None, "a buffer is taken before it is free"
        return i, self.items[i], readers

    def free(self, i, *tokens):
        self.readers[i] = tokens


def build(nc, A, out):
    f32, f32r = mybir.dt.float32, mybir.dt.float32r
    ALU, ACT, AX = mybir.AluOpType, mybir.ActivationFunctionType, mybir.AxisListType
    stack = ExitStack()
    with stack:
        def sb(name, shape, dt=f32):
            return stack.enter_context(nc.sbuf_tensor(name, shape, dt))

        with nc.sbuf_tensor("att", [P, 10240], f32) as att, nc.sbuf_tensor("oHL", [P, 2, KT, S], f32r) as oHL:
            pass
        aHL = sb("aHL", [P, 2, FT, S], f32r)
        sb("fill", [P, 14336 - 2 * FT * S], f32)
        raw = sb("raw", [P, NRAW, 2048])
        whi = sb("whi", [P, NSPL, 2048], f32r)
        wlo = sb("wlo", [P, NSPL, 2048], f32r)
        x = sb("x", [P, 2, D])
        hHL = sb("hHL", [P, 2, KT, S], f32r)
        gtb = sb("gtb", [P, 2, D])
        acc = sb("acc", [P, 2, D])
        xn = sb("xn", [P, 2, D])
        tmpt = sb("tmp", [P, 7, 512])
        sm = sb("sm", [P, NSM])
        modc = sb("modc", [P, 6, 8])
        ccol = sb("ccol", [P, 3, 8])
        ident = sb("ident", [P, P])
        ones = sb("ones", [P, P])
        tri_ge = sb("tri_ge", [P, P])
        tri_le = sb("tri_le", [P, P])
        msk = sb("msk", [P, P])
        st = sb("st", [P, 64])
        rope = sb("rope", [P, 4, 2, 64])
        wfgH = sb("wfgH", [P, KT, H], f32r)
        wfgL = sb("wfgL", [P, KT, H], f32r)
        kgt = sb("kgt", [P, 64])
        phalf = sb("phalf", [P, 16])
        ncum = sb("ncum", [H, S])
        mat = stack.enter_context(nc.psum_tensor("mat", [P, 8, 512], f32))

        sem = lambda n: stack.enter_context(nc.semaphore(n))
        PE, AC, DV, PO, SP = (Queue(e, sem(n)) for e, n in (
            (nc.tensor, "s_pe"), (nc.scalar, "s_act"), (nc.vector, "s_dve"), (nc.gpsimd, "s_pool"), (nc.sync, "s_sp")))
        s_raw = [sem(f"s_raw{i}") for i in range(NRAW)]
        s_in = [sem(f"s_in{i}") for i in range(8)]
        s_out = sem("s_out")

        aH, aL = aHL[:, 0], aHL[:, 1]
        hH, hL = hHL[:, 0], hHL[:, 1]
        oH, oL = oHL[:, 0], oHL[:, 1]
        bank_readers = [() for _ in range(8)]
        tmp = Slots([tmpt[:, i, :] for i in range(7)])
        last_att = [()]
        last_o = [()]
        last_a = [()]

        def bank(b):
            return mat[:, b, :]

        class Banks:
            def __init__(self, ids):
                self.ids, self.at = ids, 0

            def take(self):
                b = self.ids[self.at % len(self.ids)]
                self.at += 1
                return b

        ring = Banks([4, 5, 7])
        mring = Banks([6])

        def load(dst, src, i):
            return SP.dma(lambda e: e.dma_start(dst, src), s_in[i], 16)

        t_sm = load(sm[:, :], A["smalls"], 0)

        m0 = DV.do(lambda e: e.memset(ident[:, :], 0.0))
        m1 = DV.do(lambda e: e.memset(ones[:, :], 1.0))
        m2 = DV.do(lambda e: e.memset(phalf[:, :], -0.5))
        k0 = PO.do(lambda e: e.affine_select(out=ident[:, :], in_=ident[:, :], compare_op=ALU.not_equal, fill=1.0,
                                             base=0, pattern=[[-1, P]], channel_multiplier=1), m0, m1, m2)
        k1 = PO.do(lambda e: e.affine_select(out=tri_ge[:, :], in_=ones[:, :], compare_op=ALU.is_ge, fill=0.0,
                                             base=0, pattern=[[-1, P]], channel_multiplier=1))
        k2 = PO.do(lambda e: e.affine_select(out=tri_le[:, :], in_=ones[:, :], compare_op=ALU.is_ge, fill=0.0,
                                             base=0, pattern=[[1, P]], channel_multiplier=-1))
        t_const = k2

        def strict_mask(l_tokens):
            return PO.do(lambda e: e.affine_select(out=msk[:, :], in_=ones[:, :], compare_op=ALU.is_gt, fill=0.0,
                                                   base=0, pattern=[[1, P]], channel_multiplier=-1), *l_tokens)

        t_c = AC.do(lambda e: e.activation(ccol[:, :, :], sm[:, 0:24].rearrange("p (a b) -> p a b", a=3), ACT.Silu), t_sm)

        nraw = [0]
        raw_free = [()] * NRAW

        def fetch(src):
            i = nraw[0] % NRAW
            v = 16 * (nraw[0] // NRAW + 1)
            nraw[0] += 1
            return i, SP.dma(lambda e: e.dma_start(raw[:, i, :], src), s_raw[i], v, *raw_free[i])

        wseq = []
        for l in range(LAYERS):
            if l < 2:
                wseq += [("qkv%d" % l, 8 + i) for i in range(4)]
                for j in range(4):
                    wseq += [("qkv%d" % l, j), ("qkv%d" % l, 4 + j)]
            elif l == 2:
                wseq += [("qkv2", i) for i in range(12)]
            else:
                for j in range(4):
                    wseq += [("qkv3", 4 + j), ("qkv3", 8 + j), ("qkv3", j)]
            wseq += [("wo%d" % l, i) for i in range(4)]
            for j in range(11):
                wseq += [("gate%d" % l, j), ("up%d" % l, j)]
            wseq += [("down%d" % l, i) for i in range(11)]
        split_free = [()] * NSPL
        ready = []
        nsplit = [0]

        def split_next():
            if nsplit[0] == len(wseq):
                return
            name, c = wseq[nsplit[0]]
            s = nsplit[0] % NSPL
            nsplit[0] += 1
            i, t = fetch(A[name][c])
            hi = AC.do(lambda e: e.activation(whi[:, s, :], raw[:, i, :], ACT.Copy), t, *split_free[s])
            lo = DV.do(lambda e: e.tensor_tensor(out=wlo[:, s, :], in0=raw[:, i, :], in1=whi[:, s, :].bitcast(f32),
                                                 op=ALU.subtract), t, hi, *split_free[s])
            raw_free[i] = (lo,)
            ready.append((s, hi, lo, name))

        nused = [0]

        def chunk(name):
            s, hi, lo, got = ready[nused[0]]
            assert got == name, (got, name)
            nused[0] += 1
            PE.wait(hi, lo)
            return s, whi[:, s, :], wlo[:, s, :]

        def used(s, token):
            split_free[s] = (token,)

        modq = [(l, p, i) for l in range(LAYERS) for p in range(6) for i in range(4)]
        nmod = [0]
        acc_free = [(), ()]
        pending = []
        modt = {}
        gfree = [(), ()]
        cfree = [()]

        def mod_step():
            while pending:
                pending.pop(0)()
            if nmod[0] == len(modq):
                return
            l, p, q = modq[nmod[0]]
            nmod[0] += 1
            i, t = fetch(A["mod%d" % l][4 * p + q])
            accs = [(0, 0 if l < 2 else 1)] + ([(1, 2)] if l == 2 and p < 2 else [])
            last = None
            for a, c in accs:
                for j in range(2):
                    kt = 2 * q + j
                    src = raw[:, i, 1024 * j:1024 * j + 1024]
                    cs = ccol[:, c, kt:kt + 1]
                    if kt == 0:
                        last = DV.do(lambda e, src=src, cs=cs, a=a: e.tensor_scalar(acc[:, a, :], src, cs, None, ALU.mult),
                                     t, t_c, *acc_free[a])
                    else:
                        last = DV.do(lambda e, src=src, cs=cs, a=a: e.scalar_tensor_tensor(
                            out=acc[:, a, :], in0=src, scalar=cs, in1=acc[:, a, :], op0=ALU.mult, op1=ALU.add),
                            t, acct[a])
                    acct[a] = last
            raw_free[i] = (last,)
            if q == 3:
                if p in (2, 5):
                    gi, gtok = fetch(A["gb"][2 * l + (p == 5):2 * l + (p == 5) + 1, :].to_broadcast([P, 2048]))
                    pending.append(lambda: gate_rows(l, p, acct[0], gi, gtok))
                else:
                    for a, c in accs:
                        pending.append(lambda a=a: columns(l, p, a, acct[a]))

        acct = [None, None]

        def columns(l, p, a, t_acc):
            b = mring.take()
            PE.wait(t_acc, m1, *bank_readers[b])
            for k in range(8):
                f = lambda e, k=k: e.matmul(bank(b)[:, k:k + 1], acc[:, a, k * P:k * P + P], ones[:, 0:1],
                                            start=True, stop=True)
                t = PE.do(f) if k == 7 else PE.quiet(f)
            acc_free[a] = (t,)
            row = (4 if a else 0 if p < 3 else 2) + (p in (1, 4))
            o, _ = SM[f"b{l}{p}"]
            t1 = DV.do(lambda e: e.tensor_tensor(out=modc[:, row, :], in0=bank(b)[:, 0:8], in1=sm[:, o:o + 8],
                                                 op=ALU.add), t, t_sm, *cfree[0])
            bank_readers[b] = (t1,)
            if p in (1, 4):
                o2, _ = SM[f"g{l}" + ("a" if p == 1 else "f")]
                t1 = DV.do(lambda e: e.scalar_tensor_tensor(out=modc[:, row, :], in0=modc[:, row, :], scalar=1.0,
                                                            in1=sm[:, o2:o2 + 8], op0=ALU.add, op1=ALU.mult), t1)
            modt[(l, p, a)] = t1

        def gate_rows(l, p, t_acc, gi, gtok):
            g = int(p == 5)
            for half in range(2):
                b = mring.take()
                c = slice(512 * half, 512 * half + 512)
                t = PE.do(lambda e: e.matmul(bank(b), ones[:, :], acc[:, 0, c], start=True, stop=True),
                          t_acc, m1, *bank_readers[b])
                t1 = DV.do(lambda e: e.tensor_tensor(out=gtb[:, g, c], in0=bank(b), in1=raw[:, gi, c], op=ALU.add),
                           t, gtok, *gfree[g])
                bank_readers[b] = (t1,)
                if l < 2:
                    c2 = slice(1024 + 512 * half, 1536 + 512 * half)
                    t1 = DV.do(lambda e: e.tensor_tensor(out=gtb[:, g, c], in0=gtb[:, g, c], in1=raw[:, gi, c2],
                                                         op=ALU.mult), t1, gtok)
            acc_free[0] = (t,)
            raw_free[gi] = (t1,)
            modt[(l, p, 0)] = t1

        mod_debt = [0.0]

        def mods(rate, upto):
            mod_debt[0] += rate
            while mod_debt[0] >= 1.0:
                mod_debt[0] -= 1.0
                if nmod[0] < len(modq) and modq[nmod[0]][:2] <= upto:
                    mod_step()
                elif pending:
                    pending.pop(0)()

        def mods_through(l, p):
            while nmod[0] < len(modq) and modq[nmod[0]][:2] <= (l, p):
                mod_step()
            while pending:
                pending.pop(0)()

        stn = [0]

        def cols(n):
            if stn[0] + n > 64:
                stn[0] = 0
            stn[0] += n
            return st[:, stn[0] - n:stn[0]]

        def rstd(ss, n, width, t):
            a = PO.do(lambda e: e.tensor_scalar(ss, ss, 1.0 / n, EPS, ALU.mult, ALU.add), t)
            return PO.do(lambda e: e.tensor_tensor(out=ss, in0=ss, in1=phalf[:, 0:width], op=ALU.pow), a, m2)

        xn_free = [(), ()]

        def norm_T(src, tsrc, row, dstH, dstL, tmod, wr):
            tx = []
            for t in range(2):
                ss = cols(1)
                a = AC.do(lambda e: e.activation(xn[:, t, :], src[:, t, :], ACT.Square, accum_out=ss), tsrc[t], *xn_free[t])
                r = rstd(ss, D, 1, a)
                tx.append(AC.do(lambda e: e.activation(xn[:, t, :], src[:, t, :], ACT.Copy, scale=ss), r))
            last = []
            for k2_ in range(4):
                b = ring.take()
                PE.wait(*tx, t_const, *bank_readers[b])
                for j in range(2):
                    for t in range(2):
                        f = lambda e, j=j, t=t: e.transpose(bank(b)[:, 256 * j + P * t:256 * j + P * t + P],
                                                            xn[:, t, (2 * k2_ + j) * P:(2 * k2_ + j + 1) * P], ident[:, :])
                        pt = PE.do(f) if j == t == 1 else PE.quiet(f)
                i, tm, fr = tmp.take()
                for j in range(2):
                    kt = 2 * k2_ + j
                    e1 = AC.do(lambda e, j=j, kt=kt: e.activation(tm[:, 256 * j:256 * j + 256], bank(b)[:, 256 * j:256 * j + 256],
                                                                 ACT.Identity, bias=modc[:, row, kt:kt + 1],
                                                                 scale=modc[:, row + 1, kt:kt + 1]), pt, *fr, *tmod)
                bank_readers[b] = (e1,)
                last = split_T(tm.rearrange("p (a b) -> p a b", a=2), e1, dstH[:, 2 * k2_:2 * k2_ + 2, :],
                               dstL[:, 2 * k2_:2 * k2_ + 2, :], wr)
                tmp.free(i, *last)
            xn_free[0] = xn_free[1] = (pt,)
            cfree[0] = (e1,)
            return last

        def split_T(src, t, dh, dl, wr):
            a = AC.do(lambda e: e.activation(dh, src, ACT.Copy), t, *wr)
            b = DV.do(lambda e: e.tensor_tensor(out=dl, in0=src, in1=dh.bitcast(f32), op=ALU.subtract), a, *wr)
            return a, b

        def featmajor(name, th, sH, sL):
            s, wh, wl = chunk(name)
            wh = wh.rearrange("p (k n) -> p k n", k=8)
            wl = wl.rearrange("p (k n) -> p k n", k=8)
            b = bring.take()
            PE.wait(*th, *bank_readers[b])
            for i in range(2):
                o = bank(b)[:, 256 * i:256 * i + 256]
                for k in range(KT):
                    for n, (w, h) in enumerate(((wh, sH), (wh, sL), (wl, sH))):
                        f = lambda e, o=o, w=w, h=h, k=k, n=n, i=i: e.matmul(
                            o, w[:, k, P * i:P * i + P], h[:, k, :], start=(k == 0 and n == 0),
                            stop=(k == KT - 1 and n == 2))
                        t = PE.do(f) if (i == 1 and k == KT - 1 and n == 2) else PE.quiet(f)
            used(s, t)
            return b, t

        bring = Banks([4, 5, 7])

        def tokmajor(name, th, sH, sL, nk, first):
            s, wh, wl = chunk(name)
            wh = wh.rearrange("p (k n) -> p k n", k=2)
            wl = wl.rearrange("p (k n) -> p k n", k=2)
            PE.wait(*th)
            if first == 0:
                for b in range(4):
                    PE.wait(*bank_readers[b])
            for j in range(2):
                k = 2 * first + j
                for t in range(2):
                    for n, (h, w, half) in enumerate([(sH, wh, 0), (sH, wh, 1), (sH, wl, 0), (sH, wl, 1),
                                                      (sL, wh, 0), (sL, wh, 1)]):
                        f = lambda e, h=h, w=w, half=half, j=j, k=k, t=t, n=n: e.matmul(
                            mat[:, 2 * t + half, :], h[:, k, P * t:P * t + P], w[:, j, 512 * half:512 * half + 512],
                            start=(k == 0 and n < 2), stop=(k == nk - 1 and n >= 4))
                        tok = PE.do(f) if (j == 1 and t == 1 and n == 5) else PE.quiet(f)
            used(s, tok)
            return tok

        def post(l, g, t_mm, tgt):
            tx = []
            for t in range(2):
                flat = mat[:, 2 * t:2 * t + 2, :]
                xv = xn[:, t, :].rearrange("p (a b) -> p a b", a=2)
                gv = gtb[:, g, :].rearrange("p (a b) -> p a b", a=2)
                if l < 2:
                    ss = cols(1)
                    a = AC.do(lambda e: e.activation(xv, flat, ACT.Square, accum_out=ss), t_mm, *xn_free[t])
                    r = rstd(ss, D, 1, a)
                    b = DV.do(lambda e: e.scalar_tensor_tensor(out=xv, in0=flat, scalar=ss, in1=gv, op0=ALU.mult,
                                                               op1=ALU.mult), r, *tgt)
                else:
                    b = DV.do(lambda e: e.tensor_tensor(out=xv, in0=flat, in1=gv, op=ALU.mult), t_mm, *tgt, *xn_free[t])
                c = DV.do(lambda e: e.tensor_tensor(out=x[:, t, :], in0=x[:, t, :], in1=xn[:, t, :], op=ALU.add), b)
                bank_readers[2 * t] = bank_readers[2 * t + 1] = (b,)
                xn_free[t] = (c,)
                tx.append(c)
            gfree[g] = (b,)
            return tx

        tx0 = SP.dma(lambda e: e.dma_start(x[:, :, :], A["x"].rearrange("o (t p) d -> p (o t) d", p=P)), s_in[1], 16)
        tx = [tx0, tx0]
        mods_through(0, 1)
        for _ in range(NSPL):
            split_next()
        th = ()

        qT = att[:, 0:2048].rearrange("p (k t) -> p k t", k=8)
        kT = att[:, 2048:4096].rearrange("p (k t) -> p k t", k=8)
        v01 = att[:, 4096:6144].rearrange("p (t d) -> p t d", t=2)
        kT2 = att[:, 2048:6144].rearrange("p (k t) -> p k t", k=8)
        v2 = att[:, 6144:10240].rearrange("p (t d) -> p t d", t=4)
        att_slots = [att[:, 6144 + 384 * i:6144 + 384 * i + 384] for i in range(10)]

        hT_free = [()]
        MOD_RATE = {0: (0.8, 0.4), 1: (0.6, 0.4), 2: (0.7, 0.4), 3: (0.8, 0.0)}

        def value_product(l, th):
            for i in range(4):
                t = tokmajor("qkv%d" % l, th, hH, hL, KT, i)
                split_next()
                mods(MOD_RATE[l][0], (l, 5))
            tv = []
            for tt in range(2):
                dst = v01[:, tt, :].rearrange("p (a b) -> p a b", a=2)
                tv.append(AC.do(lambda e: e.activation(dst, mat[:, 2 * tt:2 * tt + 2, :], ACT.Copy), t,
                                *last_att[0], *last_a[0]))
                bank_readers[2 * tt] = bank_readers[2 * tt + 1] = (tv[-1],)
            return t, tv

        def qk_products(l, th):
            tq, tk = [], []
            for j in range(4):
                for n, (dst, lst) in enumerate(((qT, tq), (kT, tk))):
                    b, t = featmajor("qkv%d" % l, th, hH, hL)
                    d = dst[:, 2 * j:2 * j + 2, :]
                    src = bank(b).rearrange("p (a b) -> p a b", a=2)
                    if n == 0:
                        e1 = AC.do(lambda e: e.activation(d, src, ACT.Copy, scale=0.125), t, *last_att[0], *last_a[0])
                    else:
                        e1 = DV.do(lambda e: e.tensor_copy(d, src), t, *last_att[0], *last_a[0])
                    bank_readers[b] = (e1,)
                    lst.append(e1)
                    split_next()
                    mods(MOD_RATE[l][0], (l, 5))
            return t, tq, tk

        def values_out(h, aT, ta, tv):
            hp, ht = 64 * (h % 2), h // 2
            if h % 2 == 0:
                obank[0] = obanks.take()
            b = obank[0]
            PE.wait(*ta, *tv)
            if h % 2 == 0:
                PE.wait(*bank_readers[b])
            vh = [v01[:, i, 64 * h:64 * h + 64] for i in range(2)]
            PE.quiet(lambda e: e.matmul(bank(b)[hp:hp + 64, 0:128], vh[0], aT[:, 0:128], start=True, stop=True))
            PE.quiet(lambda e: e.matmul(bank(b)[hp:hp + 64, 128:256], vh[0], aT[:, 128:256], start=True, stop=False))
            t = PE.do(lambda e: e.matmul(bank(b)[hp:hp + 64, 128:256], vh[1], aT[:, 256:384], start=False, stop=True))
            if h % 2:
                last = split_T(bank(b)[:, 0:256], t, oH[:, ht, :], oL[:, ht, :], (*last_o[0], *last_a[0]))
                bank_readers[b] = last
                o_tok[0] = last
            return t

        obanks, obank, o_tok = Banks([4, 5]), [None], [()]

        def pipeline(stages, n):
            state = [dict() for _ in range(n)]
            for step in range(n + len(stages) - 1):
                for s_ in range(len(stages) - 1, -1, -1):
                    i = step - s_
                    if 0 <= i < n:
                        stages[s_](i, state[i])
                yield

        def stick_breaking(tq, tk, tv):
            slots = Slots(att_slots)
            zb, rb = Banks([0, 1]), Banks([2, 3])
            tmask = strict_mask((m1,))

            def scores(h, o):
                hp, ht = 64 * (h % 2), h // 2
                b = zb.take()
                q, k = qT[hp:hp + 64, ht, :], kT[hp:hp + 64, ht, :]
                PE.wait(tq[ht // 2], tk[ht // 2], *bank_readers[b])
                PE.quiet(lambda e: e.matmul(bank(b)[:, 0:256], k[:, 0:128], q[:, 0:256], start=True, stop=True))
                t = PE.do(lambda e: e.matmul(bank(b)[:, 256:384], k[:, 128:256], q[:, 128:256], start=True, stop=True))
                i, z, fr = slots.take()
                o["zi"], o["z"] = i, z
                o["tz"] = AC.do(lambda e: e.activation(z, bank(b)[:, 0:384], ACT.Copy), t, *fr)
                bank_readers[b] = (o["tz"],)
                i2, w, fr2 = slots.take()
                a = DV.do(lambda e: e.scalar_tensor_tensor(out=w, in0=z, scalar=-1.0, in1=z, op0=ALU.mult, op1=ALU.max), o["tz"], *fr2)
                a = AC.do(lambda e: e.activation(w, w, ACT.Exp, scale=-1.0), a)
                a = AC.do(lambda e: e.activation(w, w, ACT.Ln, bias=1.0), a)
                o["wi"], o["w"], o["tw"] = i2, w, a

            def softplus(h, o):
                z, w = o["z"], o["w"]
                a = DV.do(lambda e: e.scalar_tensor_tensor(out=w, in0=z, scalar=0.0, in1=w, op0=ALU.max, op1=ALU.add), o["tw"])
                for c in (0, 256):
                    a = PO.do(lambda e, c=c: e.tensor_tensor(out=w[:, c:c + P], in0=w[:, c:c + P], in1=msk[:, :], op=ALU.mult),
                              a, tmask)
                o["tw"] = a

            def sums(h, o):
                b = rb.take()
                w, z = o["w"], o["z"]
                PE.wait(o["tw"], t_const, *bank_readers[b])
                PE.quiet(lambda e: e.matmul(bank(b)[:, 0:128], tri_ge[:, :], w[:, 0:128], start=True, stop=True))
                PE.quiet(lambda e: e.matmul(bank(b)[:, 128:256], tri_ge[:, :], w[:, 128:256], start=True, stop=False))
                PE.quiet(lambda e: e.matmul(bank(b)[:, 128:256], ones[:, :], w[:, 256:384], start=False, stop=True))
                t = PE.do(lambda e: e.matmul(bank(b)[:, 256:384], tri_ge[:, :], w[:, 256:384], start=True, stop=True))
                d = DV.do(lambda e: e.tensor_tensor(out=w, in0=z, in1=bank(b)[:, 0:384], op=ALU.subtract), t)
                bank_readers[b] = (d,)
                slots.free(o["zi"], d)
                for c in (0, 256):
                    d = PO.do(lambda e, c=c: e.affine_select(out=w[:, c:c + P], in_=w[:, c:c + P], compare_op=ALU.is_gt,
                                                             fill=NEG, base=0, pattern=[[1, P]], channel_multiplier=-1), d)
                o["ta"] = AC.do(lambda e: e.activation(w, w, ACT.Exp), d)

            def values(h, o):
                t = values_out(h, o["w"], (o["ta"],), tv)
                slots.free(o["wi"], t)
                last_att[0] = (t,)

            return pipeline([scores, softplus, sums, values], H)

        def forgetting(tq, tk, tv, tcum):
            slots = Slots(att_slots)
            sbk, tbk = Banks([0, 1]), Banks([2, 3])
            a = PO.do(lambda e: e.tensor_scalar(msk[:, :], ones[:, :], -1.0, None, ALU.add), *last_att[0])
            tmask = PO.do(lambda e: e.affine_select(out=msk[:, :], in_=msk[:, :], compare_op=ALU.is_ge, fill=NEG,
                                                    base=0, pattern=[[-1, P]], channel_multiplier=1), a)

            def scores(h, o):
                hp, ht = 64 * (h % 2), h // 2
                b = sbk.take()
                q, k = qT[hp:hp + 64, ht, :], kT[hp:hp + 64, ht, :]
                eh = ident[0:H, h:h + 1].to_broadcast([H, P])
                PE.wait(tq[ht // 2], tk[ht // 2], tmask, tcum, t_const, *bank_readers[b])
                for c, t0, s0 in ((0, 0, 0), (128, 128, 0), (256, 128, 128)):
                    dst = bank(b)[:, c:c + P]
                    PE.quiet(lambda e: e.matmul(dst, q[:, t0:t0 + P], k[:, s0:s0 + P], start=True, stop=False))
                    f = lambda e: e.matmul(dst, eh, ncum[:, s0:s0 + P], start=False, stop=(c == 128))
                    PE.quiet(f)
                    if c != 128:
                        f2 = lambda e: e.matmul(dst, ident[:, :], msk[:, :], start=False, stop=True)
                        t = PE.do(f2) if c == 256 else PE.quiet(f2)
                nm, rs = cols(2), cols(2)
                a = DV.do(lambda e: e.tensor_reduce(nm[:, 0:1], bank(b)[:, 0:128], AX.X, ALU.max, negate=True), t)
                a = DV.do(lambda e: e.tensor_reduce(nm[:, 1:2], bank(b)[:, 128:384], AX.X, ALU.max, negate=True), t)
                i, p, fr = slots.take()
                a2 = AC.do(lambda e: e.activation(p[:, 0:128], bank(b)[:, 0:128], ACT.Exp, bias=nm[:, 0:1],
                                                  accum_out=rs[:, 0:1]), a, *fr)
                a2 = AC.do(lambda e: e.activation(p[:, 128:384], bank(b)[:, 128:384], ACT.Exp, bias=nm[:, 1:2],
                                                  accum_out=rs[:, 1:2]), a)
                bank_readers[b] = (a2,)
                o.update(p=p, pi=i, rs=rs, t=a2)

            def normalise(h, o):
                p, rs = o["p"], o["rs"]
                a = DV.do(lambda e: e.reciprocal(rs, rs), o["t"])
                DV.do(lambda e: e.tensor_scalar(p[:, 0:128], p[:, 0:128], rs[:, 0:1], None, ALU.mult), a)
                o["t"] = DV.do(lambda e: e.tensor_scalar(p[:, 128:384], p[:, 128:384], rs[:, 1:2], None, ALU.mult), a)

            def turn(h, o):
                p = o["p"]
                b = tbk.take()
                PE.wait(o["t"], *bank_readers[b])
                for c in (0, 128):
                    PE.quiet(lambda e, c=c: e.transpose(bank(b)[:, c:c + P], p[:, c:c + P], ident[:, :]))
                t = PE.do(lambda e: e.transpose(bank(b)[:, 256:384], p[:, 256:384], ident[:, :]))
                slots.free(o["pi"], t)
                i, w, fr = slots.take()
                o["w"], o["wi"] = w, i
                o["ta"] = DV.do(lambda e: e.tensor_copy(w, bank(b)[:, 0:384]), t, *fr)
                bank_readers[b] = (o["ta"],)

            def values(h, o):
                t = values_out(h, o["w"], (o["ta"],), tv)
                slots.free(o["wi"], t)
                last_att[0] = (t,)

            return pipeline([scores, normalise, turn, values], H)

        def forget_logits(th):
            i0, _, f0 = tmp.take()
            i1, _, f1 = tmp.take()
            i2, w2, f2 = tmp.take()
            wf, wb = tmp.items[i0][:, 0:128], tmp.items[i1][:, 0:16]
            t1 = SP.dma(lambda e: e.dma_start(wf.rearrange("p (k n) -> p k n", k=8),
                                              A["w_fg"].rearrange("(k p) n -> p k n", p=P)), s_in[2], 16, *f0)
            t2 = SP.dma(lambda e: e.dma_start(wb, A["b_fg"].to_broadcast([P, H])), s_in[3], 16, *f1)
            wv = wf.rearrange("p (k n) -> p k n", k=8)
            a = AC.do(lambda e: e.activation(wfgH[:, :, :], wv, ACT.Copy), t1)
            c = DV.do(lambda e: e.tensor_tensor(out=wfgL[:, :, :], in0=wv, in1=wfgH[:, :, :].bitcast(f32),
                                                op=ALU.subtract), t1, a)
            b = ring.take()
            PE.wait(a, c, *th, *bank_readers[b])
            for t in range(2):
                for k in range(KT):
                    for n, (h_, w_) in enumerate(((hH, wfgH), (hH, wfgL), (hL, wfgH))):
                        f = lambda e, t=t, k=k, n=n, h_=h_, w_=w_: e.matmul(
                            bank(b)[:, H * t:H * t + H], h_[:, k, P * t:P * t + P], w_[:, k, :],
                            start=(k == 0 and n == 0), stop=(k == KT - 1 and n == 2))
                        tp = PE.do(f) if (t == 1 and k == KT - 1 and n == 2) else PE.quiet(f)
            z = w2[:, 0:32].rearrange("p (t n) -> p t n", t=2)
            y = w2[:, 32:64].rearrange("p (t n) -> p t n", t=2)
            a = DV.do(lambda e: e.tensor_tensor(out=z, in0=bank(b)[:, 0:32].rearrange("p (t n) -> p t n", t=2),
                                                in1=wb.unsqueeze(1).to_broadcast([P, 2, H]), op=ALU.add), tp, t2, *f2)
            bank_readers[b] = (a,)
            d = DV.do(lambda e: e.scalar_tensor_tensor(out=y, in0=z, scalar=-1.0, in1=z, op0=ALU.mult, op1=ALU.max), a)
            d = AC.do(lambda e: e.activation(y, y, ACT.Exp, scale=-1.0), d)
            d = AC.do(lambda e: e.activation(y, y, ACT.Ln, bias=1.0), d)
            g = DV.do(lambda e: e.tensor_single_scalar(z, z, 0.0, ALU.min), a)
            g = DV.do(lambda e: e.tensor_tensor(out=y, in0=y, in1=z, op=ALU.subtract), d, g)
            b2 = ring.take()
            PE.wait(g, t_const, *bank_readers[b2])
            PE.quiet(lambda e: e.matmul(bank(b2)[0:H, 0:128], y[:, 0, :], tri_le[:, :], start=True, stop=True))
            PE.quiet(lambda e: e.matmul(bank(b2)[0:H, 128:256], y[:, 0, :], ones[:, :], start=True, stop=False))
            t = PE.do(lambda e: e.matmul(bank(b2)[0:H, 128:256], y[:, 1, :], tri_le[:, :], start=False, stop=True))
            r = DV.do(lambda e: e.tensor_copy(ncum[:, :], bank(b2)[0:H, 0:256]), t)
            bank_readers[b2] = (r,)
            tmp.free(i0, a, c)
            tmp.free(i1, a)
            tmp.free(i2, t)
            return r

        def out_product(name, th, nch, sH, sL, rate, upto):
            for i in range(nch):
                t = tokmajor(name, th, sH, sL, 2 * nch, i)
                split_next()
                mods(rate, upto)
            return t

        def differential(th, tmod):
            i0, tb, f0 = tmp.take()
            t_tab = SP.dma(lambda e: e.dma_start(tb, A["rope"]), s_in[4], 16, *f0)
            i1, gb_, f1 = tmp.take()
            t_g = SP.dma(lambda e: e.dma_start(gb_[:, 0:256], A["qkg"].to_broadcast([P, 256])), s_in[5], 16, *f1)
            tv_ = tb[:, 0:256].rearrange("p (c t d) -> p c t d", c=2, t=2)
            gv_ = gb_[:, 0:256].rearrange("p (n c d) -> p n c d", n=2, c=2)
            tr = []
            for n in range(2):
                for c in range(2):
                    tr.append(DV.do(lambda e, n=n, c=c: e.scalar_tensor_tensor(
                        out=rope[:, 2 * n + c, :, :], in0=tv_[:, c], scalar=(0.125 if n == 0 else 1.0),
                        in1=gv_[:, n, c].unsqueeze(1).to_broadcast([P, 2, 64]), op0=ALU.mult, op1=ALU.mult), t_tab, t_g))
            tkg = DV.do(lambda e: e.tensor_copy(kgt[:, :], gv_[:, 1, 0]), t_g)
            tr.append(tkg)
            tmp.free(i0, *tr)
            tmp.free(i1, *tr)
            cx = att[:, 8192:10240].rearrange("p (t d) -> p t d", t=2)
            tcx = SP.dma(lambda e: e.dma_start(cx, A["ctx"].rearrange("o (t p) d -> p (o t) d", p=P)), s_in[6], 16,
                         *last_att[0], *last_a[0])
            tc = norm_T(cx, [tcx, tcx], 4, oH, oL, tmod, (*last_o[0], *last_a[0]))
            lam = lam_value(f_ready=())
            kgain = kgt[:, :]
            thc = (*th, *tc)
            units = []
            for g in range(6):
                kind, half = g // 2, g % 2
                toks = range(2) if kind == 0 else range(4)
                bs = [(4 * (g % 2)) + t for t in toks]
                for q in range(2):
                    s, wh, wl = chunk("qkv2")
                    wh = wh.rearrange("p (k n) -> p k n", k=4)
                    wl = wl.rearrange("p (k n) -> p k n", k=4)
                    PE.wait(*thc)
                    for t in toks:
                        if q == 0:
                            PE.wait(*bank_readers[bs[t]])
                        sH, sL, tt = (hH, hL, t) if t < 2 else (oH, oL, t - 2)
                        for j in range(4):
                            k = 4 * q + j
                            for n, (h_, w_) in enumerate(((sH, wh), (sH, wl), (sL, wh))):
                                f = lambda e, h_=h_, w_=w_, j=j, k=k, n=n, tt=tt, t=t: e.matmul(
                                    bank(bs[t]), h_[:, k, P * tt:P * tt + P], w_[:, j, :],
                                    start=(k == 0 and n == 0), stop=(k == KT - 1 and n == 2))
                                tp = PE.do(f) if (j == 3 and n == 2) else PE.quiet(f)
                        if q == 1:
                            units.append((kind, half, t, bs[t], tp))
                    used(s, tp)
                    split_next()
                    if kind == 0:
                        mods(MOD_RATE[2][0], (2, 5))
                ring2.b = 3 if g % 2 else 7
                for u in units:
                    head_unit(*u, tr, kgain)
                units = []
            last_o_read = (tp,)
            last_o[0] = last_o_read
            return tp, lam

        unit_last = [None]
        tqk = {"q": [], "k": [], "v": []}

        def head_unit(kind, half, t, b, tp, tr, kgain):
            if kind == 2:
                e1 = AC.do(lambda e: e.activation(v2[:, t, 512 * half:512 * half + 512], bank(b), ACT.Copy), tp,
                           *last_att[0], *last_a[0], xn_free[0][0])
                bank_readers[b] = (e1,)
                tqk["v"].append(e1)
                return
            i, y, fr = tmp.take()
            i2, w, fr2 = tmp.take()
            ss = cols(8)
            a = AC.do(lambda e: e.activation(y, bank(b), ACT.Square), tp, *fr)
            a = DV.do(lambda e: e.tensor_reduce(ss, y.rearrange("p (h d) -> p h d", h=8), AX.X, ALU.add), a)
            r = rstd(ss, 64, 8, a)
            yv, wv = (q_.rearrange("p (h d) -> p h d", h=8) for q_ in (y, w))
            a = DV.do(lambda e: e.tensor_tensor(out=yv, in0=bank(b).rearrange("p (h d) -> p h d", h=8),
                                                in1=ss.unsqueeze(2).to_broadcast([P, 8, 64]), op=ALU.mult), r)
            bank_readers[b] = (a,)
            if t >= 2:
                a = DV.do(lambda e: e.tensor_tensor(out=wv, in0=yv, in1=kgain.unsqueeze(1).to_broadcast([P, 8, 64]),
                                                    op=ALU.mult), a, *fr2, *tr)
            else:
                cs = rope[:, 2 * kind, t, :].unsqueeze(1).to_broadcast([P, 8, 64])
                w5 = w.rearrange("p (g n d) -> p g n d", n=2, d=16)
                y5 = y.rearrange("p (g n d) -> p g n d", n=2, d=16)
                sn = rope[:, 2 * kind + 1, t, :].rearrange("p (r n d) -> p r n d", r=2, n=2)
                for n in range(2):
                    for r_ in range(2):
                        wq = w.rearrange("p (h r n d) -> p h r n d", r=2, n=2, d=16)[:, :, r_, n, :]
                        yq = y.rearrange("p (h r n d) -> p h r n d", r=2, n=2, d=16)[:, :, r_, 1 - n, :]
                        sq = sn[:, r_, n, :].unsqueeze(1).to_broadcast([P, 8, 16])
                        b1 = DV.do(lambda e, wq=wq, yq=yq, sq=sq: e.tensor_tensor(out=wq, in0=yq, in1=sq, op=ALU.mult),
                                   a, *fr2, *tr)
                c1 = DV.do(lambda e: e.tensor_tensor(out=yv, in0=yv, in1=cs, op=ALU.mult), a, b1, *tr)
                a = DV.do(lambda e: e.tensor_tensor(out=w, in0=w, in1=y, op=ALU.add), b1, c1)
            tmp.free(i, a)
            b2 = ring2.take()
            PE.wait(a, t_const, *bank_readers[b2])
            for j in range(4):
                f = lambda e, j=j: e.transpose(bank(b2)[:, P * j:P * j + P], w[:, P * j:P * j + P], ident[:, :])
                pt = PE.do(f) if j == 3 else PE.quiet(f)
            tmp.free(i2, pt)
            dst = (qT if kind == 0 else kT2)[:, 4 * half:4 * half + 4, P * t:P * t + P]
            e1 = AC.do(lambda e: e.activation(dst, bank(b2).rearrange("p (a b) -> p a b", a=4), ACT.Copy), pt,
                       *last_att[0], *last_a[0])
            bank_readers[b2] = (e1,)
            unit_last[0] = a
            tqk["qk"[kind]].append(e1)

        class Ring2:
            def take(self):
                return self.b
        ring2 = Ring2()
        ring2.b = 7

        def lam_value(f_ready):
            i, y, fr = tmp.take()
            lm = cols(4)
            t = SP.dma(lambda e: e.dma_start(y[:, 0:256], A["lam"].to_broadcast([P, 256])), s_in[7], 16, *fr)
            y4 = y[:, 0:256].rearrange("p (n c d) -> p n c d", n=2, c=2)
            w = y[:, 256:384].rearrange("p (n d) -> p n d", n=2)
            a = DV.do(lambda e: e.tensor_tensor(out=w, in0=y4[:, :, 0], in1=y4[:, :, 1], op=ALU.mult), t)
            a = DV.do(lambda e: e.tensor_reduce(lamc[:, 0:2], w, AX.X, ALU.add), a)
            tmp.free(i, a)
            a = AC.do(lambda e: e.activation(lamc[:, 0:2], lamc[:, 0:2], ACT.Exp), a)
            a = DV.do(lambda e: e.tensor_tensor(out=lamc[:, 2:3], in0=lamc[:, 1:2], in1=lamc[:, 0:1], op=ALU.subtract), a)
            return DV.do(lambda e: e.tensor_scalar(lamc[:, 2:3], lamc[:, 2:3], -LAM_INIT, None, ALU.add), a)

        lamc = sb("lamc", [P, 4])

        def diff_attention(tlam):
            sbk, tbk, obk = Banks([0, 1, 2, 3]), Banks([4, 5]), Banks([7])
            slots = tmp
            tall = (*tqk["q"], *tqk["k"])

            def scores(n, o):
                h, t = n // 2, n % 2
                bs, es, st_ = [], [], cols(4)
                nm, rs = st_[:, 0:2], st_[:, 2:4]
                tt = []
                for m in range(2):
                    g = 8 * m + h
                    hp, ht = 64 * (g % 2), g // 2
                    b = sbk.take()
                    bs.append(b)
                    tt.append(PE.do(lambda e: e.matmul(bank(b), qT[hp:hp + 64, ht, P * t:P * t + P], kT2[hp:hp + 64, ht, :],
                                                       start=True, stop=True), *tall, *bank_readers[b]))
                for m in range(2):
                    a = DV.do(lambda e: e.tensor_reduce(nm[:, m:m + 1], bank(bs[m]), AX.X, ALU.max, negate=True), tt[m])
                    i, y, fr = slots.take()
                    a = AC.do(lambda e: e.activation(y, bank(bs[m]), ACT.Exp, bias=nm[:, m:m + 1],
                                                     accum_out=rs[:, m:m + 1]), a, *fr)
                    bank_readers[bs[m]] = (a,)
                    es.append((i, y, a))
                o.update(es=es, rs=rs)

            def combine(n, o):
                rs, (i0, y0, a0), (i1, y1, a1) = o["rs"], *o["es"]
                a = DV.do(lambda e: e.reciprocal(rs, rs), a0, a1)
                a = DV.do(lambda e: e.tensor_tensor(out=rs[:, 1:2], in0=rs[:, 1:2], in1=lamc[:, 2:3], op=ALU.mult), a, tlam)
                b = DV.do(lambda e: e.tensor_scalar(y0, y0, rs[:, 0:1], None, ALU.mult), a)
                b = DV.do(lambda e: e.scalar_tensor_tensor(out=y0, in0=y1, scalar=rs[:, 1:2], in1=y0, op0=ALU.mult,
                                                           op1=ALU.add), b)
                slots.free(i1, b)
                o["t"] = b

            def turn(n, o):
                i0, y0, _ = o["es"][0]
                b = tbk.take()
                PE.wait(o["t"], t_const, *bank_readers[b])
                for j in range(4):
                    f = lambda e, j=j: e.transpose(bank(b)[:, P * j:P * j + P], y0[:, P * j:P * j + P], ident[:, :])
                    t = PE.do(f) if j == 3 else PE.quiet(f)
                o["ta"] = AC.do(lambda e: e.activation(y0, bank(b), ACT.Copy), t)
                bank_readers[b] = (o["ta"],)

            def values(n, o):
                h, t = n // 2, n % 2
                i0, y0, _ = o["es"][0]
                b = obk.take()
                PE.wait(o["ta"], *tqk["v"], *bank_readers[b])
                for j in range(4):
                    f = lambda e, j=j: e.matmul(bank(b)[:, 0:P], y0[:, P * j:P * j + P], v2[:, j, P * h:P * h + P],
                                                start=(j == 0), stop=(j == 3))
                    tp = PE.do(f) if j == 3 else PE.quiet(f)
                slots.free(i0, tp)
                e1 = DV.do(lambda e: e.tensor_copy(xn[:, t, P * h:P * h + P], bank(b)[:, 0:P]), tp, *xn_free[t])
                bank_readers[b] = (e1,)
                last_att[0] = (tp,)
                o_done[t] = e1

            for _ in pipeline([scores, combine, turn, values], 16):
                mods(MOD_RATE[2][0], (2, 5))
            i, gs, fr = tmp.take()
            tg = SP.dma(lambda e: e.dma_start(gs[:, 0:128], A["subln"].to_broadcast([P, P])), s_in[0], 32, *fr)
            tg = DV.do(lambda e: e.tensor_scalar(gs[:, 0:128], gs[:, 0:128], 1.0 - LAM_INIT, None, ALU.mult), tg)
            tn = []
            for t in range(2):
                ss = cols(8)
                for half in range(2):
                    i2, w, fr2 = tmp.take()
                    a = AC.do(lambda e: e.activation(w, xn[:, t, 512 * half:512 * half + 512], ACT.Square), o_done[t], *fr2)
                    a = DV.do(lambda e: e.tensor_reduce(ss[:, 4 * half:4 * half + 4], w.rearrange("p (h d) -> p h d", h=4),
                                                        AX.X, ALU.add), a)
                    tmp.free(i2, a)
                r = rstd(ss, 128, 8, a)
                xv = xn[:, t, :].rearrange("p (h d) -> p h d", h=8)
                a = DV.do(lambda e: e.tensor_tensor(out=xv, in0=xv, in1=ss.unsqueeze(2).to_broadcast([P, 8, P]), op=ALU.mult),
                          r, o_done[t])
                tn.append(DV.do(lambda e: e.tensor_tensor(out=xv, in0=xv, in1=gs[:, 0:128].unsqueeze(1).to_broadcast([P, 8, P]),
                                                          op=ALU.mult), a, tg))
            tmp.free(i, tn[-1])
            for k2_ in range(4):
                b = ring.take()
                PE.wait(*tn, *bank_readers[b])
                for j in range(2):
                    for t in range(2):
                        f = lambda e, j=j, t=t: e.transpose(bank(b)[:, 256 * j + P * t:256 * j + P * t + P],
                                                            xn[:, t, (2 * k2_ + j) * P:(2 * k2_ + j + 1) * P], ident[:, :])
                        pt = PE.do(f) if j == t == 1 else PE.quiet(f)
                last = split_T(bank(b).rearrange("p (a b) -> p a b", a=2), pt, oH[:, 2 * k2_:2 * k2_ + 2, :],
                               oL[:, 2 * k2_:2 * k2_ + 2, :], last_o[0])
                bank_readers[b] = last
            xn_free[0] = xn_free[1] = (pt,)
            return last

        o_done = [None, None]

        def short_conv(th):
            buf = att[:, 0:2 * 2 * 258].rearrange("p (b i t) -> p b i t", b=2, i=2)
            tz = DV.do(lambda e: e.memset(att[:, 0:1032], 0.0), *last_att[0], *last_a[0])
            prev = [(), ()]
            for j in range(4):
                bc, tc = featmajor("qkv3", th, hH, hL)
                i, cc, fr = tmp.take()
                a = AC.do(lambda e: e.activation(cc, bank(bc), ACT.Copy), tc, *fr)
                bank_readers[bc] = (a,)
                split_next()
                mods(MOD_RATE[3][0], (3, 5))
                bu, tu = featmajor("qkv3", th, hH, hL)
                pb = buf[:, j % 2]
                a = DV.do(lambda e: e.tensor_tensor(out=pb[:, :, 1:257], in0=bank(bu).rearrange("p (a b) -> p a b", a=2),
                                                    in1=cc.rearrange("p (a b) -> p a b", a=2), op=ALU.mult),
                          tu, a, tz, *prev[j % 2])
                tmp.free(i, a)
                bank_readers[bu] = (a,)
                i, y, fr = tmp.take()
                yv = y.rearrange("p (a b) -> p a b", a=2)
                for n in range(2):
                    f_ = 2 * j + n
                    w = [sm[:, SM[f"sc{k}"][0] + f_:SM[f"sc{k}"][0] + f_ + 1] for k in range(3)]
                    c = DV.do(lambda e: e.tensor_scalar(yv[:, n], pb[:, n, 1:257], w[1], None, ALU.mult), a, *fr)
                    c = DV.do(lambda e: e.scalar_tensor_tensor(out=yv[:, n], in0=pb[:, n, 0:256], scalar=w[0], in1=yv[:, n],
                                                               op0=ALU.mult, op1=ALU.add), c)
                    c = DV.do(lambda e: e.scalar_tensor_tensor(out=yv[:, n], in0=pb[:, n, 2:258], scalar=w[2], in1=yv[:, n],
                                                               op0=ALU.mult, op1=ALU.add), c)
                prev[j % 2] = (c,)
                split_next()
                mods(MOD_RATE[3][0], (3, 5))
                bb, tb = featmajor("qkv3", th, hH, hL)
                c = DV.do(lambda e: e.tensor_tensor(out=y, in0=bank(bb), in1=y, op=ALU.mult), tb, c)
                bank_readers[bb] = (c,)
                last = split_T(yv, c, oH[:, 2 * j:2 * j + 2, :], oL[:, 2 * j:2 * j + 2, :], (*last_o[0], *last_a[0]))
                tmp.free(i, *last)
                split_next()
                mods(MOD_RATE[3][0], (3, 5))
            return last, tb

        def ffn(l, th):
            free_a = (*last_a[0], *last_att[0], *last_o[0])
            rate = MOD_RATE[l][1]
            upto = (l + 1, 2)
            ta = []
            for j in range(11):
                bg, tg = featmajor("gate%d" % l, th, hH, hL)
                g = bank(bg).rearrange("p (a b) -> p a b", a=2)
                i, y, fr = tmp.take()
                yv = y.rearrange("p (a b) -> p a b", a=2)
                if l < 2:
                    col = lambda name, n: sm[:, SM[name][0] + 2 * j + n:SM[name][0] + 2 * j + n + 1]
                    for n in range(2):
                        a = AC.do(lambda e: e.activation(yv[:, n], g[:, n], ACT.Identity, bias=col(f"bc{l}", n),
                                                         scale=col(f"wc{l}2", n)), tg, *fr)
                    for n in range(2):
                        c = DV.do(lambda e: e.scalar_tensor_tensor(out=yv[:, n, 1:256], in0=g[:, n, 0:255],
                                                                   scalar=col(f"wc{l}1", n), in1=yv[:, n, 1:256],
                                                                   op0=ALU.mult, op1=ALU.add), a)
                    for n in range(2):
                        a = DV.do(lambda e: e.scalar_tensor_tensor(out=yv[:, n, 2:256], in0=g[:, n, 0:254],
                                                                   scalar=col(f"wc{l}0", n), in1=yv[:, n, 2:256],
                                                                   op0=ALU.mult, op1=ALU.add), c)
                    bank_readers[bg] = (a,)
                    a = AC.do(lambda e: e.activation(y, y, ACT.Silu), a)
                else:
                    a = AC.do(lambda e: e.activation(y, bank(bg), ACT.Silu), tg, *fr)
                    bank_readers[bg] = (a,)
                split_next()
                mods(rate, upto)
                bu, tu = featmajor("up%d" % l, th, hH, hL)
                a = DV.do(lambda e: e.tensor_tensor(out=y, in0=bank(bu), in1=y, op=ALU.mult), tu, a)
                bank_readers[bu] = (a,)
                last = split_T(yv, a, aH[:, 2 * j:2 * j + 2, :], aL[:, 2 * j:2 * j + 2, :], free_a)
                tmp.free(i, *last)
                ta.append(last)
                split_next()
                mods(rate, upto)
            for i in range(11):
                t = tokmajor("down%d" % l, ta[i], aH, aL, FT, i)
                split_next()
                mods(rate, upto)
            last_a[0] = (t,)
            return tu, t

        for l in range(LAYERS):
            tmod = (modt[(l, 0, 0)], modt[(l, 1, 0)])
            th = norm_T(x, tx, 0, hH, hL, tmod, hT_free[0])
            if l < 2:
                if l == 1:
                    tcum = forget_logits(th)
                t, tv = value_product(l, th)
                t, tq, tk = qk_products(l, th)
                hT_free[0] = (t,)
                AC.quiet(lambda e: e.preload_act_table_set("natural_log_exp_and_others"))
                gen = stick_breaking(tq, tk, tv) if l == 0 else forgetting(tq, tk, tv, tcum)
                for _ in gen:
                    mods(MOD_RATE[l][0], (l, 5))
                to = o_tok[0]
            elif l == 2:
                t, tlam = differential(th, (modt[(2, 0, 1)], modt[(2, 1, 1)]))
                hT_free[0] = (t,)
                to = diff_attention(tlam)
            else:
                to, t = short_conv(th)
                hT_free[0] = (t,)
                last_att[0] = (to[1],)
            t = out_product("wo%d" % l, to, 4, oH, oL, MOD_RATE[l][0], (l, 5))
            last_o[0] = (t,)
            mods_through(l, 4)
            tx = post(l, 0, t, (modt[(l, 2, 0)],))
            tmod = (modt[(l, 3, 0)], modt[(l, 4, 0)])
            th = norm_T(x, tx, 2, hH, hL, tmod, hT_free[0])
            mods_through(l, 5)
            t_h, t = ffn(l, th)
            hT_free[0] = (t_h,)
            if l + 1 < LAYERS:
                mods_through(l + 1, 1)
            tx = post(l, 1, t, (modt[(l, 5, 0)],))

        SP.dma(lambda e: e.dma_start(out.rearrange("o (t p) d -> p (o t) d", p=P), x[:, :, :]), s_out, 16, *tx)
        SP.wait((s_out, 16))


def kernel(**inputs):
    import concourse.bacc as _bacc
    from concourse import mybir as _mybir
    from concourse.bass_utils import run_bass_kernel_spmd as _run

    I = {k: np.asarray(v) for k, v in inputs.items() if k.startswith(("win_", "cf_")) is False}

    def feat(w):
        return np.ascontiguousarray(w.reshape(8, P, -1, 256).transpose(2, 1, 0, 3)).reshape(-1, P, 2048)

    def tok(w):
        return np.ascontiguousarray(w.reshape(-1, 2, P, 1024).transpose(0, 2, 1, 3)).reshape(-1, P, 2048)

    def tok512(w):
        return np.ascontiguousarray(w.reshape(2, 4, P, -1, 512).transpose(3, 0, 2, 1, 4)).reshape(-1, P, 2048)

    def cols(v):
        return np.ascontiguousarray(v.reshape(-1, P).T)

    arrays = {}
    for l in range(4):
        b, i = l // 2, l % 2
        mod, bm = (I["w_mod"][i], I["b_mod"][i]) if b == 0 else (I["ada_w_2"][i], I["ada_b_2"][i])
        arrays[f"mod{l}"] = np.concatenate([tok(mod[:, 1024 * p:1024 * p + 1024]) for p in range(6)])
        if b == 0:
            q = I["w_qkv"][i]
            arrays[f"qkv{l}"] = np.concatenate([feat(q[:, :2048]), tok(q[:, 2048:])])
            arrays[f"wo{l}"] = tok(I["w_o"][i])
            arrays[f"gate{l}"] = feat(I["w_ffn_gate"][i])
            arrays[f"up{l}"] = feat(I["w_ffn_up"][i])
            arrays[f"down{l}"] = tok(I["w_ffn_down"][i])
        else:
            arrays[f"qkv{l}"] = tok512(I["diff_w_qkv_2"][0]) if i == 0 else feat(I["sc_w_in_2"][0])
            arrays[f"wo{l}"] = tok(I["diff_w_o_2"][0] if i == 0 else I["sc_w_out_2"][0])
            arrays[f"gate{l}"] = feat(I["ffn_w_gate_up_2"][i][:, :FF])
            arrays[f"up{l}"] = feat(I["ffn_w_gate_up_2"][i][:, FF:])
            arrays[f"down{l}"] = tok(I["ffn_w_down_2"][i])
    parts = {"c": I["c"][0], "c2": I["c_2"][0], "cc": I["c_ctx_2"]}
    for l in range(4):
        b, i = l // 2, l % 2
        bm = I["b_mod"][i] if b == 0 else I["ada_b_2"][i]
        parts[f"g{l}a"] = I["g_mix_pre"][i] if b == 0 else I["norm1_2"][i]
        parts[f"g{l}f"] = I["g_ffn_pre"][i] if b == 0 else I["norm2_2"][i]
        for p in (0, 1, 3, 4):
            parts[f"b{l}{p}"] = bm[1024 * p:1024 * p + 1024]
        if b == 0:
            for k in range(3):
                parts[f"wc{l}{k}"] = I["w_conv"][i, k]
            parts[f"bc{l}"] = I["b_conv"][i]
    for k in range(3):
        parts[f"sc{k}"] = I["sc_conv_w_2"][0, k]
    arrays["smalls"] = np.ascontiguousarray(np.concatenate([cols(parts[n]) for n in SM], axis=1))
    gb = []
    for l in range(4):
        b, i = l // 2, l % 2
        bm = I["b_mod"][i] if b == 0 else I["ada_b_2"][i]
        for p, g in ((2, "g_mix_post"), (5, "g_ffn_post")):
            row = bm[1024 * p:1024 * p + 1024]
            gb.append(np.concatenate([row, I[g][i] if b == 0 else row]))
    arrays["gb"] = np.stack(gb)
    arrays["x"] = I["x"]
    arrays["ctx"] = I["ctx_2"]
    arrays["w_fg"] = np.ascontiguousarray(I["w_fg"][0])
    arrays["b_fg"] = np.ascontiguousarray(I["b_fg"])
    t = np.arange(S)
    inv = (np.float32(10000.0) ** (-np.arange(16, dtype=np.float32) / np.float32(16))).astype(np.float32)
    ar = (t // 64).astype(np.float32)[:, None] * inv
    ac = (t % 64).astype(np.float32)[:, None] * inv
    cs = np.concatenate([np.cos(ar), np.cos(ar), np.cos(ac), np.cos(ac)], axis=1)
    sn = np.concatenate([-np.sin(ar), np.sin(ar), -np.sin(ac), np.sin(ac)], axis=1)
    tab = np.stack([cs, sn]).astype(np.float32).reshape(2, 2, P, 64).transpose(2, 0, 1, 3).reshape(P, 256)
    arrays["rope"] = np.ascontiguousarray(np.concatenate([tab, tab], axis=1))
    swap = np.concatenate([np.arange(16, 32), np.arange(0, 16), np.arange(48, 64), np.arange(32, 48)])
    qn, kn = I["diff_q_norm_2"][0], I["diff_k_norm_2"][0]
    arrays["qkg"] = np.concatenate([qn, qn[swap], kn, kn[swap]])[None, :]
    arrays["lam"] = np.concatenate([I["diff_lam_q1_2"][0], I["diff_lam_k1_2"][0], I["diff_lam_q2_2"][0],
                                    I["diff_lam_k2_2"][0]])[None, :]
    arrays["subln"] = np.ascontiguousarray(I["diff_subln_2"])

    nc = _bacc.Bacc("TRN2", target_bir_lowering=False, num_devices=1)
    A, feed = {}, {}
    for name, a in arrays.items():
        feed["in_" + name] = a
        A[name] = nc.dram_tensor("in_" + name, a.shape, _mybir.dt.from_np(a.dtype), kind="ExternalInput").ap()
    o = nc.dram_tensor("out_0_dram", (1, S, D), _mybir.dt.float32, kind="ExternalOutput").ap()
    build(nc, A, o)
    r = _run(nc, [feed], core_ids=[0])
    return r.results[0]["out_0_dram"]
```

```python
import numpy as np
from contextlib import ExitStack
import concourse.bass as bass
from concourse import mybir

D, S, FF, H, P = 1024, 256, 2816, 16, 128
KT, FT = D // P, FF // P
EPS = 1e-6
NRAW, NSPL = 4, 6
LAYERS = 4
LAM_INIT = 0.8 - 0.6 * float(np.exp(-0.3 * 0))
NEG = -1e30

SM = {}


def _layout():
    at = 0
    for name, n in [("c", 8), ("c2", 8), ("cc", 8)] + [(f"g{l}{k}", 8) for l in range(4) for k in "af"] + \
            [(f"b{l}{p}", 8) for l in range(4) for p in (0, 1, 3, 4)] + \
            [(f"wc{l}{k}", FT) for l in range(2) for k in range(3)] + [(f"bc{l}", FT) for l in range(2)] + \
            [(f"sc{k}", 8) for k in range(3)] + [("bf", 1)]:
        SM[name] = (at, n)
        at += n
    return at


NSM = _layout()


class Queue:

    def __init__(self, eng, sem):
        self.eng, self.sem, self.n, self.seen = eng, sem, 0, {}

    def wait(self, *tokens):
        for sem, value in tokens:
            if self.seen.get(sem.name, 0) < value:
                self.eng.wait_ge(sem, value)
                self.seen[sem.name] = value

    def do(self, f, *tokens):
        self.wait(*tokens)
        self.n += 1
        f(self.eng).then_inc(self.sem, 1)
        return self.sem, self.n

    def quiet(self, f, *tokens):
        self.wait(*tokens)
        f(self.eng)

    def dma(self, f, sem, value, *tokens):
        self.wait(*tokens)
        f(self.eng).then_inc(sem, 16)
        return sem, value


class Slots:

    def __init__(self, items):
        self.items, self.at, self.readers = items, 0, [()] * len(items)

    def take(self):
        i = self.at % len(self.items)
        self.at += 1
        readers, self.readers[i] = self.readers[i], None
        assert readers is not None, "a buffer is taken before it is free"
        return i, self.items[i], readers

    def free(self, i, *tokens):
        self.readers[i] = tokens


def build(nc, A, out):
    f32, f32r = mybir.dt.float32, mybir.dt.float32r
    ALU, ACT, AX = mybir.AluOpType, mybir.ActivationFunctionType, mybir.AxisListType
    stack = ExitStack()
    with stack:
        def sb(name, shape, dt=f32):
            return stack.enter_context(nc.sbuf_tensor(name, shape, dt))

        with nc.sbuf_tensor("att", [P, 10240], f32) as att, nc.sbuf_tensor("oHL", [P, 2, KT, S], f32r) as oHL:
            pass
        aHL = sb("aHL", [P, 2, FT, S], f32r)
        sb("fill", [P, 14336 - 2 * FT * S], f32)
        raw = sb("raw", [P, NRAW, 2048])
        whi = sb("whi", [P, NSPL, 1024], f32r)
        wlo = sb("wlo", [P, NSPL, 1024], f32r)
        x = sb("x", [P, 2, D])
        hHL = sb("hHL", [P, 2, KT, S], f32r)
        gtb = sb("gtb", [P, 2, D])
        acc = sb("acc", [P, 2, D])
        xn = sb("xn", [P, 2, D])
        tmpt = sb("tmp", [P, 7, 512])
        sm = sb("sm", [P, NSM])
        modc = sb("modc", [P, 6, 8])
        ccol = sb("ccol", [P, 3, 8])
        ident = sb("ident", [P, P])
        ones = sb("ones", [P, P])
        tri_ge = sb("tri_ge", [P, P])
        tri_le = sb("tri_le", [P, P])
        msk = sb("msk", [P, P])
        st = sb("st", [P, 64])
        rope = sb("rope", [P, 4, 2, 64])
        kgt = sb("kgt", [P, 64])
        phalf = sb("phalf", [P, 16])
        ncum = sb("ncum", [H, S])
        mat = stack.enter_context(nc.psum_tensor("mat", [P, 8, 512], f32))

        sem = lambda n: stack.enter_context(nc.semaphore(n))
        PE, AC, DV, PO, SP = (Queue(e, sem(n)) for e, n in (
            (nc.tensor, "s_pe"), (nc.scalar, "s_act"), (nc.vector, "s_dve"), (nc.gpsimd, "s_pool"), (nc.sync, "s_sp")))
        s_raw = [sem(f"s_raw{i}") for i in range(NRAW)]
        s_in = [sem(f"s_in{i}") for i in range(8)]
        s_out = sem("s_out")

        aH, aL = aHL[:, 0], aHL[:, 1]
        hH, hL = hHL[:, 0], hHL[:, 1]
        oH, oL = oHL[:, 0], oHL[:, 1]
        bank_readers = [() for _ in range(8)]
        tmp = Slots([tmpt[:, i, :] for i in range(7)])
        last_att = [()]
        last_o = [()]
        last_a = [()]

        def bank(b):
            return mat[:, b, :]

        class Banks:
            def __init__(self, ids):
                self.ids, self.at = ids, 0

            def take(self):
                b = self.ids[self.at % len(self.ids)]
                self.at += 1
                return b

        ring = Banks([4, 5, 7])
        mring = Banks([6])

        def load(dst, src, i):
            return SP.dma(lambda e: e.dma_start(dst, src), s_in[i], 16)

        t_sm = load(sm[:, :], A["smalls"], 0)

        m0 = DV.do(lambda e: e.memset(ident[:, :], 0.0))
        m1 = DV.do(lambda e: e.memset(ones[:, :], 1.0))
        m2 = DV.do(lambda e: e.memset(phalf[:, :], -0.5))
        k0 = PO.do(lambda e: e.affine_select(out=ident[:, :], in_=ident[:, :], compare_op=ALU.not_equal, fill=1.0,
                                             base=0, pattern=[[-1, P]], channel_multiplier=1), m0, m1, m2)
        k1 = PO.do(lambda e: e.affine_select(out=tri_ge[:, :], in_=ones[:, :], compare_op=ALU.is_ge, fill=0.0,
                                             base=0, pattern=[[-1, P]], channel_multiplier=1))
        k2 = PO.do(lambda e: e.affine_select(out=tri_le[:, :], in_=ones[:, :], compare_op=ALU.is_ge, fill=0.0,
                                             base=0, pattern=[[1, P]], channel_multiplier=-1))
        t_const = k2
        one_row = ones[0:H, 0:1].to_broadcast([H, S])

        def strict_mask(l_tokens):
            return PO.do(lambda e: e.affine_select(out=msk[:, :], in_=ones[:, :], compare_op=ALU.is_gt, fill=0.0,
                                                   base=0, pattern=[[1, P]], channel_multiplier=-1), *l_tokens)

        t_c = AC.do(lambda e: e.activation(ccol[:, :, :], sm[:, 0:24].rearrange("p (a b) -> p a b", a=3), ACT.Silu), t_sm)

        nraw = [0]
        raw_free = [()] * NRAW

        def fetch(src):
            i = nraw[0] % NRAW
            v = 16 * (nraw[0] // NRAW + 1)
            nraw[0] += 1
            free, raw_free[i] = raw_free[i], None
            assert free is not None, "a slot of the ring is filled before it is free"
            dst = raw[:, i, 0:src.shape[-1]]
            return i, SP.dma(lambda e: e.dma_start(dst, src), s_raw[i], v, *free)

        wseq = []
        for l in range(LAYERS):
            if l < 2:
                wseq += [("wfg", 0)] if l == 1 else []
                wseq += [("qkv%d" % l, 8 + i) for i in range(4)]
                for j in range(4):
                    wseq += [("qkv%d" % l, j), ("qkv%d" % l, 4 + j)]
            elif l == 2:
                wseq += [("qkv2", i) for i in (8, 9, 10, 11, 4, 5, 6, 7, 0, 1, 2, 3)]
            else:
                for j in range(4):
                    wseq += [("qkv3", 4 + j), ("qkv3", 8 + j), ("qkv3", j)]
            wseq += [("wo%d" % l, i) for i in range(4)]
            for j in range(11):
                wseq += [("gate%d" % l, j), ("up%d" % l, j)]
            wseq += [("down%d" % l, i) for i in range(11)]
        split_free = [()] * NSPL
        ready = []
        nsplit = [0]

        hseq = [(name, c, h) for name, c in wseq for h in range(2)]
        part = [None]

        def split_half():
            if nsplit[0] == len(hseq):
                return
            s = nsplit[0] % NSPL
            name, c, half = hseq[nsplit[0]]
            if half == 0:
                part[0] = fetch(A[name][c])
            i, t = part[0]
            nsplit[0] += 1
            if name == "wfg" and half:
                ready.append((s, *ready[-1][1:]))
                return
            src = raw[:, i, 1024 * half:1024 * half + 1024]
            free, split_free[s] = split_free[s], None
            assert free is not None, "a slot is split into before TensorE has done with it"
            hi = AC.do(lambda e: e.activation(whi[:, s, :], src, ACT.Copy), t, *free)
            lo = DV.do(lambda e: e.tensor_tensor(out=wlo[:, s, :], in0=src, in1=whi[:, s, :].bitcast(f32),
                                                 op=ALU.subtract), t, hi, *free)
            if half or name == "wfg":
                raw_free[i] = (lo,)
            ready.append((s, hi, lo, name))

        nused = [0]

        def half_chunk(name):
            s, hi, lo, got = ready[nused[0]]
            assert got == name, (got, name)
            nused[0] += 1
            PE.wait(hi, lo)
            return s, whi[:, s, :], wlo[:, s, :]

        def used(s, token):
            split_free[s] = (token,)

        modq = [(l, p, i) for l in range(LAYERS) for p in range(6) for i in range(4)]
        nmod = [0]
        acc_free = [(), ()]
        pending = []
        modt = {}
        gfree = [(), ()]
        cfree = []

        def mod_step():
            while pending:
                pending.pop(0)()
            if nmod[0] == len(modq):
                return
            l, p, q = modq[nmod[0]]
            nmod[0] += 1
            i, t = fetch(A["mod%d" % l][4 * p + q])
            accs = [(0, 0 if l < 2 else 1)] + ([(1, 2)] if l == 2 and p < 2 else [])
            last = None
            for a, c in accs:
                for j in range(2):
                    kt = 2 * q + j
                    src = raw[:, i, 1024 * j:1024 * j + 1024]
                    cs = ccol[:, c, kt:kt + 1]
                    if kt == 0:
                        last = DV.do(lambda e, src=src, cs=cs, a=a: e.tensor_scalar(acc[:, a, :], src, cs, None, ALU.mult),
                                     t, t_c, *acc_free[a])
                    else:
                        last = DV.do(lambda e, src=src, cs=cs, a=a: e.scalar_tensor_tensor(
                            out=acc[:, a, :], in0=src, scalar=cs, in1=acc[:, a, :], op0=ALU.mult, op1=ALU.add),
                            t, acct[a])
                    acct[a] = last
            raw_free[i] = (last,)
            if q == 3:
                if p in (2, 5):
                    gi, gtok = fetch(A["gb"][2 * l + (p == 5):2 * l + (p == 5) + 1, :].to_broadcast([P, 2048]))
                    pending.append(lambda: gate_rows(l, p, acct[0], gi, gtok))
                else:
                    for a, c in accs:
                        pending.append(lambda a=a: columns(l, p, a, acct[a]))

        acct = [None, None]

        def columns(l, p, a, t_acc):
            b = mring.take()
            PE.wait(t_acc, m1, *bank_readers[b])
            for k in range(8):
                f = lambda e, k=k: e.matmul(bank(b)[:, k:k + 1], acc[:, a, k * P:k * P + P], ones[:, 0:1],
                                            start=True, stop=True)
                t = PE.do(f) if k == 7 else PE.quiet(f)
            acc_free[a] = (t,)
            row = (4 if a else 0 if p < 3 else 2) + (p in (1, 4))
            o, _ = SM[f"b{l}{p}"]
            t1 = DV.do(lambda e: e.tensor_tensor(out=modc[:, row, :], in0=bank(b)[:, 0:8], in1=sm[:, o:o + 8],
                                                 op=ALU.add), t, t_sm, *cfree)
            del cfree[:]
            bank_readers[b] = (t1,)
            if p in (1, 4):
                o2, _ = SM[f"g{l}" + ("a" if p == 1 else "f")]
                t1 = DV.do(lambda e: e.scalar_tensor_tensor(out=modc[:, row, :], in0=modc[:, row, :], scalar=1.0,
                                                            in1=sm[:, o2:o2 + 8], op0=ALU.add, op1=ALU.mult), t1)
            modt[(l, p, a)] = t1

        def gate_rows(l, p, t_acc, gi, gtok):
            g = int(p == 5)
            for half in range(2):
                b = mring.take()
                c = slice(512 * half, 512 * half + 512)
                t = PE.do(lambda e: e.matmul(bank(b), ones[:, :], acc[:, 0, c], start=True, stop=True),
                          t_acc, m1, *bank_readers[b])
                t1 = DV.do(lambda e: e.tensor_tensor(out=gtb[:, g, c], in0=bank(b), in1=raw[:, gi, c], op=ALU.add),
                           t, gtok, *gfree[g])
                bank_readers[b] = (t1,)
                if l < 2:
                    c2 = slice(1024 + 512 * half, 1536 + 512 * half)
                    t1 = DV.do(lambda e: e.tensor_tensor(out=gtb[:, g, c], in0=gtb[:, g, c], in1=raw[:, gi, c2],
                                                         op=ALU.mult), t1, gtok)
            acc_free[0] = (t,)
            raw_free[gi] = (t1,)
            modt[(l, p, 0)] = t1

        mod_debt = [0.0]

        def mods(rate, upto):
            mod_debt[0] += rate
            while mod_debt[0] >= 1.0:
                mod_debt[0] -= 1.0
                if nmod[0] < len(modq) and modq[nmod[0]][:2] <= upto:
                    mod_step()
                elif pending:
                    pending.pop(0)()

        def mods_through(l, p):
            while nmod[0] < len(modq) and modq[nmod[0]][:2] <= (l, p):
                mod_step()
            while pending:
                pending.pop(0)()

        stn = [0]

        def cols(n):
            if stn[0] + n > 64:
                stn[0] = 0
            stn[0] += n
            return st[:, stn[0] - n:stn[0]]

        def rstd(ss, n, width, t):
            a = PO.do(lambda e: e.tensor_scalar(ss, ss, 1.0 / n, EPS, ALU.mult, ALU.add), t)
            return PO.do(lambda e: e.tensor_tensor(out=ss, in0=ss, in1=phalf[:, 0:width], op=ALU.pow), a, m2)

        xn_free = [(), ()]

        def norm_rows(src, tsrc):
            tx = []
            for t in range(2):
                ss = cols(1)
                a = AC.do(lambda e: e.activation(xn[:, t, :], src[:, t, :], ACT.Square, accum_out=ss), tsrc[t], *xn_free[t])
                r = rstd(ss, D, 1, a)
                tx.append(DV.do(lambda e: e.tensor_scalar(xn[:, t, :], src[:, t, :], ss, None, ALU.mult), r))
            return tx

        def norm_T(tx, row, dstH, dstL, tmod, wr):
            last = []
            for k2_ in range(4):
                b = ring.take()
                PE.wait(tx[0], t_const, *bank_readers[b])
                for t in range(2):
                    for j in range(2):
                        PE.wait(tx[t])
                        f = lambda e: e.transpose(bank(b)[:, 256 * j + P * t:256 * j + P * t + P],
                                                  xn[:, t, (2 * k2_ + j) * P:(2 * k2_ + j + 1) * P], ident[:, :])
                        if j == t == 1:
                            pt = PE.do(f)
                        else:
                            PE.quiet(f)
                i, tm, fr = tmp.take()
                for j in range(2):
                    kt = 2 * k2_ + j
                    o = tm[:, 256 * j:256 * j + 256]
                    g, h = modc[:, row + 1, kt:kt + 1], modc[:, row, kt:kt + 1]
                    if k2_ % 2:
                        e1 = AC.do(lambda e: e.activation(o, bank(b)[:, 256 * j:256 * j + 256], ACT.Identity,
                                                          bias=h, scale=g), pt, *fr, *tmod)
                    else:
                        e1 = DV.do(lambda e: e.tensor_scalar(o, bank(b)[:, 256 * j:256 * j + 256], g, h,
                                                             ALU.mult, ALU.add), pt, *fr, *tmod)
                bank_readers[b] = (e1,)
                cfree.append(e1)
                last += [split_T(tm.rearrange("p (a b) -> p a b", a=2), e1, dstH[:, 2 * k2_:2 * k2_ + 2, :],
                                 dstL[:, 2 * k2_:2 * k2_ + 2, :], wr)] * 2
                tmp.free(i, *last[-1])
            xn_free[0] = xn_free[1] = (pt,)
            return last

        def split_T(src, t, dh, dl, wr):
            a = AC.do(lambda e: e.activation(dh, src, ACT.Copy), t, *wr)
            b = DV.do(lambda e: e.tensor_tensor(out=dl, in0=src, in1=dh.bitcast(f32), op=ALU.subtract), a, *wr)
            return a, b

        def featmajor(name, th, sH, sL, tiles=2):
            b = bring.take()
            for i in range(tiles):
                s, wh, wl = half_chunk(name)
                wh = wh.rearrange("p (k n) -> p k n", k=8)
                wl = wl.rearrange("p (k n) -> p k n", k=8)
                if i == 0:
                    PE.wait(*bank_readers[b])
                o = bank(b)[:, 256 * i:256 * i + 256]
                for k in range(KT):
                    PE.wait(*th[k])
                    for n, (w, h) in enumerate(((wh, sH), (wh, sL), (wl, sH))):
                        f = lambda e: e.matmul(o, w[:, k, :], h[:, k, :], start=(k == 0 and n == 0),
                                               stop=(k == KT - 1 and n == 2))
                        if k == KT - 1 and n == 2:
                            t = PE.do(f)
                        else:
                            PE.quiet(f)
                used(s, t)
            return b, t

        bring = Banks([4, 7])

        def tokmajor(name, th, sH, sL, nk, first):
            last = first == nk // 2 - 1
            hs = []
            toks = [None, None]
            for j in range(2):
                s, wh, wl = half_chunk(name)
                hs.append((s, wh, wl))
                k = 2 * first + j
                if last and j == 0:
                    continue
                for t in range(2):
                    if first == 0 and j == 0:
                        PE.wait(*bank_readers[2 * t], *bank_readers[2 * t + 1])
                    for jj in (range(2) if last else (j,)):
                        k = 2 * first + jj
                        PE.wait(*th[k])
                        _, wh, wl = hs[jj]
                        for n, (h, w, half) in enumerate([(sH, wh, 0), (sH, wh, 1), (sH, wl, 0), (sH, wl, 1),
                                                          (sL, wh, 0), (sL, wh, 1)]):
                            f = lambda e: e.matmul(
                                mat[:, 2 * t + half, :], h[:, k, P * t:P * t + P], w[:, 512 * half:512 * half + 512],
                                start=(k == 0 and n < 2), stop=(k == nk - 1 and n >= 4))
                            if n == 5 and (jj == 1 or not last):
                                toks[t] = PE.do(f)
                            else:
                                PE.quiet(f)
                if not last:
                    used(s, toks[1])
            if last:
                for s, _, _ in hs:
                    used(s, toks[1])
            return toks

        def post(l, g, t_mm, tgt):
            tx = []
            for t in range(2):
                flat = mat[:, 2 * t:2 * t + 2, :]
                xv = xn[:, t, :].rearrange("p (a b) -> p a b", a=2)
                gv = gtb[:, g, :].rearrange("p (a b) -> p a b", a=2)
                if l < 2:
                    ss = cols(1)
                    a = AC.do(lambda e: e.activation(xv, flat, ACT.Square, accum_out=ss), t_mm[t], *xn_free[t])
                    r = rstd(ss, D, 1, a)
                    b = DV.do(lambda e: e.scalar_tensor_tensor(out=xv, in0=flat, scalar=ss, in1=gv, op0=ALU.mult,
                                                               op1=ALU.mult), r, *tgt)
                else:
                    b = DV.do(lambda e: e.tensor_tensor(out=xv, in0=flat, in1=gv, op=ALU.mult), t_mm[t], *tgt, *xn_free[t])
                c = DV.do(lambda e: e.tensor_tensor(out=x[:, t, :], in0=x[:, t, :], in1=xn[:, t, :], op=ALU.add), b)
                bank_readers[2 * t] = bank_readers[2 * t + 1] = (b,)
                xn_free[t] = (c,)
                tx.append(c)
            gfree[g] = (b,)
            return tx

        tx0 = SP.dma(lambda e: e.dma_start(x[:, :, :], A["x"].rearrange("o (t p) d -> p (o t) d", p=P)), s_in[1], 16)
        tx = [tx0, tx0]

        qT = att[:, 0:2048].rearrange("p (k t) -> p k t", k=8)
        kT = att[:, 2048:4096].rearrange("p (k t) -> p k t", k=8)
        v01 = att[:, 4096:6144].rearrange("p (t d) -> p t d", t=2)
        kT2 = att[:, 2048:6144].rearrange("p (k t) -> p k t", k=8)
        v2 = att[:, 6144:10240].rearrange("p (t d) -> p t d", t=4)
        att_slots = [att[:, 6144 + 384 * i:6144 + 384 * i + 384] for i in range(10)]

        hT_free = [()]
        MOD_RATE = {0: (0.8, 0.4), 1: (0.6, 0.4), 2: (0.7, 0.4), 3: (0.8, 0.0)}

        def value_product(l, th):
            for i in range(4):
                toks = tokmajor("qkv%d" % l, th, hH, hL, KT, i)
                if i < 3:
                    split_half()
                    split_half()
                    mods(MOD_RATE[l][0], (l, 5))
            split_half()
            tv = []
            for tt in range(2):
                dst = v01[:, tt, :].rearrange("p (a b) -> p a b", a=2)
                tv.append(AC.do(lambda e: e.activation(dst, mat[:, 2 * tt:2 * tt + 2, :], ACT.Copy), toks[tt],
                                *last_att[0], *last_a[0]))
                bank_readers[2 * tt] = bank_readers[2 * tt + 1] = (tv[-1],)
            split_half()
            return tv

        def qk_products(l, th, start_attention):
            tq, tk = [], []
            gen = None
            for j in range(4):
                for n, (dst, lst) in enumerate(((qT, tq), (kT, tk))):
                    b, t = featmajor("qkv%d" % l, th, hH, hL)
                    d = dst[:, 2 * j:2 * j + 2, :]
                    src = bank(b).rearrange("p (a b) -> p a b", a=2)
                    split_half()
                    if n == 0:
                        e1 = AC.do(lambda e: e.activation(d, src, ACT.Copy, scale=0.125), t, *last_att[0], *last_a[0])
                    else:
                        e1 = DV.do(lambda e: e.tensor_copy(d, src), t, *last_att[0], *last_a[0])
                    bank_readers[b] = (e1,)
                    lst.append(e1)
                    split_half()
                    mods(MOD_RATE[l][0], (l, 5))
                    if j:
                        next(gen)
                        next(gen)
                if j == 0:
                    gen = start_attention(tq, tk)
            hT_free[0] = (t,)
            for _ in gen:
                mods(MOD_RATE[l][0], (l, 5))

        def values_out(h, aT, ta, tv):
            hp, ht = 64 * (h % 2), h // 2
            if h % 2 == 0:
                obank[0] = obanks.take()
            b = obank[0]
            PE.wait(*ta, *tv)
            if h % 2 == 0:
                PE.wait(*bank_readers[b])
            vh = [v01[:, i, 64 * h:64 * h + 64] for i in range(2)]
            PE.quiet(lambda e: e.matmul(bank(b)[hp:hp + 64, 0:128], vh[0], aT[:, 0:128], start=True, stop=True))
            PE.quiet(lambda e: e.matmul(bank(b)[hp:hp + 64, 128:256], vh[0], aT[:, 128:256], start=True, stop=False))
            t = PE.do(lambda e: e.matmul(bank(b)[hp:hp + 64, 128:256], vh[1], aT[:, 256:384], start=False, stop=True))
            if h % 2:
                last = split_T(bank(b)[:, 0:256], t, oH[:, ht, :], oL[:, ht, :], (*last_o[0], *last_a[0]))
                bank_readers[b] = last
                o_tok[0].append(last)
            return t

        obanks, obank, o_tok = Banks([5]), [None], [()]

        def pipeline(stages, n):
            state = [dict() for _ in range(n)]
            for step in range(n + len(stages) - 1):
                for s_ in range(len(stages) - 1, -1, -1):
                    i = step - s_
                    if 0 <= i < n and stages[s_]:
                        stages[s_](i, state[i])
                yield

        def stick_breaking(tq, tk, tv):
            slots = Slots(att_slots)
            zb, rb = Banks([0, 1]), Banks([2, 3])
            tmask = strict_mask((m1,))

            def scores(h, o):
                hp, ht = 64 * (h % 2), h // 2
                b = zb.take()
                q, k = qT[hp:hp + 64, ht, :], kT[hp:hp + 64, ht, :]
                PE.wait(tq[ht // 2], tk[ht // 2], *bank_readers[b])
                PE.quiet(lambda e: e.matmul(bank(b)[:, 0:256], k[:, 0:128], q[:, 0:256], start=True, stop=True))
                t = PE.do(lambda e: e.matmul(bank(b)[:, 256:384], k[:, 128:256], q[:, 128:256], start=True, stop=True))
                i, z, fr = slots.take()
                o["zi"], o["z"] = i, z
                o["tz"] = AC.do(lambda e: e.activation(z, bank(b)[:, 0:384], ACT.Copy), t, *fr)
                bank_readers[b] = (o["tz"],)
                i2, w, fr2 = slots.take()
                a = DV.do(lambda e: e.scalar_tensor_tensor(out=w, in0=z, scalar=-1.0, in1=z, op0=ALU.mult, op1=ALU.max), o["tz"], *fr2)
                a = AC.do(lambda e: e.activation(w, w, ACT.Exp, scale=-1.0), a)
                a = AC.do(lambda e: e.activation(w, w, ACT.Ln, bias=1.0), a)
                o["wi"], o["w"], o["tw"] = i2, w, a

            def softplus(h, o):
                z, w = o["z"], o["w"]
                a = DV.do(lambda e: e.scalar_tensor_tensor(out=w, in0=z, scalar=0.0, in1=w, op0=ALU.max, op1=ALU.add), o["tw"])
                wd = w.rearrange("p (n t) -> p n t", n=3)[:, 0::2, :]
                o["tw"] = PO.do(lambda e: e.tensor_tensor(out=wd, in0=wd, in1=msk[:, :].unsqueeze(1).to_broadcast([P, 2, P]),
                                                          op=ALU.mult), a, tmask)

            def sums(h, o):
                b = rb.take()
                w, z = o["w"], o["z"]
                PE.wait(o["tw"], t_const, *bank_readers[b])
                PE.quiet(lambda e: e.matmul(bank(b)[:, 0:128], tri_ge[:, :], w[:, 0:128], start=True, stop=True))
                PE.quiet(lambda e: e.matmul(bank(b)[:, 128:256], tri_ge[:, :], w[:, 128:256], start=True, stop=False))
                PE.quiet(lambda e: e.matmul(bank(b)[:, 128:256], ones[:, :], w[:, 256:384], start=False, stop=True))
                t = PE.do(lambda e: e.matmul(bank(b)[:, 256:384], tri_ge[:, :], w[:, 256:384], start=True, stop=True))
                d = DV.do(lambda e: e.tensor_tensor(out=w, in0=z, in1=bank(b)[:, 0:384], op=ALU.subtract), t)
                bank_readers[b] = (d,)
                slots.free(o["zi"], d)
                wd = w.rearrange("p (n t) -> p n t", n=3)[:, 0::2, :]
                d = PO.do(lambda e: e.affine_select(out=wd, in_=wd, compare_op=ALU.is_gt, fill=NEG, base=0,
                                                    pattern=[[0, 2], [1, P]], channel_multiplier=-1), d)
                o["ta"] = AC.do(lambda e: e.activation(w, w, ACT.Exp), d)

            def values(h, o):
                t = values_out(h, o["w"], (o["ta"],), tv)
                slots.free(o["wi"], t)
                last_att[0] = (t,)

            return pipeline([scores, softplus, None, sums, None, values], H)

        def forgetting(tq, tk, tv, tcum):
            slots = Slots(att_slots)
            sbk, tbk = Banks([0, 1]), Banks([2, 3])
            a = PO.do(lambda e: e.tensor_scalar(msk[:, :], ones[:, :], -1.0, None, ALU.add), *last_att[0])
            tmask = PO.do(lambda e: e.affine_select(out=msk[:, :], in_=msk[:, :], compare_op=ALU.is_ge, fill=NEG,
                                                    base=0, pattern=[[-1, P]], channel_multiplier=1), a)

            def scores(h, o):
                hp, ht = 64 * (h % 2), h // 2
                b = sbk.take()
                q, k = qT[hp:hp + 64, ht, :], kT[hp:hp + 64, ht, :]
                eh = ident[0:H, h:h + 1].to_broadcast([H, P])
                PE.wait(tq[ht // 2], tk[ht // 2], tmask, tcum, t_const, *bank_readers[b])
                for c, t0, s0 in ((0, 0, 0), (128, 128, 0), (256, 128, 128)):
                    dst = bank(b)[:, c:c + P]
                    PE.quiet(lambda e: e.matmul(dst, q[:, t0:t0 + P], k[:, s0:s0 + P], start=True, stop=False))
                    f = lambda e: e.matmul(dst, eh, ncum[:, s0:s0 + P], start=False, stop=(c == 128))
                    PE.quiet(f)
                    if c != 128:
                        f2 = lambda e: e.matmul(dst, ident[:, :], msk[:, :], start=False, stop=True)
                        t = PE.do(f2) if c == 256 else PE.quiet(f2)
                nm, rs = cols(2), cols(2)
                a = DV.do(lambda e: e.tensor_reduce(nm[:, 0:1], bank(b)[:, 0:128], AX.X, ALU.max, negate=True), t)
                a = DV.do(lambda e: e.tensor_reduce(nm[:, 1:2], bank(b)[:, 128:384], AX.X, ALU.max, negate=True), t)
                i, p, fr = slots.take()
                a2 = AC.do(lambda e: e.activation(p[:, 0:128], bank(b)[:, 0:128], ACT.Exp, bias=nm[:, 0:1],
                                                  accum_out=rs[:, 0:1]), a, *fr)
                a2 = AC.do(lambda e: e.activation(p[:, 128:384], bank(b)[:, 128:384], ACT.Exp, bias=nm[:, 1:2],
                                                  accum_out=rs[:, 1:2]), a)
                bank_readers[b] = (a2,)
                o.update(p=p, pi=i, rs=rs, t=a2)

            def normalise(h, o):
                p, rs = o["p"], o["rs"]
                a = DV.do(lambda e: e.reciprocal(rs, rs), o["t"])
                DV.do(lambda e: e.tensor_scalar(p[:, 0:128], p[:, 0:128], rs[:, 0:1], None, ALU.mult), a)
                o["t"] = DV.do(lambda e: e.tensor_scalar(p[:, 128:384], p[:, 128:384], rs[:, 1:2], None, ALU.mult), a)

            def turn(h, o):
                p = o["p"]
                b = tbk.take()
                PE.wait(o["t"], *bank_readers[b])
                for c in (0, 128):
                    PE.quiet(lambda e, c=c: e.transpose(bank(b)[:, c:c + P], p[:, c:c + P], ident[:, :]))
                t = PE.do(lambda e: e.transpose(bank(b)[:, 256:384], p[:, 256:384], ident[:, :]))
                slots.free(o["pi"], t)
                i, w, fr = slots.take()
                o["w"], o["wi"] = w, i
                o["ta"] = DV.do(lambda e: e.tensor_copy(w, bank(b)[:, 0:384]), t, *fr)
                bank_readers[b] = (o["ta"],)

            def values(h, o):
                t = values_out(h, o["w"], (o["ta"],), tv)
                slots.free(o["wi"], t)
                last_att[0] = (t,)

            return pipeline([scores, normalise, None, turn, None, values], H)

        def forget_logits(th):
            b, tp = featmajor("wfg", th, hH, hL, tiles=1)
            used(half_chunk("wfg")[0], tp)
            split_half()
            split_half()
            i2, w2, f2 = tmp.take()
            z, y = w2[0:H, 0:256], w2[0:H, 256:512]
            bf = sm[0:H, SM["bf"][0]:SM["bf"][0] + 1]
            a = DV.do(lambda e: e.tensor_scalar(z, bank(b)[0:H, 0:256], bf, None, ALU.add), tp, *f2)
            bank_readers[b] = (a,)
            d = DV.do(lambda e: e.scalar_tensor_tensor(out=y, in0=z, scalar=-1.0, in1=z, op0=ALU.mult, op1=ALU.max), a)
            d = AC.do(lambda e: e.activation(y, y, ACT.Exp, scale=-1.0), d)
            d = AC.do(lambda e: e.activation(y, y, ACT.Ln, bias=1.0), d)
            g = DV.do(lambda e: e.scalar_tensor_tensor(out=z, in0=z, scalar=0.0, in1=y, op0=ALU.min, op1=ALU.subtract), d)
            r = DV.do(lambda e: e.tensor_tensor_scan(out=y, data0=one_row, data1=z, initial=0.0, op0=ALU.mult,
                                                     op1=ALU.subtract), g, m1)
            r = DV.do(lambda e: e.tensor_copy(ncum[:, :], y), r)
            tmp.free(i2, r)
            return r

        def out_product(name, th, nch, sH, sL, rate, upto):
            for i in range(nch):
                t = tokmajor(name, th, sH, sL, 2 * nch, i)
                if i < nch - 1:
                    split_half()
                    split_half()
                    mods(rate, upto)
            return t

        def differential(th, tmod):
            i0, tb, f0 = tmp.take()
            t_tab = SP.dma(lambda e: e.dma_start(tb, A["rope"]), s_in[4], 16, *f0)
            i1, gb_, f1 = tmp.take()
            t_g = SP.dma(lambda e: e.dma_start(gb_[:, 0:256], A["qkg"].to_broadcast([P, 256])), s_in[5], 16, *f1)
            tv_ = tb[:, 0:256].rearrange("p (c t d) -> p c t d", c=2, t=2)
            gv_ = gb_[:, 0:256].rearrange("p (n c d) -> p n c d", n=2, c=2)
            tr = []
            for n in range(2):
                for c in range(2):
                    tr.append(DV.do(lambda e, n=n, c=c: e.scalar_tensor_tensor(
                        out=rope[:, 2 * n + c, :, :], in0=tv_[:, c], scalar=(0.125 if n == 0 else 1.0),
                        in1=gv_[:, n, c].unsqueeze(1).to_broadcast([P, 2, 64]), op0=ALU.mult, op1=ALU.mult), t_tab, t_g))
            tkg = DV.do(lambda e: e.tensor_copy(kgt[:, :], gv_[:, 1, 0]), t_g)
            tr.append(tkg)
            tmp.free(i0, *tr)
            tmp.free(i1, *tr)
            tc = None
            cx = att[:, 8192:10240].rearrange("p (t d) -> p t d", t=2)
            tcx = SP.dma(lambda e: e.dma_start(cx, A["ctx"].rearrange("o (t p) d -> p (o t) d", p=P)), s_in[6], 16,
                         *last_att[0], *last_a[0])
            kgain = kgt[:, :]
            units, turns = [], []
            order = [(2, 0), (2, 1), (1, 0), (1, 1), (0, 0), (0, 1)]
            for g, (kind, half) in enumerate(order):
                toks = range(2) if kind == 0 else range(4)
                bs = [(2 * (g % 2) if kind == 0 else 0) + t for t in toks]
                for q in range(2):
                    for t in toks:
                        if q == 0:
                            PE.wait(*bank_readers[bs[t]])
                    hs = [half_chunk("qkv2") for _ in range(2)]
                    for t in toks:
                        if t == 2 and tc is None:
                            tc = norm_T(norm_rows(cx, [tcx, tcx]), 4, oH, oL, tmod, (*last_o[0], *last_a[0]))
                            lam = lam_value()
                        sH, sL, tt, tk_ = (hH, hL, t, th) if t < 2 else (oH, oL, t - 2, tc)
                        for p2 in range(2):
                            _, wh, wl = hs[p2]
                            wh = wh.rearrange("p (k n) -> p k n", k=2)
                            wl = wl.rearrange("p (k n) -> p k n", k=2)
                            for j in range(2):
                                k = 4 * q + 2 * p2 + j
                                PE.wait(*tk_[k])
                                for n, (h_, w_) in enumerate(((sH, wh), (sH, wl), (sL, wh))):
                                    f = lambda e: e.matmul(bank(bs[t]), h_[:, k, P * tt:P * tt + P], w_[:, j, :],
                                                           start=(k == 0 and n == 0), stop=(k == KT - 1 and n == 2))
                                    if p2 == 1 and j == 1 and n == 2:
                                        tp = PE.do(f)
                                    else:
                                        PE.quiet(f)
                        if q == 1:
                            units.append((kind, half, t, bs[t], tp))
                    for s_, _, _ in hs:
                        used(s_, tp)
                    if q == 1:
                        while turns:
                            turns.pop(0)()
                        normed = [head_norm(*u) for u in units]
                        scaled = [head_scale(*u, n) for u, n in zip(units, normed) if n]
                    split_half()
                    split_half()
                    mods(MOD_RATE[2][0], (2, 5))
                normed = [(*n, a_) for n, a_ in zip(normed, scaled)] if kind < 2 else normed
                turns = [head_rope(*u, n, tr, kgain) for u, n in zip(units, normed) if n]
                units = []
            while turns:
                turns.pop(0)()
            last_o[0] = (tp,)
            return tp, lam

        tqk = {"q": [], "k": [], "v": []}

        def head_norm(kind, half, t, b, tp):
            if kind == 2:
                e1 = AC.do(lambda e: e.activation(v2[:, t, 512 * half:512 * half + 512], bank(b), ACT.Copy), tp,
                           *last_att[0], *last_a[0], xn_free[0][0])
                bank_readers[b] = (e1,)
                tqk["v"].append(e1)
                return None
            i, y, fr = tmp.take()
            ss = cols(8)
            a = AC.do(lambda e: e.activation(y, bank(b), ACT.Square), tp, *fr)
            a = DV.do(lambda e: e.tensor_reduce(ss, y.rearrange("p (h d) -> p h d", h=8), AX.X, ALU.add), a)
            return i, y, ss, rstd(ss, 64, 8, a)

        def head_scale(kind, half, t, b, tp, normed):
            i, y, ss, r = normed
            a = DV.do(lambda e: e.tensor_tensor(out=y.rearrange("p (h d) -> p h d", h=8),
                                                in0=bank(b).rearrange("p (h d) -> p h d", h=8),
                                                in1=ss.unsqueeze(2).to_broadcast([P, 8, 64]), op=ALU.mult), r)
            bank_readers[b] = (a,)
            return a

        def head_rope(kind, half, t, b, tp, normed, tr, kgain):
            i, y, ss, r, a = normed
            i2, w, fr2 = tmp.take()
            yv, wv = (q_.rearrange("p (h d) -> p h d", h=8) for q_ in (y, w))
            if t >= 2:
                a = DV.do(lambda e: e.tensor_tensor(out=wv, in0=yv, in1=kgain.unsqueeze(1).to_broadcast([P, 8, 64]),
                                                    op=ALU.mult), a, *fr2, *tr)
            else:
                cs = rope[:, 2 * kind, t, :].unsqueeze(1).to_broadcast([P, 8, 64])
                w5 = w.rearrange("p (g n d) -> p g n d", n=2, d=16)
                y5 = y.rearrange("p (g n d) -> p g n d", n=2, d=16)
                sn = rope[:, 2 * kind + 1, t, :].rearrange("p (r n d) -> p r n d", r=2, n=2)
                for n in range(2):
                    for r_ in range(2):
                        wq = w.rearrange("p (h r n d) -> p h r n d", r=2, n=2, d=16)[:, :, r_, n, :]
                        yq = y.rearrange("p (h r n d) -> p h r n d", r=2, n=2, d=16)[:, :, r_, 1 - n, :]
                        sq = sn[:, r_, n, :].unsqueeze(1).to_broadcast([P, 8, 16])
                        b1 = DV.do(lambda e, wq=wq, yq=yq, sq=sq: e.tensor_tensor(out=wq, in0=yq, in1=sq, op=ALU.mult),
                                   a, *fr2, *tr)
                c1 = DV.do(lambda e: e.tensor_tensor(out=yv, in0=yv, in1=cs, op=ALU.mult), a, b1, *tr)
                a = DV.do(lambda e: e.tensor_tensor(out=w, in0=w, in1=y, op=ALU.add), b1, c1)
            tmp.free(i, a)

            def turn():
                b2 = ring.take()
                PE.wait(a, t_const, *bank_readers[b2])
                for j in range(4):
                    f = lambda e: e.transpose(bank(b2)[:, P * j:P * j + P], w[:, P * j:P * j + P], ident[:, :])
                    if j == 3:
                        pt = PE.do(f)
                    else:
                        PE.quiet(f)
                tmp.free(i2, pt)
                dst = (qT if kind == 0 else kT2)[:, 4 * half:4 * half + 4, P * t:P * t + P]
                e1 = AC.do(lambda e: e.activation(dst, bank(b2).rearrange("p (a b) -> p a b", a=4), ACT.Copy), pt,
                           *last_att[0], *last_a[0])
                bank_readers[b2] = (e1,)
                tqk["qk"[kind]].append(e1)
            return turn

        def lam_value():
            i, y, fr = tmp.take()
            lm = cols(4)
            t = SP.dma(lambda e: e.dma_start(y[:, 0:256], A["lam"].to_broadcast([P, 256])), s_in[7], 16, *fr)
            y4 = y[:, 0:256].rearrange("p (n c d) -> p n c d", n=2, c=2)
            w = y[:, 256:384].rearrange("p (n d) -> p n d", n=2)
            a = DV.do(lambda e: e.tensor_tensor(out=w, in0=y4[:, :, 0], in1=y4[:, :, 1], op=ALU.mult), t)
            a = DV.do(lambda e: e.tensor_reduce(lamc[:, 0:2], w, AX.X, ALU.add), a)
            tmp.free(i, a)
            a = AC.do(lambda e: e.activation(lamc[:, 0:2], lamc[:, 0:2], ACT.Exp), a)
            a = DV.do(lambda e: e.tensor_tensor(out=lamc[:, 2:3], in0=lamc[:, 1:2], in1=lamc[:, 0:1], op=ALU.subtract), a)
            return DV.do(lambda e: e.tensor_scalar(lamc[:, 2:3], lamc[:, 2:3], -LAM_INIT, None, ALU.add), a)

        lamc = sb("lamc", [P, 4])

        def diff_attention(tlam):
            sbk, tbk, obk = Banks([0, 1, 2, 3]), Banks([4, 5]), Banks([7])
            slots = tmp
            tall = (*tqk["q"], *tqk["k"])

            def scores(n, o):
                h, t = n // 2, n % 2
                bs, es, st_ = [], [], cols(4)
                nm, rs = st_[:, 0:2], st_[:, 2:4]
                tt = []
                for m in range(2):
                    g = 8 * m + h
                    hp, ht = 64 * (g % 2), g // 2
                    b = sbk.take()
                    bs.append(b)
                    tt.append(PE.do(lambda e: e.matmul(bank(b), qT[hp:hp + 64, ht, P * t:P * t + P], kT2[hp:hp + 64, ht, :],
                                                       start=True, stop=True), *tall, *bank_readers[b]))
                for m in range(2):
                    a = DV.do(lambda e: e.tensor_reduce(nm[:, m:m + 1], bank(bs[m]), AX.X, ALU.max, negate=True), tt[m])
                    i, y, fr = slots.take()
                    a = AC.do(lambda e: e.activation(y, bank(bs[m]), ACT.Exp, bias=nm[:, m:m + 1],
                                                     accum_out=rs[:, m:m + 1]), a, *fr)
                    bank_readers[bs[m]] = (a,)
                    es.append((i, y, a))
                o.update(es=es, rs=rs)

            def combine(n, o):
                rs, (i0, y0, a0), (i1, y1, a1) = o["rs"], *o["es"]
                a = DV.do(lambda e: e.reciprocal(rs, rs), a0, a1)
                a = DV.do(lambda e: e.tensor_tensor(out=rs[:, 1:2], in0=rs[:, 1:2], in1=lamc[:, 2:3], op=ALU.mult), a, tlam)
                b = DV.do(lambda e: e.tensor_scalar(y0, y0, rs[:, 0:1], None, ALU.mult), a)
                b = DV.do(lambda e: e.scalar_tensor_tensor(out=y0, in0=y1, scalar=rs[:, 1:2], in1=y0, op0=ALU.mult,
                                                           op1=ALU.add), b)
                slots.free(i1, b)
                o["t"] = b

            def turn(n, o):
                i0, y0, _ = o["es"][0]
                b = tbk.take()
                PE.wait(o["t"], t_const, *bank_readers[b])
                for j in range(4):
                    f = lambda e, j=j: e.transpose(bank(b)[:, P * j:P * j + P], y0[:, P * j:P * j + P], ident[:, :])
                    t = PE.do(f) if j == 3 else PE.quiet(f)
                o["ta"] = AC.do(lambda e: e.activation(y0, bank(b), ACT.Copy), t)
                bank_readers[b] = (o["ta"],)

            def values(n, o):
                h, t = n // 2, n % 2
                i0, y0, _ = o["es"][0]
                b = obk.take()
                PE.wait(o["ta"], *tqk["v"], *bank_readers[b])
                for j in range(4):
                    f = lambda e, j=j: e.matmul(bank(b)[:, 0:P], y0[:, P * j:P * j + P], v2[:, j, P * h:P * h + P],
                                                start=(j == 0), stop=(j == 3))
                    tp = PE.do(f) if j == 3 else PE.quiet(f)
                slots.free(i0, tp)
                e1 = DV.do(lambda e: e.tensor_copy(xn[:, t, P * h:P * h + P], bank(b)[:, 0:P]), tp, *xn_free[t])
                bank_readers[b] = (e1,)
                last_att[0] = (tp,)
                o_done[t] = e1

            for _ in pipeline([scores, combine, turn, values], 16):
                mods(MOD_RATE[2][0], (2, 5))
            i, gs, fr = tmp.take()
            tg = SP.dma(lambda e: e.dma_start(gs[:, 0:128], A["subln"].to_broadcast([P, P])), s_in[0], 32, *fr)
            tg = DV.do(lambda e: e.tensor_scalar(gs[:, 0:128], gs[:, 0:128], 1.0 - LAM_INIT, None, ALU.mult), tg)
            tn = []
            for t in range(2):
                ss = cols(8)
                for half in range(2):
                    i2, w, fr2 = tmp.take()
                    a = AC.do(lambda e: e.activation(w, xn[:, t, 512 * half:512 * half + 512], ACT.Square), o_done[t], *fr2)
                    a = DV.do(lambda e: e.tensor_reduce(ss[:, 4 * half:4 * half + 4], w.rearrange("p (h d) -> p h d", h=4),
                                                        AX.X, ALU.add), a)
                    tmp.free(i2, a)
                r = rstd(ss, 128, 8, a)
                xv = xn[:, t, :].rearrange("p (h d) -> p h d", h=8)
                a = DV.do(lambda e: e.tensor_tensor(out=xv, in0=xv, in1=ss.unsqueeze(2).to_broadcast([P, 8, P]), op=ALU.mult),
                          r, o_done[t])
                tn.append(DV.do(lambda e: e.tensor_tensor(out=xv, in0=xv, in1=gs[:, 0:128].unsqueeze(1).to_broadcast([P, 8, P]),
                                                          op=ALU.mult), a, tg))
            tmp.free(i, tn[-1])
            to = []
            for k2_ in range(4):
                b = ring.take()
                PE.wait(*tn, *bank_readers[b])
                for j in range(2):
                    for t in range(2):
                        f = lambda e, j=j, t=t: e.transpose(bank(b)[:, 256 * j + P * t:256 * j + P * t + P],
                                                            xn[:, t, (2 * k2_ + j) * P:(2 * k2_ + j + 1) * P], ident[:, :])
                        pt = PE.do(f) if j == t == 1 else PE.quiet(f)
                last = split_T(bank(b).rearrange("p (a b) -> p a b", a=2), pt, oH[:, 2 * k2_:2 * k2_ + 2, :],
                               oL[:, 2 * k2_:2 * k2_ + 2, :], last_o[0])
                to += [last, last]
                bank_readers[b] = last
            xn_free[0] = xn_free[1] = (pt,)
            return to

        o_done = [None, None]

        def short_conv(th):
            buf = att[:, 0:2 * 2 * 258].rearrange("p (b i t) -> p b i t", b=2, i=2)
            tz = DV.do(lambda e: e.memset(att[:, 0:1032], 0.0), *last_att[0], *last_a[0])
            prev = [(), ()]
            to = []
            for j in range(4):
                bc, tc = featmajor("qkv3", th, hH, hL)
                i, cc, fr = tmp.take()
                split_half()
                a = AC.do(lambda e: e.activation(cc, bank(bc), ACT.Copy), tc, *fr)
                bank_readers[bc] = (a,)
                split_half()
                mods(MOD_RATE[3][0], (3, 5))
                bu, tu = featmajor("qkv3", th, hH, hL)
                pb = buf[:, j % 2]
                split_half()
                a = DV.do(lambda e: e.tensor_tensor(out=pb[:, :, 1:257], in0=bank(bu).rearrange("p (a b) -> p a b", a=2),
                                                    in1=cc.rearrange("p (a b) -> p a b", a=2), op=ALU.mult),
                          tu, a, tz, *prev[j % 2])
                tmp.free(i, a)
                bank_readers[bu] = (a,)
                split_half()
                i, y, fr = tmp.take()
                yv = y.rearrange("p (a b) -> p a b", a=2)
                w = [[sm[:, SM[f"sc{k}"][0] + 2 * j + n:SM[f"sc{k}"][0] + 2 * j + n + 1] for k in range(3)] for n in range(2)]
                for n in range(2):
                    c = DV.do(lambda e: e.tensor_scalar(yv[:, n], pb[:, n, 1:257], w[n][1], None, ALU.mult), a, *fr)
                for k, lo_ in ((0, 0), (2, 2)):
                    c0 = c
                    for n in range(2):
                        c = DV.do(lambda e: e.scalar_tensor_tensor(out=yv[:, n], in0=pb[:, n, lo_:lo_ + 256],
                                                                   scalar=w[n][k], in1=yv[:, n], op0=ALU.mult,
                                                                   op1=ALU.add), c0)
                prev[j % 2] = (c,)
                mods(MOD_RATE[3][0], (3, 5))
                bb, tb = featmajor("qkv3", th, hH, hL)
                split_half()
                c = DV.do(lambda e: e.tensor_tensor(out=y, in0=bank(bb), in1=y, op=ALU.mult), tb, c)
                bank_readers[bb] = (c,)
                last = split_T(yv, c, oH[:, 2 * j:2 * j + 2, :], oL[:, 2 * j:2 * j + 2, :], (*last_o[0], *last_a[0]))
                tmp.free(i, *last)
                to += [last, last]
                split_half()
                mods(MOD_RATE[3][0], (3, 5))
            last_att[0] = (c,)
            last = to
            return last, tb

        def ffn(l, th):
            free_a = (*last_a[0], *last_att[0], *last_o[0])
            rate = MOD_RATE[l][1]
            upto = (l + 1, 2)
            ta = []
            for j in range(11):
                bg, tg = featmajor("gate%d" % l, th, hH, hL)
                split_half()
                g = bank(bg).rearrange("p (a b) -> p a b", a=2)
                i, y, fr = tmp.take()
                yv = y.rearrange("p (a b) -> p a b", a=2)
                if l < 2:
                    col = lambda name, n: sm[:, SM[name][0] + 2 * j + n:SM[name][0] + 2 * j + n + 1]
                    for n in range(2):
                        a = AC.do(lambda e: e.activation(yv[:, n], g[:, n], ACT.Identity, bias=col(f"bc{l}", n),
                                                         scale=col(f"wc{l}2", n)), tg, *fr)
                    for n in range(2):
                        c = DV.do(lambda e: e.scalar_tensor_tensor(out=yv[:, n, 1:256], in0=g[:, n, 0:255],
                                                                   scalar=col(f"wc{l}1", n), in1=yv[:, n, 1:256],
                                                                   op0=ALU.mult, op1=ALU.add), a)
                    for n in range(2):
                        a = DV.do(lambda e: e.scalar_tensor_tensor(out=yv[:, n, 2:256], in0=g[:, n, 0:254],
                                                                   scalar=col(f"wc{l}0", n), in1=yv[:, n, 2:256],
                                                                   op0=ALU.mult, op1=ALU.add), c)
                    bank_readers[bg] = (a,)
                    split_half()
                    a = AC.do(lambda e: e.activation(y, y, ACT.Silu), a)
                else:
                    a = AC.do(lambda e: e.activation(y, bank(bg), ACT.Silu), tg, *fr)
                    bank_readers[bg] = (a,)
                    split_half()
                mods(rate, upto)
                bu, tu = featmajor("up%d" % l, th, hH, hL)
                split_half()
                a = DV.do(lambda e: e.tensor_tensor(out=y, in0=bank(bu), in1=y, op=ALU.mult), tu, a)
                bank_readers[bu] = (a,)
                last = split_T(yv, a, aH[:, 2 * j:2 * j + 2, :], aL[:, 2 * j:2 * j + 2, :], free_a)
                tmp.free(i, *last)
                ta += [last, last]
                split_half()
                mods(rate, upto)
            for i in range(11):
                t = tokmajor("down%d" % l, ta, aH, aL, FT, i)
                if i < 10:
                    split_half()
                    split_half()
                    mods(rate, upto)
            last_a[0] = (t[1],)
            return tu, t

        tn = norm_rows(x, tx)
        mods_through(0, 1)
        for _ in range(NSPL):
            split_half()
        for l in range(LAYERS):
            tmod = (modt[(l, 0, 0)], modt[(l, 1, 0)])
            th = norm_T(tn, 0, hH, hL, tmod, hT_free[0])
            if l:
                split_half()
                split_half()
            if l < 2:
                if l == 1:
                    tcum = forget_logits(th)
                tv = value_product(l, th)
                AC.quiet(lambda e: e.preload_act_table_set("natural_log_exp_and_others"))
                o_tok[0] = []
                qk_products(l, th, lambda tq, tk: stick_breaking(tq, tk, tv) if l == 0 else forgetting(tq, tk, tv, tcum))
                to = o_tok[0]
            elif l == 2:
                t, tlam = differential(th, (modt[(2, 0, 1)], modt[(2, 1, 1)]))
                hT_free[0] = (t,)
                to = diff_attention(tlam)
            else:
                to, t = short_conv(th)
                hT_free[0] = (t,)
            t = out_product("wo%d" % l, to, 4, oH, oL, MOD_RATE[l][0], (l, 5))
            last_o[0] = (t[1],)
            mods_through(l, 4)
            tx = post(l, 0, t, (modt[(l, 2, 0)],))
            tn = norm_rows(x, tx)
            tmod = (modt[(l, 3, 0)], modt[(l, 4, 0)])
            th = norm_T(tn, 2, hH, hL, tmod, hT_free[0])
            split_half()
            split_half()
            mods_through(l, 5)
            t_h, t = ffn(l, th)
            hT_free[0] = (t_h,)
            if l + 1 < LAYERS:
                mods_through(l + 1, 1)
            tx = post(l, 1, t, (modt[(l, 5, 0)],))
            if l + 1 < LAYERS:
                tn = norm_rows(x, tx)

        SP.dma(lambda e: e.dma_start(out.rearrange("o (t p) d -> p (o t) d", p=P), x[:, :, :]), s_out, 16, *tx)
        SP.wait((s_out, 16))


def kernel(**inputs):
    import concourse.bacc as _bacc
    from concourse import mybir as _mybir
    from concourse.bass_utils import run_bass_kernel_spmd as _run

    I = {k: np.asarray(v) for k, v in inputs.items() if k.startswith(("win_", "cf_")) is False}

    def feat(w):
        return np.ascontiguousarray(w.reshape(8, P, -1, 2, P).transpose(2, 1, 3, 0, 4)).reshape(-1, P, 2048)

    def tok(w):
        return np.ascontiguousarray(w.reshape(-1, 2, P, 1024).transpose(0, 2, 1, 3)).reshape(-1, P, 2048)

    def tok512(w):
        return np.ascontiguousarray(w.reshape(2, 4, P, -1, 512).transpose(3, 0, 2, 1, 4)).reshape(-1, P, 2048)

    def cols(v):
        return np.ascontiguousarray(v.reshape(-1, P).T)

    arrays = {}
    for l in range(4):
        b, i = l // 2, l % 2
        mod, bm = (I["w_mod"][i], I["b_mod"][i]) if b == 0 else (I["ada_w_2"][i], I["ada_b_2"][i])
        arrays[f"mod{l}"] = np.concatenate([tok(mod[:, 1024 * p:1024 * p + 1024]) for p in range(6)])
        if b == 0:
            q = I["w_qkv"][i]
            arrays[f"qkv{l}"] = np.concatenate([feat(q[:, :2048]), tok(q[:, 2048:])])
            arrays[f"wo{l}"] = tok(I["w_o"][i])
            arrays[f"gate{l}"] = feat(I["w_ffn_gate"][i])
            arrays[f"up{l}"] = feat(I["w_ffn_up"][i])
            arrays[f"down{l}"] = tok(I["w_ffn_down"][i])
        else:
            arrays[f"qkv{l}"] = tok512(I["diff_w_qkv_2"][0]) if i == 0 else feat(I["sc_w_in_2"][0])
            arrays[f"wo{l}"] = tok(I["diff_w_o_2"][0] if i == 0 else I["sc_w_out_2"][0])
            arrays[f"gate{l}"] = feat(I["ffn_w_gate_up_2"][i][:, :FF])
            arrays[f"up{l}"] = feat(I["ffn_w_gate_up_2"][i][:, FF:])
            arrays[f"down{l}"] = tok(I["ffn_w_down_2"][i])
    parts = {"c": I["c"][0], "c2": I["c_2"][0], "cc": I["c_ctx_2"]}
    for l in range(4):
        b, i = l // 2, l % 2
        bm = I["b_mod"][i] if b == 0 else I["ada_b_2"][i]
        parts[f"g{l}a"] = I["g_mix_pre"][i] if b == 0 else I["norm1_2"][i]
        parts[f"g{l}f"] = I["g_ffn_pre"][i] if b == 0 else I["norm2_2"][i]
        for p in (0, 1, 3, 4):
            parts[f"b{l}{p}"] = bm[1024 * p:1024 * p + 1024]
        if b == 0:
            for k in range(3):
                parts[f"wc{l}{k}"] = I["w_conv"][i, k]
            parts[f"bc{l}"] = I["b_conv"][i]
    for k in range(3):
        parts[f"sc{k}"] = I["sc_conv_w_2"][0, k]
    bf = np.zeros(P, np.float32)
    bf[:H] = I["b_fg"][0]
    parts["bf"] = bf
    arrays["smalls"] = np.ascontiguousarray(np.concatenate([cols(parts[n]) for n in SM], axis=1))
    gb = []
    for l in range(4):
        b, i = l // 2, l % 2
        bm = I["b_mod"][i] if b == 0 else I["ada_b_2"][i]
        for p, g in ((2, "g_mix_post"), (5, "g_ffn_post")):
            row = bm[1024 * p:1024 * p + 1024]
            gb.append(np.concatenate([row, I[g][i] if b == 0 else row]))
    arrays["gb"] = np.stack(gb)
    arrays["x"] = I["x"]
    arrays["ctx"] = I["ctx_2"]
    wfg = np.zeros((1, P, 8, P), np.float32)
    wfg[0, :, :, :H] = I["w_fg"][0].reshape(8, P, H).transpose(1, 0, 2)
    arrays["wfg"] = wfg.reshape(1, P, 1024)
    t = np.arange(S)
    inv = (np.float32(10000.0) ** (-np.arange(16, dtype=np.float32) / np.float32(16))).astype(np.float32)
    ar = (t // 64).astype(np.float32)[:, None] * inv
    ac = (t % 64).astype(np.float32)[:, None] * inv
    cs = np.concatenate([np.cos(ar), np.cos(ar), np.cos(ac), np.cos(ac)], axis=1)
    sn = np.concatenate([-np.sin(ar), np.sin(ar), -np.sin(ac), np.sin(ac)], axis=1)
    tab = np.stack([cs, sn]).astype(np.float32).reshape(2, 2, P, 64).transpose(2, 0, 1, 3).reshape(P, 256)
    arrays["rope"] = np.ascontiguousarray(np.concatenate([tab, tab], axis=1))
    swap = np.concatenate([np.arange(16, 32), np.arange(0, 16), np.arange(48, 64), np.arange(32, 48)])
    qn, kn = I["diff_q_norm_2"][0], I["diff_k_norm_2"][0]
    arrays["qkg"] = np.concatenate([qn, qn[swap], kn, kn[swap]])[None, :]
    arrays["lam"] = np.concatenate([I["diff_lam_q1_2"][0], I["diff_lam_k1_2"][0], I["diff_lam_q2_2"][0],
                                    I["diff_lam_k2_2"][0]])[None, :]
    arrays["subln"] = np.ascontiguousarray(I["diff_subln_2"])

    nc = _bacc.Bacc("TRN2", target_bir_lowering=False, num_devices=1)
    A, feed = {}, {}
    for name, a in arrays.items():
        feed["in_" + name] = a
        A[name] = nc.dram_tensor("in_" + name, a.shape, _mybir.dt.from_np(a.dtype), kind="ExternalInput").ap()
    o = nc.dram_tensor("out_0_dram", (1, S, D), _mybir.dt.float32, kind="ExternalOutput").ap()
    build(nc, A, o)
    r = _run(nc, [feed], core_ids=[0])
    return r.results[0]["out_0_dram"]
```

```python
import numpy as np
from contextlib import ExitStack
import concourse.bass as bass
from concourse import mybir

D, S, FF, H, P = 1024, 256, 2816, 16, 128
KT, FT = D // P, FF // P
EPS = 1e-6
NRAW, NSPL = 4, 6
LAYERS = 4
LAM_INIT = 0.8 - 0.6 * float(np.exp(-0.3 * 0))
NEG = -1e30

SM = {}


def _layout():
    at = 0
    for name, n in [("c", 8), ("c2", 8), ("cc", 8)] + [(f"g{l}{k}", 8) for l in range(4) for k in "af"] + \
            [(f"b{l}{p}", 8) for l in range(4) for p in (0, 1, 3, 4)] + \
            [(f"wc{l}{k}", FT) for l in range(2) for k in range(3)] + [(f"bc{l}", FT) for l in range(2)] + \
            [(f"sc{k}", 8) for k in range(3)] + [("bf", 1)]:
        SM[name] = (at, n)
        at += n
    return at


NSM = _layout()


class Queue:

    def __init__(self, eng, sem):
        self.eng, self.sem, self.n, self.seen = eng, sem, 0, {}

    def wait(self, *tokens):
        for sem, value in tokens:
            if self.seen.get(sem.name, 0) < value:
                self.eng.wait_ge(sem, value)
                self.seen[sem.name] = value

    def do(self, f, *tokens):
        self.wait(*tokens)
        self.n += 1
        f(self.eng).then_inc(self.sem, 1)
        return self.sem, self.n

    def quiet(self, f, *tokens):
        self.wait(*tokens)
        f(self.eng)

    def dma(self, f, sem, value, *tokens):
        self.wait(*tokens)
        f(self.eng).then_inc(sem, 16)
        return sem, value


class Slots:

    def __init__(self, items):
        self.items, self.at, self.readers = items, 0, [()] * len(items)

    def take(self):
        i = self.at % len(self.items)
        self.at += 1
        readers, self.readers[i] = self.readers[i], None
        assert readers is not None, "a buffer is taken before it is free"
        return i, self.items[i], readers

    def free(self, i, *tokens):
        self.readers[i] = tokens


def build(nc, A, out):
    f32, f32r = mybir.dt.float32, mybir.dt.float32r
    ALU, ACT, AX = mybir.AluOpType, mybir.ActivationFunctionType, mybir.AxisListType
    stack = ExitStack()
    with stack:
        def sb(name, shape, dt=f32):
            return stack.enter_context(nc.sbuf_tensor(name, shape, dt))

        with nc.sbuf_tensor("att", [P, 10240], f32) as att, nc.sbuf_tensor("oHL", [P, 2, KT, S], f32r) as oHL:
            pass
        aHL = sb("aHL", [P, 2, FT, S], f32r)
        sb("fill", [P, 14336 - 2 * FT * S], f32)
        raw = sb("raw", [P, NRAW, 2048])
        whi = sb("whi", [P, NSPL, 1024], f32r)
        wlo = sb("wlo", [P, NSPL, 1024], f32r)
        x = sb("x", [P, 2, D])
        hHL = sb("hHL", [P, 2, KT, S], f32r)
        gtb = sb("gtb", [P, 2, D])
        acc = sb("acc", [P, 2, D])
        xn = sb("xn", [P, 2, D])
        tmpt = sb("tmp", [P, 7, 512])
        sm = sb("sm", [P, NSM])
        modc = sb("modc", [P, 6, 8])
        ccol = sb("ccol", [P, 3, 8])
        ident = sb("ident", [P, P])
        ones = sb("ones", [P, P])
        tri_ge = sb("tri_ge", [P, P])
        tri_le = sb("tri_le", [P, P])
        msk = sb("msk", [P, P])
        st = sb("st", [P, 64])
        rope = sb("rope", [P, 4, 2, 64])
        kgt = sb("kgt", [P, 64])
        lamc = sb("lamc", [P, 4])
        subln = sb("subln", [P, P])
        phalf = sb("phalf", [P, 1])
        epsc = sb("epsc", [P, 1])
        ncum = sb("ncum", [H, S])
        mat = stack.enter_context(nc.psum_tensor("mat", [P, 8, 512], f32))

        sem = lambda n: stack.enter_context(nc.semaphore(n))
        PE, AC, DV, PO, SP = (Queue(e, sem(n)) for e, n in (
            (nc.tensor, "s_pe"), (nc.scalar, "s_act"), (nc.vector, "s_dve"), (nc.gpsimd, "s_pool"), (nc.sync, "s_sp")))
        s_raw = [sem(f"s_raw{i}") for i in range(NRAW)]
        s_in = [sem(f"s_in{i}") for i in range(8)]
        s_out = sem("s_out")

        aH, aL = aHL[:, 0], aHL[:, 1]
        hH, hL = hHL[:, 0], hHL[:, 1]
        oH, oL = oHL[:, 0], oHL[:, 1]
        bank_readers = [() for _ in range(8)]
        tmp = Slots([tmpt[:, i, :] for i in range(7)])
        last_att = [()]
        last_o = [()]
        last_a = [()]

        def bank(b):
            return mat[:, b, :]

        class Banks:
            def __init__(self, ids):
                self.ids, self.at = ids, 0

            def take(self):
                b = self.ids[self.at % len(self.ids)]
                self.at += 1
                return b

        ring = Banks([4, 5, 7])

        def load(dst, src, i):
            return SP.dma(lambda e: e.dma_start(dst, src), s_in[i], 16)

        t_sm = load(sm[:, :], A["smalls"], 0)

        m0 = DV.do(lambda e: e.memset(ident[:, :], 0.0))
        m1 = DV.do(lambda e: e.memset(ones[:, :], 1.0))
        m2 = DV.do(lambda e: e.memset(phalf[:, :], -0.5))
        k0 = PO.do(lambda e: e.affine_select(out=ident[:, :], in_=ident[:, :], compare_op=ALU.not_equal, fill=1.0,
                                             base=0, pattern=[[-1, P]], channel_multiplier=1), m0, m1, m2)
        k1 = PO.do(lambda e: e.affine_select(out=tri_ge[:, :], in_=ones[:, :], compare_op=ALU.is_ge, fill=0.0,
                                             base=0, pattern=[[-1, P]], channel_multiplier=1))
        k2 = PO.do(lambda e: e.affine_select(out=tri_le[:, :], in_=ones[:, :], compare_op=ALU.is_ge, fill=0.0,
                                             base=0, pattern=[[1, P]], channel_multiplier=-1))
        t_const = k2
        t_eps = DV.do(lambda e: e.memset(epsc[:, :], EPS))
        one_row = ones[0:H, 0:1].to_broadcast([H, S])

        def strict_mask(l_tokens):
            return PO.do(lambda e: e.affine_select(out=msk[:, :], in_=ones[:, :], compare_op=ALU.is_gt, fill=0.0,
                                                   base=0, pattern=[[1, P]], channel_multiplier=-1), *l_tokens)

        t_c = AC.do(lambda e: e.activation(ccol[:, :, :], sm[:, 0:24].rearrange("p (a b) -> p a b", a=3), ACT.Silu), t_sm)

        nraw = [0]
        raw_free = [()] * NRAW

        def fetch(src):
            i = nraw[0] % NRAW
            v = 16 * (nraw[0] // NRAW + 1)
            nraw[0] += 1
            while raw_free[i] is None:
                pending.pop(0)[1]()
            free, raw_free[i] = raw_free[i], None
            dst = raw[:, i, 0:src.shape[-1]]
            return i, SP.dma(lambda e: e.dma_start(dst, src), s_raw[i], v, *free)

        wseq = []
        for l in range(LAYERS):
            if l < 2:
                wseq += [("qkv%d" % l, 8 + i) for i in range(4)]
                wseq += [("wfg", 0)] if l == 1 else []
                for j in range(4):
                    wseq += [("qkv%d" % l, j), ("qkv%d" % l, 4 + j)]
            elif l == 2:
                wseq += [("qkv2", i) for i in (0, 1, 4, 5, 8, 9, 2, 3, 6, 7, 10, 11)]
            else:
                for j in range(4):
                    wseq += [("qkv3", 4 + j), ("qkv3", 8 + j), ("qkv3", j)]
            wseq += [("wo%d" % l, i) for i in range(4)]
            for j in range(11):
                wseq += [("gate%d" % l, j), ("up%d" % l, j)]
            wseq += [("down%d" % l, i) for i in range(11)]
        split_free = [()] * NSPL
        ready = []
        nsplit = [0]

        hseq = [(name, c, h) for name, c in wseq for h in range(2)]
        part = [None]

        def split_half():
            if nsplit[0] == len(hseq):
                return
            s = nsplit[0] % NSPL
            name, c, half = hseq[nsplit[0]]
            if half == 0:
                part[0] = fetch(A[name][c])
            i, t = part[0]
            nsplit[0] += 1
            if name == "wfg" and half:
                ready.append((s, *ready[-1][1:]))
                return
            src = raw[:, i, 1024 * half:1024 * half + 1024]
            free, split_free[s] = split_free[s], None
            assert free is not None, "a slot is split into before TensorE has done with it"
            hi = AC.do(lambda e: e.activation(whi[:, s, :], src, ACT.Copy), t, *free)
            lo = DV.do(lambda e: e.tensor_tensor(out=wlo[:, s, :], in0=src, in1=whi[:, s, :].bitcast(f32),
                                                 op=ALU.subtract), t, hi, *free)
            if half or name == "wfg":
                raw_free[i] = (lo,)
            ready.append((s, hi, lo, name))
            mods()

        nused = [0]

        def half_chunk(name):
            s, hi, lo, got = ready[nused[0]]
            assert got == name, (got, name)
            nused[0] += 1
            PE.wait(hi, lo)
            return s, whi[:, s, :], wlo[:, s, :]

        def used(s, token):
            split_free[s] = (token,)

        modq = [(l, p, i) for l in range(LAYERS) for p in range(6) for i in range(4)]
        nmod = [0]
        acc_free = [(), ()]
        pending = []
        modt = {}
        gfree = [(), ()]
        cfree = []

        def mod_step():
            if nmod[0] == 2 * len(modq):
                return
            (l, p, q), j = modq[nmod[0] // 2], nmod[0] % 2
            nmod[0] += 1
            if j == 0:
                mod_chunk[0] = fetch(A["mod%d" % l][4 * p + q])
            i, t = mod_chunk[0]
            accs = [(0, 0 if l < 2 else 1), (1, 2)] if l == 2 and p < 2 else [(p % 2, 0 if l < 2 else 1)]
            last = None
            kt = 2 * q + j
            for a, c in accs:
                while kt == 0 and acc_free[a] is None:
                    pending.pop(0)[1]()
                src = raw[:, i, 1024 * j:1024 * j + 1024]
                cs = ccol[:, c, kt:kt + 1]
                if kt == 0:
                    last = DV.do(lambda e: e.tensor_scalar(acc[:, a, :], src, cs, None, ALU.mult), t, t_c, *acc_free[a])
                else:
                    last = DV.do(lambda e: e.scalar_tensor_tensor(out=acc[:, a, :], in0=src, scalar=cs, in1=acc[:, a, :],
                                                                  op0=ALU.mult, op1=ALU.add), t, acct[a])
                acct[a] = last
            if j == 0:
                return
            raw_free[i] = (last,)
            if q == 3:
                for a, c in accs:
                    acc_free[a] = None
                if p in (2, 5):
                    gate_rows(l, p, accs[0][0])
                else:
                    for a, c in accs:
                        columns(l, p, a, int(c == 2))

        acct, mod_chunk = [None, None], [None]

        def later(l, p, f):
            pending.append(((l, p), f))

        def idle():
            pass

        def columns(l, p, a, ctx):
            b, t_acc, o = 6, acct[a], SM[f"b{l}{p}"][0]
            row = (4 if ctx else 0 if p < 3 else 2) + (p in (1, 4))

            def products():
                PE.wait(t_acc, m1, *bank_readers[b])
                for k in range(8):
                    f = lambda e, k=k: e.matmul(bank(b)[:, k:k + 1], acc[:, a, k * P:k * P + P], ones[:, 0:1],
                                                start=True, stop=True)
                    t = PE.do(f) if k == 7 else PE.quiet(f)
                acc_free[a] = (t,)

            def finish():
                t1 = DV.do(lambda e: e.tensor_tensor(out=modc[:, row, :], in0=bank(b)[:, 0:8], in1=sm[:, o:o + 8],
                                                     op=ALU.add), *acc_free[a], t_sm, *cfree)
                del cfree[:]
                bank_readers[b] = (t1,)
                if p in (1, 4):
                    o2, _ = SM[f"g{l}" + ("a" if p == 1 else "f")]
                    t1 = DV.do(lambda e: e.scalar_tensor_tensor(out=modc[:, row, :], in0=modc[:, row, :], scalar=1.0,
                                                                in1=sm[:, o2:o2 + 8], op0=ALU.add, op1=ALU.mult), t1)
                modt[(l, p, ctx)] = t1

            for f in (idle, idle, products, idle, finish):
                later(l, p, f)

        s_gate, ngate, seen = [sem(f"s_gate{i}") for i in range(4)], [0] * 4, [()] * 4

        def gate_rows(l, p, a):
            g, b, t_acc, o = int(p == 5), 6, acct[a], {}
            row = A["gb"][2 * l + g:2 * l + g + 1, :]

            def rows(dst, src, which, *tokens):
                ngate[which] += 16
                return SP.dma(lambda e: e.dma_start(dst, src.to_broadcast(list(dst.shape))), s_gate[which], ngate[which],
                              *tokens, *seen[which])

            o["bias"] = rows(gtb[:, g, :], row[:, 0:D], g, *gfree[g])

            def product(c):
                o["t"] = PE.do(lambda e: e.matmul(bank(b), ones[:, :], acc[:, a, c], start=True, stop=True),
                               t_acc, m1, *bank_readers[b])
                if c.start:
                    acc_free[a] = (o["t"],)
                if l < 2:
                    o["i"], o["gain"], fr = tmp.take()
                    o["tg"] = rows(o["gain"], row[:, D + c.start:D + c.stop], 3 if c.start else 2, *fr)

            def finish(c):
                if l < 2:
                    t1 = DV.do(lambda e: e.tensor_tensor(out=gtb[:, g, c], in0=bank(b), in1=gtb[:, g, c], op=ALU.add),
                               o["t"], o["bias"])
                    bank_readers[b] = (t1,)
                    t1 = DV.do(lambda e: e.tensor_tensor(out=gtb[:, g, c], in0=gtb[:, g, c], in1=o["gain"],
                                                         op=ALU.mult), t1, o["tg"])
                    tmp.free(o["i"], t1)
                    seen[3 if c.start else 2] = seen[g] = (t1,)
                else:
                    t1 = DV.do(lambda e: e.tensor_tensor(out=gtb[:, g, c], in0=bank(b), in1=gtb[:, g, c], op=ALU.add),
                               o["t"], o["bias"])
                    seen[g] = bank_readers[b] = (t1,)
                if c.start:
                    modt[(l, p, 0)] = t1

            c0, c1 = slice(0, 512), slice(512, 1024)
            for f in (idle, idle, idle, lambda: product(c0), idle, lambda: finish(c0), idle, idle,
                      lambda: product(c1), idle, lambda: finish(c1)):
                later(l, p, f)

        mod_rate, mod_debt = [0.0, (0, 1)], [0.0]

        def at_rate(rate, upto):
            mod_rate[:] = rate, upto

        def more_to_do(upto):
            return nmod[0] < 2 * len(modq) and modq[nmod[0] // 2][:2] <= upto

        def mods():
            if pending:
                pending.pop(0)[1]()
            mod_debt[0] += mod_rate[0]
            while mod_debt[0] >= 1.0:
                mod_debt[0] -= 1.0
                if more_to_do(mod_rate[1]):
                    mod_step()

        def mods_through(l, p):
            while more_to_do((l, p)):
                mod_step()
            while pending and pending[0][0] <= (l, p):
                pending.pop(0)[1]()

        stn = [0]

        def cols(n):
            if stn[0] + n > 64:
                stn[0] = 0
            stn[0] += n
            return st[:, stn[0] - n:stn[0]]

        def rstd(ss, n, width, t):
            a = PO.do(lambda e: e.tensor_scalar(ss, ss, 1.0 / n, EPS, ALU.mult, ALU.add), t)
            return PO.do(lambda e: e.tensor_tensor(out=ss, in0=ss, in1=phalf[:, 0:width], op=ALU.pow), a, m2)

        xn_free = [(), ()]

        def rstd_log(ss, n, t):
            a = AC.do(lambda e: e.activation(ss, ss, ACT.Ln, scale=1.0 / n, bias=epsc[:, 0:1]), t, t_eps)
            return AC.do(lambda e: e.activation(ss, ss, ACT.Exp, scale=-0.5), a)

        def norm_rows(src, t, tsrc):
            return [scale_rows(src, t, *row_rstd(src, t, tsrc))] * 2

        def row_rstd(src, t, tsrc):
            ss = cols(1)
            a = AC.do(lambda e: e.activation(xn[:, t, :], src[:, t, :], ACT.Square, accum_out=ss), tsrc, *xn_free[t])
            return ss, rstd(ss, D, 1, a)

        def scale_rows(src, t, ss, r):
            return DV.do(lambda e: e.tensor_scalar(xn[:, t, :], src[:, t, :], ss, None, ALU.mult), r)

        def norm_T(tx, t, row, dstH, dstL, tmod, wr, groups=(0, 1), engines=(0, 1), tails=None):
            last = []
            for g in groups:
                b = ring.take()
                PE.wait(tx[g], t_const, *bank_readers[b])
                for j in range(4):
                    f = lambda e: e.transpose(bank(b)[:, P * j:P * j + P], xn[:, t, (4 * g + j) * P:(4 * g + j + 1) * P],
                                              ident[:, :])
                    pt = PE.do(f) if j == 3 else PE.quiet(f)
                i, tm, fr = tmp.take()
                for j in range(4):
                    kt = 4 * g + j
                    o, src = tm[:, P * j:P * j + P], bank(b)[:, P * j:P * j + P]
                    gain, shift = modc[:, row + 1, kt:kt + 1], modc[:, row, kt:kt + 1]
                    if engines[g] == 0:
                        e1 = DV.do(lambda e: e.tensor_scalar(o, src, gain, shift, ALU.mult, ALU.add), pt, *fr, *tmod)
                    else:
                        e1 = AC.do(lambda e: e.activation(o, src, ACT.Identity, bias=shift, scale=gain), pt, *fr, *tmod)
                bank_readers[b] = (e1,)
                cfree.append(e1)
                head, tail = (d[:, 4 * g:4 * g + 4, P * t:P * t + P] for d in (dstH, dstL))
                tv = tm.rearrange("p (a b) -> p a b", a=4)
                if tails is None:
                    last += [split_T(tv, e1, head, tail, wr)] * 4
                    tmp.free(i, *last[-1])
                else:
                    a = AC.do(lambda e: e.activation(head, tv, ACT.Copy), e1, *wr)

                    def rest(i=i, tv=tv, a=a, head=head, tail=tail):
                        c = DV.do(lambda e: e.tensor_tensor(out=tail, in0=tv, in1=head.bitcast(f32), op=ALU.subtract),
                                  a, *wr)
                        tmp.free(i, a, c)
                        return [(a, c)] * 4
                    tails.append(rest)
            xn_free[t] = (pt,)
            return last

        def split_T(src, t, dh, dl, wr):
            a = AC.do(lambda e: e.activation(dh, src, ACT.Copy), t, *wr)
            b = DV.do(lambda e: e.tensor_tensor(out=dl, in0=src, in1=dh.bitcast(f32), op=ALU.subtract), a, *wr)
            return a, b

        def featmajor(name, th, sH, sL, tiles=2, between=None):
            b = bring.take()
            for i in range(tiles):
                s, wh, wl = half_chunk(name)
                wh = wh.rearrange("p (k n) -> p k n", k=8)
                wl = wl.rearrange("p (k n) -> p k n", k=8)
                if i == 0:
                    PE.wait(*bank_readers[b])
                o = bank(b)[:, 256 * i:256 * i + 256]
                for k in range(KT):
                    PE.wait(*th[0][k], *th[1][k])
                    for n, (w, h) in enumerate(((wh, sH), (wh, sL), (wl, sH))):
                        f = lambda e: e.matmul(o, w[:, k, :], h[:, k, :], start=(k == 0 and n == 0),
                                               stop=(k == KT - 1 and n == 2))
                        if k == KT - 1 and n == 2:
                            t = PE.do(f)
                        else:
                            PE.quiet(f)
                used(s, t)
                if i == 0 and between:
                    between()
            return b, t

        bring = Banks([4, 7])

        def tokmajor(name, th, sH, sL, nk, groups, mid=None):
            k0, toks = 0, [None, None]
            for g, n in enumerate(groups):
                last = k0 + 2 * n == nk
                halves = {}
                order = [(j, t) for j in range(2) for t in range(2)] if n == 1 and not last else \
                    [(j, t) for t in range(2) for j in range(2 * n)]
                for j, t in order:
                    if j not in halves:
                        halves[j] = half_chunk(name)
                    s, wh, wl = halves[j]
                    k = k0 + j
                    PE.wait(*th[t][k])
                    if k == 0:
                        PE.wait(*bank_readers[2 * t], *bank_readers[2 * t + 1])
                    for m, (h, w, half) in enumerate([(sH, wh, 0), (sH, wh, 1), (sH, wl, 0), (sH, wl, 1),
                                                      (sL, wh, 0), (sL, wh, 1)]):
                        f = lambda e: e.matmul(
                            mat[:, 2 * t + half, :], h[:, k, P * t:P * t + P], w[:, 512 * half:512 * half + 512],
                            start=(k == 0 and m < 2), stop=(k == nk - 1 and m >= 4))
                        if m == 5:
                            toks[t] = PE.do(f)
                        else:
                            PE.quiet(f)
                    if t == 1:
                        used(s, toks[1])
                        if not last:
                            split_half()
                    if mid and (g, j, t) == (0, 1, 0):
                        mid()
                k0 += 2 * n
            return toks

        def post(l, g, t, t_mm, tgt):
            flat = mat[:, 2 * t:2 * t + 2, :]
            xv = xn[:, t, :].rearrange("p (a b) -> p a b", a=2)
            gv = gtb[:, g, :].rearrange("p (a b) -> p a b", a=2)
            if l < 2:
                ss = cols(1)
                a = AC.do(lambda e: e.activation(xv, flat, ACT.Square, accum_out=ss), t_mm, *xn_free[t])
                r = rstd(ss, D, 1, a)
                b = DV.do(lambda e: e.scalar_tensor_tensor(out=xv, in0=flat, scalar=ss, in1=gv, op0=ALU.mult,
                                                           op1=ALU.mult), r, *tgt)
            else:
                b = DV.do(lambda e: e.tensor_tensor(out=xv, in0=flat, in1=gv, op=ALU.mult), t_mm, *tgt, *xn_free[t])
            c = DV.do(lambda e: e.tensor_tensor(out=x[:, t, :], in0=x[:, t, :], in1=xn[:, t, :], op=ALU.add), b)
            bank_readers[2 * t] = bank_readers[2 * t + 1] = (b,)
            xn_free[t] = (c,)
            gfree[g] = (b,)
            return c

        def columns_of(l, p):
            mods_through(l, p)
            return modt[(l, p - 1, 0)], modt[(l, p, 0)]

        def post_rows(l, g, t, t_mm, tgt, fill):
            ss, ss2 = cols(1), cols(2)
            r = ()
            if l < 2:
                a = AC.do(lambda e: e.activation(xn[:, t, :].rearrange("p (a b) -> p a b", a=2), mat[:, 2 * t:2 * t + 2, :],
                                                 ACT.Square, accum_out=ss), t_mm, *xn_free[t])
                r = (rstd(ss, D, 1, a),)
            fill()
            for h in range(2):
                c = slice(512 * h, 512 * h + 512)
                if l < 2:
                    b = DV.do(lambda e: e.scalar_tensor_tensor(out=xn[:, t, c], in0=bank(2 * t + h), scalar=ss,
                                                               in1=gtb[:, g, c], op0=ALU.mult, op1=ALU.mult), *r, *tgt)
                else:
                    b = DV.do(lambda e: e.tensor_tensor(out=xn[:, t, c], in0=bank(2 * t + h), in1=gtb[:, g, c],
                                                        op=ALU.mult), t_mm, *tgt, *xn_free[t])
                a = DV.do(lambda e: e.tensor_tensor(out=x[:, t, c], in0=x[:, t, c], in1=xn[:, t, c], op=ALU.add), b)
                a = AC.do(lambda e: e.activation(xn[:, t, c], x[:, t, c], ACT.Square, scale=2.0 ** -5,
                                                 accum_out=ss2[:, h:h + 1]), a)
            bank_readers[2 * t] = bank_readers[2 * t + 1] = gfree[g] = (b,)
            a = PO.do(lambda e: e.tensor_scalar(ss2[:, 0:1], ss2[:, 0:1], ss2[:, 1:2], EPS, ALU.add, ALU.add), a)
            a = PO.do(lambda e: e.tensor_tensor(out=ss2[:, 0:1], in0=ss2[:, 0:1], in1=phalf[:, :], op=ALU.pow), a, m2)
            return [DV.do(lambda e: e.tensor_scalar(xn[:, t, c], x[:, t, c], ss2[:, 0:1], None, ALU.mult), a)
                    for c in (slice(0, 512), slice(512, 1024))]

        def boundary(l, g, t_mm, tgt, row, upto):
            x0 = post(l, g, 0, t_mm[0], tgt)
            rs = norm_rows(x, 0, x0)
            tmod = columns_of(*upto)
            wr, tails = hT_free[0], []
            r1 = post_rows(l, g, 1, t_mm[1], tgt, lambda: norm_T(rs, 0, row, hH, hL, tmod, wr, (0,), (1, 1), tails))
            norm_T(rs, 0, row, hH, hL, tmod, wr, (1,), (1, 1), tails)
            t00 = tails[0]()
            t10 = norm_T(r1, 1, row, hH, hL, tmod, wr, (0,), (0, 0))
            t01 = tails[1]()
            t11 = norm_T(r1, 1, row, hH, hL, tmod, wr, (1,), (1, 1))
            for _ in range(4):
                split_half()
            return [t00 + t01, t10 + t11]

        def boundary_by_tile(l, g, t_mm, tgt, row, upto, early=2):
            wr = hT_free[0]
            x0 = post(l, g, 0, t_mm[0], tgt)
            r0 = norm_rows(x, 0, x0)
            tmod = columns_of(*upto)
            x1 = post(l, g, 1, t_mm[1], tgt)
            th = [norm_T(r0, 0, row, hH, hL, tmod, wr, engines=(1, 1)), None]
            r1 = norm_rows(x, 1, x1)
            for _ in range(early):
                split_half()

            def finish():
                th[1] = norm_T(r1, 1, row, hH, hL, tmod, wr)
                for _ in range(4 - early):
                    split_half()
            return th, finish

        tx0 = SP.dma(lambda e: e.dma_start(x[:, :, :], A["x"].rearrange("o (t p) d -> p (o t) d", p=P)), s_in[1], 16)

        qT = att[:, 0:2048].rearrange("p (k t) -> p k t", k=8)
        kT = att[:, 2048:4096].rearrange("p (k t) -> p k t", k=8)
        v01 = att[:, 4096:6144].rearrange("p (t d) -> p t d", t=2)
        kT2 = att[:, 2048:6144].rearrange("p (k t) -> p k t", k=8)
        v2 = att[:, 6144:10240].rearrange("p (t d) -> p t d", t=4)
        att_slots = [att[:, 6144 + 384 * i:6144 + 384 * i + 384] for i in range(10)]

        hT_free = [()]
        RATE_QKV2 = (0.0, 0.6, 1.2)
        MOD_RATE = {0: (0.6, 0.4), 1: (0.4, 0.4), 2: (0.3, 0.4), 3: (0.6, 0.4)}

        def value_product(l, th, mid):
            toks = tokmajor("qkv%d" % l, th, hH, hL, KT, [2, 2], mid)
            split_half()
            split_half()
            tv = []
            for tt in range(2):
                dst = v01[:, tt, :].rearrange("p (a b) -> p a b", a=2)
                tv.append(AC.do(lambda e: e.activation(dst, mat[:, 2 * tt:2 * tt + 2, :], ACT.Copy), toks[tt],
                                *last_att[0], *last_a[0]))
                bank_readers[2 * tt] = bank_readers[2 * tt + 1] = (tv[-1],)
                split_half()
            return tv

        def qk_products(l, th, start_attention):
            tq, tk = [], []
            gen = None
            for j in range(4):
                for n, (dst, lst) in enumerate(((qT, tq), (kT, tk))):
                    def between():
                        split_half()
                        if gen:
                            next(gen)

                    b, t = featmajor("qkv%d" % l, th, hH, hL, between=between)
                    d = dst[:, 2 * j:2 * j + 2, :]
                    src = bank(b).rearrange("p (a b) -> p a b", a=2)
                    if n == 0:
                        e1 = AC.do(lambda e: e.activation(d, src, ACT.Copy, scale=0.125), t, *last_att[0], *last_a[0])
                    else:
                        e1 = AC.do(lambda e: e.activation(d, src, ACT.Copy), t, *last_att[0], *last_a[0])
                    bank_readers[b] = (e1,)
                    lst.append(e1)
                    split_half()
                    if gen:
                        next(gen)
                if j == 0:
                    gen = start_attention(tq, tk)
            hT_free[0] = (t,)
            for _ in gen:
                mods()
                mods()

        def values_out(h, aT, ta, tv):
            hp, ht = 64 * (h % 2), h // 2
            ob = mat[:, 5, 0:256]
            PE.wait(*ta, *tv)
            if h % 2 == 0:
                PE.wait(*bank_readers[5])
            vh = [v01[:, i, 64 * h:64 * h + 64] for i in range(2)]
            PE.quiet(lambda e: e.matmul(ob[hp:hp + 64, 0:128], vh[0], aT[:, 0:128], start=True, stop=True))
            PE.quiet(lambda e: e.matmul(ob[hp:hp + 64, 128:256], vh[0], aT[:, 128:256], start=True, stop=False))
            t = PE.do(lambda e: e.matmul(ob[hp:hp + 64, 128:256], vh[1], aT[:, 256:384], start=False, stop=True))
            if h % 2:
                i, y, fr = tmp.take()
                e1 = AC.do(lambda e: e.activation(y[:, 0:256], ob, ACT.Copy), t, *fr)
                bank_readers[5] = (e1,)
                last = split_T(y[:, 0:256], e1, oH[:, ht, :], oL[:, ht, :], (*last_o[0], *last_a[0]))
                tmp.free(i, *last)
                o_tok[0].append(last)
            return t

        o_tok = [()]

        def pipeline(stages, n):
            state = [dict() for _ in range(n)]
            for step in range(n + len(stages) - 1):
                for s_ in range(len(stages) - 1, -1, -1):
                    i = step - s_
                    if 0 <= i < n and stages[s_]:
                        stages[s_](i, state[i])
                yield

        def stick_breaking(tq, tk, tv):
            slots = Slots(att_slots)
            zb, rb = Banks([0, 1]), Banks([2, 3])
            tmask = strict_mask((m1,))

            def scores(h, o):
                hp, ht = 64 * (h % 2), h // 2
                b = zb.take()
                q, k = qT[hp:hp + 64, ht, :], kT[hp:hp + 64, ht, :]
                PE.wait(tq[ht // 2], tk[ht // 2], *bank_readers[b])
                PE.quiet(lambda e: e.matmul(bank(b)[:, 0:256], k[:, 0:128], q[:, 0:256], start=True, stop=True))
                t = PE.do(lambda e: e.matmul(bank(b)[:, 256:384], k[:, 128:256], q[:, 128:256], start=True, stop=True))
                i, z, fr = slots.take()
                o["zi"], o["z"] = i, z
                o["tz"] = AC.do(lambda e: e.activation(z, bank(b)[:, 0:384], ACT.Copy), t, *fr)
                bank_readers[b] = (o["tz"],)

            def logs(h, o):
                z = o["z"]
                i2, w, fr2 = slots.take()
                a = AC.do(lambda e: e.activation(w, z, ACT.Abs), o["tz"], *fr2)
                a = AC.do(lambda e: e.activation(w, w, ACT.Exp, scale=-1.0), a)
                a = AC.do(lambda e: e.activation(w, w, ACT.Ln, bias=1.0), a)
                o["wi"], o["w"], o["tw"] = i2, w, a

            def softplus(h, o):
                z, w = o["z"], o["w"]
                a = DV.do(lambda e: e.scalar_tensor_tensor(out=w, in0=z, scalar=0.0, in1=w, op0=ALU.max, op1=ALU.add), o["tw"])
                wd = w.rearrange("p (n t) -> p n t", n=3)[:, 0::2, :]
                o["tw"] = PO.do(lambda e: e.tensor_tensor(out=wd, in0=wd, in1=msk[:, :].unsqueeze(1).to_broadcast([P, 2, P]),
                                                          op=ALU.mult), a, tmask)

            def sums(h, o):
                b = rb.take()
                w, z = o["w"], o["z"]
                PE.wait(o["tw"], t_const, *bank_readers[b])
                PE.quiet(lambda e: e.matmul(bank(b)[:, 0:128], tri_ge[:, :], w[:, 0:128], start=True, stop=True))
                PE.quiet(lambda e: e.matmul(bank(b)[:, 128:256], tri_ge[:, :], w[:, 128:256], start=True, stop=False))
                PE.quiet(lambda e: e.matmul(bank(b)[:, 128:256], ones[:, :], w[:, 256:384], start=False, stop=True))
                t = PE.do(lambda e: e.matmul(bank(b)[:, 256:384], tri_ge[:, :], w[:, 256:384], start=True, stop=True))
                d = DV.do(lambda e: e.tensor_tensor(out=w, in0=z, in1=bank(b)[:, 0:384], op=ALU.subtract), t)
                bank_readers[b] = (d,)
                slots.free(o["zi"], d)
                wd = w.rearrange("p (n t) -> p n t", n=3)[:, 0::2, :]
                d = PO.do(lambda e: e.affine_select(out=wd, in_=wd, compare_op=ALU.is_gt, fill=NEG, base=0,
                                                    pattern=[[0, 2], [1, P]], channel_multiplier=-1), d)
                o["ts"] = d

            def weights(h, o):
                o["ta"] = AC.do(lambda e: e.activation(o["w"], o["w"], ACT.Exp), o["ts"])

            def values(h, o):
                t = values_out(h, o["w"], (o["ta"],), tv)
                slots.free(o["wi"], t)
                last_att[0] = (t,)

            return pipeline([scores, logs, softplus, sums, weights, values], H)

        def forgetting(tq, tk, tv, tcum):
            slots = Slots(att_slots)
            sbk, tbk = Banks([0, 1]), Banks([2, 3])
            a = PO.do(lambda e: e.tensor_scalar(msk[:, :], ones[:, :], -1.0, None, ALU.add), *last_att[0])
            tmask = PO.do(lambda e: e.affine_select(out=msk[:, :], in_=msk[:, :], compare_op=ALU.is_ge, fill=NEG,
                                                    base=0, pattern=[[-1, P]], channel_multiplier=1), a)

            def scores(h, o):
                hp, ht = 64 * (h % 2), h // 2
                b = sbk.take()
                q, k = qT[hp:hp + 64, ht, :], kT[hp:hp + 64, ht, :]
                eh = ident[0:H, h:h + 1].to_broadcast([H, P])
                PE.wait(tq[ht // 2], tk[ht // 2], tmask, tcum, t_const, *bank_readers[b])
                for c, t0, s0 in ((0, 0, 0), (128, 128, 0), (256, 128, 128)):
                    dst = bank(b)[:, c:c + P]
                    PE.quiet(lambda e: e.matmul(dst, q[:, t0:t0 + P], k[:, s0:s0 + P], start=True, stop=False))
                    f = lambda e: e.matmul(dst, eh, ncum[:, s0:s0 + P], start=False, stop=(c == 128))
                    PE.quiet(f)
                    if c != 128:
                        f2 = lambda e: e.matmul(dst, ident[:, :], msk[:, :], start=False, stop=True)
                        t = PE.do(f2) if c == 256 else PE.quiet(f2)
                nm, rs = cols(2), cols(2)
                a = DV.do(lambda e: e.tensor_reduce(nm[:, 0:1], bank(b)[:, 0:128], AX.X, ALU.max, negate=True), t)
                a = DV.do(lambda e: e.tensor_reduce(nm[:, 1:2], bank(b)[:, 128:384], AX.X, ALU.max, negate=True), t)
                o.update(nm=nm, rs=rs, tm=a, b=b)

            def weights(h, o):
                nm, rs, a, b = o["nm"], o["rs"], o["tm"], o["b"]
                i, p, fr = slots.take()
                a2 = AC.do(lambda e: e.activation(p[:, 0:128], bank(b)[:, 0:128], ACT.Exp, bias=nm[:, 0:1],
                                                  accum_out=rs[:, 0:1]), a, *fr)
                a2 = AC.do(lambda e: e.activation(p[:, 128:384], bank(b)[:, 128:384], ACT.Exp, bias=nm[:, 1:2],
                                                  accum_out=rs[:, 1:2]), a)
                bank_readers[b] = (a2,)
                o.update(p=p, pi=i, t=a2)

            def normalise(h, o):
                p, rs = o["p"], o["rs"]
                a = DV.do(lambda e: e.reciprocal(rs, rs), o["t"])
                DV.do(lambda e: e.tensor_scalar(p[:, 0:128], p[:, 0:128], rs[:, 0:1], None, ALU.mult), a)
                o["t"] = DV.do(lambda e: e.tensor_scalar(p[:, 128:384], p[:, 128:384], rs[:, 1:2], None, ALU.mult), a)

            def turn(h, o):
                p = o["p"]
                b = tbk.take()
                PE.wait(o["t"], *bank_readers[b])
                for c in (0, 128):
                    PE.quiet(lambda e, c=c: e.transpose(bank(b)[:, c:c + P], p[:, c:c + P], ident[:, :]))
                t = PE.do(lambda e: e.transpose(bank(b)[:, 256:384], p[:, 256:384], ident[:, :]))
                slots.free(o["pi"], t)
                i, w, fr = slots.take()
                o["w"], o["wi"] = w, i
                o["ta"] = AC.do(lambda e: e.activation(w, bank(b)[:, 0:384], ACT.Copy), t, *fr)
                bank_readers[b] = (o["ta"],)

            def values(h, o):
                t = values_out(h, o["w"], (o["ta"],), tv)
                slots.free(o["wi"], t)
                last_att[0] = (t,)

            return pipeline([scores, weights, normalise, turn, values], H)

        def forget_logits(th):
            b, tp = featmajor("wfg", th, hH, hL, tiles=1)
            used(half_chunk("wfg")[0], tp)
            split_half()
            split_half()
            i2, w2, f2 = tmp.take()
            z, y = w2[0:H, 0:256], w2[0:H, 256:512]
            bf = sm[0:H, SM["bf"][0]:SM["bf"][0] + 1]
            a = DV.do(lambda e: e.tensor_scalar(z, bank(b)[0:H, 0:256], bf, None, ALU.add), tp, *f2)
            bank_readers[b] = (a,)
            d = DV.do(lambda e: e.scalar_tensor_tensor(out=y, in0=z, scalar=-1.0, in1=z, op0=ALU.mult, op1=ALU.max), a)
            d = AC.do(lambda e: e.activation(y, y, ACT.Exp, scale=-1.0), d)
            d = AC.do(lambda e: e.activation(y, y, ACT.Ln, bias=1.0), d)
            g = DV.do(lambda e: e.scalar_tensor_tensor(out=z, in0=z, scalar=0.0, in1=y, op0=ALU.min, op1=ALU.subtract), d)
            r = DV.do(lambda e: e.tensor_tensor_scan(out=y, data0=one_row, data1=z, initial=0.0, op0=ALU.mult,
                                                     op1=ALU.subtract), g, m1)
            r = DV.do(lambda e: e.tensor_copy(ncum[:, :], y), r)
            tmp.free(i2, r)
            return r

        def out_product(name, to):
            return tokmajor(name, [to, to], oH, oL, KT, [1, 1, 2])

        def diff_tables():
            i0, tb, f0 = tmp.take()
            t_tab = SP.dma(lambda e: e.dma_start(tb, A["rope"]), s_in[4], 16, *f0)
            i1, gb_, f1 = tmp.take()
            t_g = SP.dma(lambda e: e.dma_start(gb_[:, 0:256], A["qkg"].to_broadcast([P, 256])), s_in[5], 16, *f1)
            tv_ = tb[:, 0:256].rearrange("p (c t d) -> p c t d", c=2, t=2)
            gv_ = gb_[:, 0:256].rearrange("p (n c d) -> p n c d", n=2, c=2)
            tr = []
            for n in range(2):
                for c in range(2):
                    tr.append(DV.do(lambda e, n=n, c=c: e.scalar_tensor_tensor(
                        out=rope[:, 2 * n + c, :, :], in0=tv_[:, c], scalar=(0.125 if n == 0 else 1.0),
                        in1=gv_[:, n, c].unsqueeze(1).to_broadcast([P, 2, 64]), op0=ALU.mult, op1=ALU.mult), t_tab, t_g))
            tkg = DV.do(lambda e: e.tensor_copy(kgt[:, :], gv_[:, 1, 0]), t_g)
            tr.append(tkg)
            tmp.free(i0, *tr)
            tmp.free(i1, *tr)
            tg = SP.dma(lambda e: e.dma_start(subln[:, :], A["subln"].to_broadcast([P, P])), s_in[0], 32, t_sm)
            tg = DV.do(lambda e: e.tensor_scalar(subln[:, :], subln[:, :], 1.0 - LAM_INIT, None, ALU.mult), tg, t_c)
            return tr, tg, lam_value()

        def differential(th, mid, tmod, tr):
            AC.quiet(lambda e: e.preload_act_table_set("natural_log_exp_and_others"))
            tc = None
            cx = att[:, 8192:10240].rearrange("p (t d) -> p t d", t=2)
            tcx = SP.dma(lambda e: e.dma_start(cx, A["ctx"].rearrange("o (t p) d -> p (o t) d", p=P)), s_in[6], 16,
                         *last_att[0], *last_a[0])
            kgain = kgt[:, :]
            units, turns = [], []
            order = [(0, 0), (1, 0), (2, 0), (0, 1), (1, 1), (2, 1)]
            for g, (kind, half) in enumerate(order):
                toks = range(2) if kind == 0 else range(4)
                bs = [(2 if kind == 0 else 0) + t for t in toks]
                for q in range(2):
                    hs = [half_chunk("qkv2") for _ in range(2)]
                    for t in toks:
                        if t == 1 and (g, q) == (0, 0):
                            mid()
                            rc = [norm_rows(cx, i, tcx) for i in range(2)]
                        if t == 1 and (g, q) == (0, 1):
                            tc = [norm_T(rc[i], i, 4, oH, oL, tmod, (*last_o[0], *last_a[0])) for i in range(2)]
                        if q == 0:
                            PE.wait(*bank_readers[bs[t]])
                        sH, sL, tt, tk_ = (hH, hL, t, th[t]) if t < 2 else (oH, oL, t - 2, tc[t - 2])
                        for p2 in range(2):
                            _, wh, wl = hs[p2]
                            wh = wh.rearrange("p (k n) -> p k n", k=2)
                            wl = wl.rearrange("p (k n) -> p k n", k=2)
                            for j in range(2):
                                k = 4 * q + 2 * p2 + j
                                PE.wait(*tk_[k])
                                for n, (h_, w_) in enumerate(((sH, wh), (sH, wl), (sL, wh))):
                                    f = lambda e: e.matmul(bank(bs[t]), h_[:, k, P * tt:P * tt + P], w_[:, j, :],
                                                           start=(k == 0 and n == 0), stop=(k == KT - 1 and n == 2))
                                    if p2 == 1 and j == 1 and n == 2:
                                        tp = PE.do(f)
                                    else:
                                        PE.quiet(f)
                        if q == 1:
                            units.append((kind, half, t, bs[t], tp))
                    for s_, _, _ in hs:
                        used(s_, tp)
                    if q == 1:
                        while turns:
                            turns.pop(0)()
                        if kind == 2:
                            copy_v(units)
                            normed = []
                        else:
                            normed = head_norms(units)
                    at_rate(RATE_QKV2[kind] if (g, q) != (5, 1) else 0.0, (3, 1))
                    split_half()
                    split_half()
                turns = [head_rope(kind, half, t, n, tr, kgain) for t, n in enumerate(normed)]
                units = []
            while turns:
                turns.pop(0)()
            last_o[0] = (tp,)
            return tp

        tqk = {"q": [], "k": [], "v": []}

        def copy_v(units):
            for kind, half, t, b, tp in units:
                e1 = AC.do(lambda e: e.activation(v2[:, t, 512 * half:512 * half + 512], bank(b), ACT.Copy), tp,
                           *last_att[0], *last_a[0], *xn_free[0])
                bank_readers[b] = (e1,)
                tqk["v"].append(e1)

        def head_norms(units):
            n = len(units)
            ss = cols(8 * n)
            ys = []
            for kind, half, t, b, tp in units:
                i, y, fr = tmp.take()
                a = AC.do(lambda e: e.activation(y, bank(b), ACT.Copy), tp, *fr)
                bank_readers[b] = (a,)
                ys.append((i, y, a))
            for t, (i, y, a) in enumerate(ys):
                sq = xn[:, t // 2, 512 * (t % 2):512 * (t % 2) + 512]
                a = AC.do(lambda e: e.activation(sq, y, ACT.Square), a, *xn_free[t // 2])
                r = DV.do(lambda e: e.tensor_reduce(ss[:, 8 * t:8 * t + 8], sq.rearrange("p (h d) -> p h d", h=8),
                                                    AX.X, ALU.add), a)
                xn_free[t // 2] = (*(xn_free[t // 2] if t % 2 else ()), r)
            r = rstd_log(ss, 64, r)
            out = []
            for t, (i, y, a) in enumerate(ys):
                yv = y.rearrange("p (h d) -> p h d", h=8)
                sv = ss[:, 8 * t:8 * t + 8].unsqueeze(2).to_broadcast([P, 8, 64])
                out.append((i, y, DV.do(lambda e: e.tensor_tensor(out=yv, in0=yv, in1=sv, op=ALU.mult), r)))
            return out

        def head_rope(kind, half, t, normed, tr, kgain):
            i, y, a = normed
            i2, w, fr2 = tmp.take()
            yv, wv = (q_.rearrange("p (h d) -> p h d", h=8) for q_ in (y, w))
            if t >= 2:
                a = PO.do(lambda e: e.tensor_tensor(out=wv, in0=yv, in1=kgain.unsqueeze(1).to_broadcast([P, 8, 64]),
                                                    op=ALU.mult), a, *fr2, *tr)
            else:
                cs = rope[:, 2 * kind, t, :].unsqueeze(1).to_broadcast([P, 8, 64])
                w5 = w.rearrange("p (g n d) -> p g n d", n=2, d=16)
                y5 = y.rearrange("p (g n d) -> p g n d", n=2, d=16)
                sn = rope[:, 2 * kind + 1, t, :].rearrange("p (r n d) -> p r n d", r=2, n=2)
                for n in range(2):
                    for r_ in range(2):
                        wq = w.rearrange("p (h r n d) -> p h r n d", r=2, n=2, d=16)[:, :, r_, n, :]
                        yq = y.rearrange("p (h r n d) -> p h r n d", r=2, n=2, d=16)[:, :, r_, 1 - n, :]
                        sq = sn[:, r_, n, :].unsqueeze(1).to_broadcast([P, 8, 16])
                        b1 = DV.do(lambda e, wq=wq, yq=yq, sq=sq: e.tensor_tensor(out=wq, in0=yq, in1=sq, op=ALU.mult),
                                   a, *fr2, *tr)
                c1 = PO.do(lambda e: e.tensor_tensor(out=yv, in0=yv, in1=cs, op=ALU.mult), a, b1, *tr)
                a = DV.do(lambda e: e.tensor_tensor(out=w, in0=w, in1=y, op=ALU.add), b1, c1)
            tmp.free(i, a)

            def turn():
                b2 = ring.take()
                PE.wait(a, t_const, *bank_readers[b2])
                for j in range(4):
                    f = lambda e: e.transpose(bank(b2)[:, P * j:P * j + P], w[:, P * j:P * j + P], ident[:, :])
                    if j == 3:
                        pt = PE.do(f)
                    else:
                        PE.quiet(f)
                tmp.free(i2, pt)
                dst = (qT if kind == 0 else kT2)[:, 4 * half:4 * half + 4, P * t:P * t + P]
                e1 = AC.do(lambda e: e.activation(dst, bank(b2).rearrange("p (a b) -> p a b", a=4), ACT.Copy), pt,
                           *last_att[0], *last_a[0])
                bank_readers[b2] = (e1,)
                tqk["qk"[kind]].append(e1)
            return turn

        def lam_value():
            i, y, fr = tmp.take()
            lm = cols(4)
            t = SP.dma(lambda e: e.dma_start(y[:, 0:256], A["lam"].to_broadcast([P, 256])), s_in[7], 16, *fr)
            y4 = y[:, 0:256].rearrange("p (n c d) -> p n c d", n=2, c=2)
            w = y[:, 256:384].rearrange("p (n d) -> p n d", n=2)
            a = DV.do(lambda e: e.tensor_tensor(out=w, in0=y4[:, :, 0], in1=y4[:, :, 1], op=ALU.mult), t)
            a = DV.do(lambda e: e.tensor_reduce(lamc[:, 0:2], w, AX.X, ALU.add), a)
            tmp.free(i, a)
            a = AC.do(lambda e: e.activation(lamc[:, 0:2], lamc[:, 0:2], ACT.Exp), a)
            a = DV.do(lambda e: e.tensor_tensor(out=lamc[:, 2:3], in0=lamc[:, 1:2], in1=lamc[:, 0:1], op=ALU.subtract), a)
            return DV.do(lambda e: e.tensor_scalar(lamc[:, 2:3], lamc[:, 2:3], -LAM_INIT, None, ALU.add), a)


        def diff_attention(tlam, tg):
            sbk, tbk, obk = Banks([0, 1, 2, 3]), Banks([4, 5]), Banks([7])
            gs = subln[:, :]
            slots = tmp
            tall = (*tqk["q"], *tqk["k"])

            def scores(n, o):
                h, t = n // 2, n % 2
                bs, es, st_ = [], [], cols(4)
                nm, rs = st_[:, 0:2], st_[:, 2:4]
                tt = []
                for m in range(2):
                    g = 8 * m + h
                    hp, ht = 64 * (g % 2), g // 2
                    b = sbk.take()
                    bs.append(b)
                    tt.append(PE.do(lambda e: e.matmul(bank(b), qT[hp:hp + 64, ht, P * t:P * t + P], kT2[hp:hp + 64, ht, :],
                                                       start=True, stop=True), *tall, *bank_readers[b]))
                for m in range(2):
                    a = DV.do(lambda e: e.tensor_reduce(nm[:, m:m + 1], bank(bs[m]), AX.X, ALU.max, negate=True), tt[m])
                    i, y, fr = slots.take()
                    a = AC.do(lambda e: e.activation(y, bank(bs[m]), ACT.Exp, bias=nm[:, m:m + 1],
                                                     accum_out=rs[:, m:m + 1]), a, *fr)
                    bank_readers[bs[m]] = (a,)
                    es.append((i, y, a))
                o.update(es=es, rs=rs)

            def combine(n, o):
                rs, (i0, y0, a0), (i1, y1, a1) = o["rs"], *o["es"]
                q = o["q"] = cols(3)
                a = DV.do(lambda e: e.reciprocal(q[:, 0:2], rs), a0, a1)
                a = DV.do(lambda e: e.scalar_tensor_tensor(out=q[:, 2:3], in0=q[:, 1:2], scalar=lamc[:, 2:3],
                                                           in1=rs[:, 0:1], op0=ALU.mult, op1=ALU.mult), a, tlam)
                b = DV.do(lambda e: e.scalar_tensor_tensor(out=y0, in0=y1, scalar=q[:, 2:3], in1=y0, op0=ALU.mult,
                                                           op1=ALU.add), a)
                slots.free(i1, b)
                o["t"] = b

            def turn(n, o):
                i0, y0, _ = o["es"][0]
                b = tbk.take()
                PE.wait(o["t"], t_const, *bank_readers[b])
                for j in range(4):
                    f = lambda e, j=j: e.transpose(bank(b)[:, P * j:P * j + P], y0[:, P * j:P * j + P], ident[:, :])
                    t = PE.do(f) if j == 3 else PE.quiet(f)
                o["ta"] = AC.do(lambda e: e.activation(y0, bank(b), ACT.Copy), t)
                bank_readers[b] = (o["ta"],)

            def values(n, o):
                h, t = n // 2, n % 2
                i0, y0, _ = o["es"][0]
                b = obk.take()
                PE.wait(o["ta"], *tqk["v"], *bank_readers[b])
                for j in range(4):
                    f = lambda e, j=j: e.matmul(bank(b)[:, 0:P], y0[:, P * j:P * j + P], v2[:, j, P * h:P * h + P],
                                                start=(j == 0), stop=(j == 3))
                    tp = PE.do(f) if j == 3 else PE.quiet(f)
                o["xo"], o["ss"] = xn[:, t, P * h:P * h + P], cols(1)
                e1 = AC.do(lambda e: e.activation(o["xo"], bank(b)[:, 0:P], ACT.Identity, scale=o["q"][:, 0:1]), tp,
                           o["t"], *xn_free[t])
                bank_readers[b] = (e1,)
                e2 = AC.do(lambda e: e.activation(y0[:, 0:P], o["xo"], ACT.Square, accum_out=o["ss"]), e1)
                slots.free(i0, e2)
                last_att[0] = (tp,)
                o["r"] = rstd(o["ss"], 128, 1, e2)

            def norm(n, o):
                o_done.append(DV.do(lambda e: e.scalar_tensor_tensor(out=o["xo"], in0=o["xo"], scalar=o["ss"],
                                                                     in1=gs, op0=ALU.mult, op1=ALU.mult), o["r"], tg))

            def features(n, o):
                if n % 4 < 3:
                    return
                b = tbk.take()
                PE.wait(o_done[n], *bank_readers[b])
                for j in range(2):
                    for t in range(2):
                        f = lambda e, j=j, t=t: e.transpose(bank(b)[:, 256 * j + P * t:256 * j + P * t + P],
                                                            xn[:, t, (n // 2 - 1 + j) * P:(n // 2 + j) * P], ident[:, :])
                        pt = PE.do(f) if j == t == 1 else PE.quiet(f)
                h = n // 2 - 1
                last = split_T(bank(b).rearrange("p (a b) -> p a b", a=2), pt, oH[:, h:h + 2, :], oL[:, h:h + 2, :],
                               last_o[0])
                to.extend([last, last])
                bank_readers[b] = last
                xn_last[0] = (pt,)

            o_done, to, xn_last = [], [], [()]
            at_rate(MOD_RATE[2][0], (3, 1))
            for _ in pipeline([scores, combine, turn, values, norm, None, features], 16):
                mods()
                mods()
            xn_free[0] = xn_free[1] = xn_last[0]
            return to

        def short_conv(th):
            buf = att[:, 0:2 * 2 * 258].rearrange("p (b i t) -> p b i t", b=2, i=2)
            tz = DV.do(lambda e: e.memset(att[:, 0:1032], 0.0), *last_att[0], *last_a[0])
            prev = [(), ()]
            to = []
            for j in range(4):
                bc, tc = featmajor("qkv3", th, hH, hL)
                i, cc, fr = tmp.take()
                split_half()
                a = AC.do(lambda e: e.activation(cc, bank(bc), ACT.Copy), tc, *fr)
                bank_readers[bc] = (a,)
                split_half()
                bu, tu = featmajor("qkv3", th, hH, hL)
                pb = buf[:, j % 2]
                split_half()
                a = DV.do(lambda e: e.tensor_tensor(out=pb[:, :, 1:257], in0=bank(bu).rearrange("p (a b) -> p a b", a=2),
                                                    in1=cc.rearrange("p (a b) -> p a b", a=2), op=ALU.mult),
                          tu, a, tz, *prev[j % 2])
                tmp.free(i, a)
                bank_readers[bu] = (a,)
                split_half()
                i, y, fr = tmp.take()
                yv = y.rearrange("p (a b) -> p a b", a=2)
                w = [[sm[:, SM[f"sc{k}"][0] + 2 * j + n:SM[f"sc{k}"][0] + 2 * j + n + 1] for k in range(3)] for n in range(2)]
                for n in range(2):
                    c = DV.do(lambda e: e.tensor_scalar(yv[:, n], pb[:, n, 1:257], w[n][1], None, ALU.mult), a, *fr)
                for k, lo_ in ((0, 0), (2, 2)):
                    c0 = c
                    for n in range(2):
                        c = DV.do(lambda e: e.scalar_tensor_tensor(out=yv[:, n], in0=pb[:, n, lo_:lo_ + 256],
                                                                   scalar=w[n][k], in1=yv[:, n], op0=ALU.mult,
                                                                   op1=ALU.add), c0)
                prev[j % 2] = (c,)
                bb, tb = featmajor("qkv3", th, hH, hL)
                split_half()
                c = DV.do(lambda e: e.tensor_tensor(out=y, in0=bank(bb), in1=y, op=ALU.mult), tb, c)
                bank_readers[bb] = (c,)
                last = split_T(yv, c, oH[:, 2 * j:2 * j + 2, :], oL[:, 2 * j:2 * j + 2, :], (*last_o[0], *last_a[0]))
                tmp.free(i, *last)
                to += [last, last]
                split_half()
            last_att[0] = (c,)
            last = to
            return last, tb

        def ffn(l, th):
            free_a = (*last_a[0], *last_att[0], *last_o[0])
            at_rate(MOD_RATE[l][1], (l + 1, 2))
            ta = []
            for j in range(11):
                bg, tg = featmajor("gate%d" % l, th, hH, hL)
                split_half()
                g = bank(bg).rearrange("p (a b) -> p a b", a=2)
                i, y, fr = tmp.take()
                yv = y.rearrange("p (a b) -> p a b", a=2)
                if l < 2:
                    col = lambda name, n: sm[:, SM[name][0] + 2 * j + n:SM[name][0] + 2 * j + n + 1]
                    for n in range(2):
                        a = AC.do(lambda e: e.activation(yv[:, n], g[:, n], ACT.Identity, bias=col(f"bc{l}", n),
                                                         scale=col(f"wc{l}2", n)), tg, *fr)
                    for n in range(2):
                        c = DV.do(lambda e: e.scalar_tensor_tensor(out=yv[:, n, 1:256], in0=g[:, n, 0:255],
                                                                   scalar=col(f"wc{l}1", n), in1=yv[:, n, 1:256],
                                                                   op0=ALU.mult, op1=ALU.add), a)
                    for n in range(2):
                        a = DV.do(lambda e: e.scalar_tensor_tensor(out=yv[:, n, 2:256], in0=g[:, n, 0:254],
                                                                   scalar=col(f"wc{l}0", n), in1=yv[:, n, 2:256],
                                                                   op0=ALU.mult, op1=ALU.add), c)
                    bank_readers[bg] = (a,)
                    split_half()
                    a = AC.do(lambda e: e.activation(y, y, ACT.Silu), a)
                else:
                    a = AC.do(lambda e: e.activation(y, bank(bg), ACT.Silu), tg, *fr)
                    bank_readers[bg] = (a,)
                    split_half()
                bu, tu = featmajor("up%d" % l, th, hH, hL)
                split_half()
                a = DV.do(lambda e: e.tensor_tensor(out=y, in0=bank(bu), in1=y, op=ALU.mult), tu, a)
                bank_readers[bu] = (a,)
                last = split_T(yv, a, aH[:, 2 * j:2 * j + 2, :], aL[:, 2 * j:2 * j + 2, :], free_a)
                tmp.free(i, *last)
                ta += [last, last]
                split_half()
            t = tokmajor("down%d" % l, [ta, ta], aH, aL, FT, [1] * 9 + [2])
            last_a[0] = (t[1],)
            return tu, t

        rows = [norm_rows(x, t, tx0) for t in range(2)]
        mods_through(0, 1)
        tmod = (modt[(0, 0, 0)], modt[(0, 1, 0)])
        for _ in range(4):
            split_half()
        th = [norm_T(rows[t], t, 0, hH, hL, tmod, ()) for t in range(2)]
        for _ in range(2):
            split_half()
        mid = None
        for l in range(LAYERS):
            at_rate(MOD_RATE[l][0], (l, 5))
            if l < 2:
                tv = value_product(l, th, mid)
                if l == 0:
                    tables = diff_tables()
                else:
                    tcum = forget_logits(th)
                AC.quiet(lambda e: e.preload_act_table_set("natural_log_exp_and_others"))
                o_tok[0] = []
                qk_products(l, th, lambda tq, tk: stick_breaking(tq, tk, tv) if l == 0 else forgetting(tq, tk, tv, tcum))
                to = o_tok[0]
            elif l == 2:
                t = differential(th, mid, (modt[(2, 0, 1)], modt[(2, 1, 1)]), tables[0])
                hT_free[0] = (t,)
                to = diff_attention(tables[2], tables[1])
            else:
                to, t = short_conv(th)
                hT_free[0] = (t,)
            t = out_product("wo%d" % l, to)
            last_o[0] = (t[1],)
            mods_through(l, 2)
            th = boundary(l, 0, t, (modt[(l, 2, 0)],), 2, (l, 4))
            t_h, t = ffn(l, th)
            hT_free[0] = (t_h,)
            mods_through(l, 5)
            if l + 1 < LAYERS:
                if l < 2:
                    th, mid = boundary_by_tile(l, 1, t, (modt[(l, 5, 0)],), 0, (l + 1, 1))
                else:
                    th = boundary(l, 1, t, (modt[(l, 5, 0)],), 0, (l + 1, 1))

        for i in range(2):
            tx = post(l, 1, i, t[i], (modt[(l, 5, 0)],))
            SP.dma(lambda e: e.dma_start(out[0, P * i:P * i + P, :], x[:, i, :]), s_out, 16 * i + 16, tx)
        SP.wait((s_out, 32))

def kernel(**inputs):
    import concourse.bacc as _bacc
    from concourse import mybir as _mybir
    from concourse.bass_utils import run_bass_kernel_spmd as _run

    I = {k: np.asarray(v) for k, v in inputs.items() if k.startswith(("win_", "cf_")) is False}

    def feat(w):
        return np.ascontiguousarray(w.reshape(8, P, -1, 2, P).transpose(2, 1, 3, 0, 4)).reshape(-1, P, 2048)

    def tok(w):
        return np.ascontiguousarray(w.reshape(-1, 2, P, 1024).transpose(0, 2, 1, 3)).reshape(-1, P, 2048)

    def tok512(w):
        return np.ascontiguousarray(w.reshape(2, 4, P, -1, 512).transpose(3, 0, 2, 1, 4)).reshape(-1, P, 2048)

    def cols(v):
        return np.ascontiguousarray(v.reshape(-1, P).T)

    arrays = {}
    for l in range(4):
        b, i = l // 2, l % 2
        mod, bm = (I["w_mod"][i], I["b_mod"][i]) if b == 0 else (I["ada_w_2"][i], I["ada_b_2"][i])
        arrays[f"mod{l}"] = np.concatenate([tok(mod[:, 1024 * p:1024 * p + 1024]) for p in range(6)])
        if b == 0:
            q = I["w_qkv"][i]
            arrays[f"qkv{l}"] = np.concatenate([feat(q[:, :2048]), tok(q[:, 2048:])])
            arrays[f"wo{l}"] = tok(I["w_o"][i])
            arrays[f"gate{l}"] = feat(I["w_ffn_gate"][i])
            arrays[f"up{l}"] = feat(I["w_ffn_up"][i])
            arrays[f"down{l}"] = tok(I["w_ffn_down"][i])
        else:
            arrays[f"qkv{l}"] = tok512(I["diff_w_qkv_2"][0]) if i == 0 else feat(I["sc_w_in_2"][0])
            arrays[f"wo{l}"] = tok(I["diff_w_o_2"][0] if i == 0 else I["sc_w_out_2"][0])
            arrays[f"gate{l}"] = feat(I["ffn_w_gate_up_2"][i][:, :FF])
            arrays[f"up{l}"] = feat(I["ffn_w_gate_up_2"][i][:, FF:])
            arrays[f"down{l}"] = tok(I["ffn_w_down_2"][i])
    parts = {"c": I["c"][0], "c2": I["c_2"][0], "cc": I["c_ctx_2"]}
    for l in range(4):
        b, i = l // 2, l % 2
        bm = I["b_mod"][i] if b == 0 else I["ada_b_2"][i]
        parts[f"g{l}a"] = I["g_mix_pre"][i] if b == 0 else I["norm1_2"][i]
        parts[f"g{l}f"] = I["g_ffn_pre"][i] if b == 0 else I["norm2_2"][i]
        for p in (0, 1, 3, 4):
            parts[f"b{l}{p}"] = bm[1024 * p:1024 * p + 1024]
        if b == 0:
            for k in range(3):
                parts[f"wc{l}{k}"] = I["w_conv"][i, k]
            parts[f"bc{l}"] = I["b_conv"][i]
    for k in range(3):
        parts[f"sc{k}"] = I["sc_conv_w_2"][0, k]
    bf = np.zeros(P, np.float32)
    bf[:H] = I["b_fg"][0]
    parts["bf"] = bf
    arrays["smalls"] = np.ascontiguousarray(np.concatenate([cols(parts[n]) for n in SM], axis=1))
    gb = []
    for l in range(4):
        b, i = l // 2, l % 2
        bm = I["b_mod"][i] if b == 0 else I["ada_b_2"][i]
        for p, g in ((2, "g_mix_post"), (5, "g_ffn_post")):
            row = bm[1024 * p:1024 * p + 1024]
            gb.append(np.concatenate([row, I[g][i] if b == 0 else row]))
    arrays["gb"] = np.stack(gb)
    arrays["x"] = I["x"]
    arrays["ctx"] = I["ctx_2"]
    wfg = np.zeros((1, P, 8, P), np.float32)
    wfg[0, :, :, :H] = I["w_fg"][0].reshape(8, P, H).transpose(1, 0, 2)
    arrays["wfg"] = wfg.reshape(1, P, 1024)
    t = np.arange(S)
    inv = (np.float32(10000.0) ** (-np.arange(16, dtype=np.float32) / np.float32(16))).astype(np.float32)
    ar = (t // 64).astype(np.float32)[:, None] * inv
    ac = (t % 64).astype(np.float32)[:, None] * inv
    cs = np.concatenate([np.cos(ar), np.cos(ar), np.cos(ac), np.cos(ac)], axis=1)
    sn = np.concatenate([-np.sin(ar), np.sin(ar), -np.sin(ac), np.sin(ac)], axis=1)
    tab = np.stack([cs, sn]).astype(np.float32).reshape(2, 2, P, 64).transpose(2, 0, 1, 3).reshape(P, 256)
    arrays["rope"] = np.ascontiguousarray(np.concatenate([tab, tab], axis=1))
    swap = np.concatenate([np.arange(16, 32), np.arange(0, 16), np.arange(48, 64), np.arange(32, 48)])
    qn, kn = I["diff_q_norm_2"][0], I["diff_k_norm_2"][0]
    arrays["qkg"] = np.concatenate([qn, qn[swap], kn, kn[swap]])[None, :]
    arrays["lam"] = np.concatenate([I["diff_lam_q1_2"][0], I["diff_lam_k1_2"][0], I["diff_lam_q2_2"][0],
                                    I["diff_lam_k2_2"][0]])[None, :]
    arrays["subln"] = np.ascontiguousarray(I["diff_subln_2"])

    nc = _bacc.Bacc("TRN2", target_bir_lowering=False, num_devices=1)
    A, feed = {}, {}
    for name, a in arrays.items():
        feed["in_" + name] = a
        A[name] = nc.dram_tensor("in_" + name, a.shape, _mybir.dt.from_np(a.dtype), kind="ExternalInput").ap()
    o = nc.dram_tensor("out_0_dram", (1, S, D), _mybir.dt.float32, kind="ExternalOutput").ap()
    build(nc, A, o)
    r = _run(nc, [feed], core_ids=[0])
    return r.results[0]["out_0_dram"]
```
